# Optimizing a Trainium2 kernel written in Bass

```python
import math
import jax, jax.numpy as jnp
from jax import lax
import numpy as np

D_MODEL = 1024
BATCH = 1
SEQ = 512
DEPTH = 2

GROUP_WIDTH = 256
MIX_WIDTH = 4 * GROUP_WIDTH
NORM_EPS = 1e-6
SSM_HEADS = 4
SSM_HEAD_DIM = 64
SSM_GROUPS = 2
SSM_STATE = 64
SSM_CONV = 4
SSM_CHUNK = 128
SSM_XBC = SSM_HEADS * SSM_HEAD_DIM + 2 * SSM_GROUPS * SSM_STATE
SSM_IN = GROUP_WIDTH + SSM_XBC + SSM_HEADS
LRU_BLOCKS = 4
LRU_BLOCK_DIM = 64
LRU_CONV = 4
LRU_C = 8.0
LRU_IN = 2 * GROUP_WIDTH
RWKV_HEADS = 4
RWKV_HEAD_DIM = 64
RWKV_DECAY_LORA = 64
RWKV_ICLR_LORA = 64
RWKV_GATE_LORA = 128
RWKV_GN_EPS = 64e-5
RWKV_IN = 3 * GROUP_WIDTH + RWKV_DECAY_LORA + RWKV_ICLR_LORA + RWKV_GATE_LORA
NSA_HEADS = 4
NSA_HEAD_DIM = 64
NSA_CMP_STRIDE = 16
NSA_CMP_LEN = 2 * NSA_CMP_STRIDE
NSA_CMP_HIDDEN = 256
NSA_SEL_BLOCK = 64
NSA_SEL_TOPN = 16
NSA_WINDOW = 512
NSA_Q_BLOCK = 128
NSA_FORCE = 1e4
NSA_IN = NSA_HEADS * NSA_HEAD_DIM + 6 * NSA_HEAD_DIM + 3 * NSA_HEADS
N_IN = SSM_IN + LRU_IN + RWKV_IN + NSA_IN
PEER_HEADS = 8
PEER_NKEYS = 128
PEER_EXPERTS = PEER_NKEYS * PEER_NKEYS
PEER_KEY_DIM = 128
PEER_TOPK = 16
PEER_TOKEN_CHUNK = 128

kernel_name = "hymba_ssd_rglru_rwkv7_nsa_peer"

def rms_norm(x, g):
    xf = x.astype(jnp.float32)
    y = xf * lax.rsqrt(jnp.mean(xf * xf, axis=-1, keepdims=True) + NORM_EPS)
    return (y * g).astype(x.dtype)

def causal_dwconv(x, w, b):
    k, c = w.shape
    y = lax.conv_general_dilated(x, w[:, None, :].astype(x.dtype), window_strides=(1,),
                                 padding=[(k - 1, 0)], dimension_numbers=('NWC', 'WIO', 'NWC'),
                                 feature_group_count=c)
    return y + b

def shift_right(t):
    return jnp.pad(t, ((0, 0), (1, 0), (0, 0)))[:, :-1]

def masked_softmax(s, mask):
    s = jnp.where(mask, s.astype(jnp.float32), -jnp.inf)
    m = jnp.max(s, axis=-1, keepdims=True)
    m = jnp.where(jnp.isfinite(m), m, 0.0)
    e = jnp.where(mask, jnp.exp(s - m), 0.0)
    return e / jnp.maximum(jnp.sum(e, axis=-1, keepdims=True), 1e-30)

def alibi_slopes(n):
    return jnp.asarray(2.0 ** (-8.0 * (np.arange(n) + 1) / n), jnp.float32)

def segsum(a):
    t = a.shape[-1]
    ar = jnp.broadcast_to(a[..., :, None], a.shape + (t,))
    ar = jnp.where(jnp.tril(jnp.ones((t, t), bool), -1), ar, 0.0)
    ss = jnp.cumsum(ar, axis=-2)
    return jnp.where(jnp.tril(jnp.ones((t, t), bool), 0), ss, -jnp.inf)

def ssd_chunked(x, a_dt, bm, cm):
    b, s, h, p = x.shape
    n = bm.shape[-1]
    q = SSM_CHUNK
    c = s // q
    x = x.reshape(b, c, q, h, p)
    bm = bm.reshape(b, c, q, h, n)
    cm = cm.reshape(b, c, q, h, n)
    a = a_dt.reshape(b, c, q, h).transpose(0, 3, 1, 2)
    a_cs = jnp.cumsum(a, axis=-1)
    decay_in = jnp.exp(segsum(a))
    scores = jnp.einsum('bclhn,bcshn->bhcls', cm, bm) * decay_in
    y_diag = jnp.einsum('bhcls,bcshp->bclhp', scores, x)
    decay_to_end = jnp.exp(a_cs[..., -1:] - a_cs).transpose(0, 2, 3, 1)
    states = jnp.einsum('bclhn,bclhp->bchpn', bm * decay_to_end[..., None], x)
    states = jnp.concatenate([jnp.zeros_like(states[:, :1]), states], axis=1)
    chunk_decay = jnp.exp(segsum(jnp.pad(a_cs[..., -1], ((0, 0), (0, 0), (1, 0)))))
    states = jnp.einsum('bhzc,bchpn->bzhpn', chunk_decay, states)[:, :-1]
    decay_from_start = jnp.exp(a_cs).transpose(0, 2, 3, 1)
    y_off = jnp.einsum('bclhn,bchpn->bclhp', cm, states) * decay_from_start[..., None]
    return (y_diag + y_off).reshape(b, s, h, p)

def ssd_mixer(cols, conv_w, conv_b, dt_bias, a_log, d_skip, norm_w):
    b, s, _ = cols.shape
    di = SSM_HEADS * SSM_HEAD_DIM
    z, xbc, dt = jnp.split(cols, [di, di + SSM_XBC], axis=-1)
    xbc = jax.nn.silu(causal_dwconv(xbc, conv_w, conv_b)).astype(jnp.float32)
    xs, bm, cm = jnp.split(xbc, [di, di + SSM_GROUPS * SSM_STATE], axis=-1)
    rep = SSM_HEADS // SSM_GROUPS
    xs = xs.reshape(b, s, SSM_HEADS, SSM_HEAD_DIM)
    bm = jnp.repeat(bm.reshape(b, s, SSM_GROUPS, SSM_STATE), rep, axis=2)
    cm = jnp.repeat(cm.reshape(b, s, SSM_GROUPS, SSM_STATE), rep, axis=2)
    dt = jax.nn.softplus(dt.astype(jnp.float32) + dt_bias.astype(jnp.float32))
    a = -jnp.exp(a_log.astype(jnp.float32))
    y = ssd_chunked(xs * dt[..., None], dt * a, bm, cm)
    y = y + xs * d_skip.astype(jnp.float32)[:, None]
    y = y.reshape(b, s, di) * jax.nn.silu(z.astype(jnp.float32))
    yg = y.reshape(b, s, SSM_GROUPS, di // SSM_GROUPS)
    yg = yg * lax.rsqrt(jnp.mean(yg * yg, axis=-1, keepdims=True) + NORM_EPS)
    return (yg.reshape(b, s, di) * norm_w).astype(cols.dtype)

def linear_recurrence(a, u):
    def combine(l, r):
        return l[0] * r[0], r[0] * l[1] + r[1]
    _, h = lax.associative_scan(combine, (a, u), axis=1)
    return h

def rglru_mixer(cols, conv_w, conv_b, wa, ba, wi, bi, lam):
    b, s, _ = cols.shape
    gate, xr = jnp.split(cols, [GROUP_WIDTH], axis=-1)
    xr = causal_dwconv(xr, conv_w, conv_b).astype(jnp.float32)
    xb = xr.reshape(b, s, LRU_BLOCKS, LRU_BLOCK_DIM)
    r = jax.nn.sigmoid(jnp.einsum('bshi,hij->bshj', xb, wa.astype(jnp.float32)) + ba)
    i = jax.nn.sigmoid(jnp.einsum('bshi,hij->bshj', xb, wi.astype(jnp.float32)) + bi)
    log_sig_lam = -jax.nn.softplus(-lam.astype(jnp.float32).reshape(LRU_BLOCKS, LRU_BLOCK_DIM))
    log_a = LRU_C * r * log_sig_lam
    a = jnp.exp(log_a)
    u = jnp.sqrt(-jnp.expm1(2.0 * log_a)) * (i * xb)
    h = linear_recurrence(a, u)
    y = h.reshape(b, s, GROUP_WIDTH) * jax.nn.gelu(gate.astype(jnp.float32))
    return y.astype(cols.dtype)

def rwkv7_scan(r, w, k, v, kk, a):
    b, s, h, n = r.shape

    def step(state, inp):
        r_t, w_t, k_t, v_t, kk_t, a_t = inp
        sa = jnp.einsum('bhij,bhj->bhi', state, -kk_t)
        state = (state * w_t[:, :, None, :] + sa[..., None] * (kk_t * a_t)[:, :, None, :]
                 + v_t[..., None] * k_t[:, :, None, :])
        y_t = jnp.einsum('bhij,bhj->bhi', state, r_t)
        return state, y_t

    xs = tuple(jnp.moveaxis(t, 1, 0) for t in (r, w, k, v, kk, a))
    state0 = jnp.zeros((b, h, n, n), jnp.float32)
    _, y = lax.scan(step, state0, xs)
    return jnp.moveaxis(y, 0, 1)

def rwkv7_mixer(cols, mu, w0, w2, a0, a2, g2, k_k, k_a, r_k, ln_w, ln_b):
    b, s, _ = cols.shape
    c = cols.astype(jnp.float32)
    c = c + (shift_right(c) - c) * mu
    g_ = GROUP_WIDTH
    r, k, v, wd, ad, gd = jnp.split(
        c, [g_, 2 * g_, 3 * g_, 3 * g_ + RWKV_DECAY_LORA, 3 * g_ + RWKV_DECAY_LORA + RWKV_ICLR_LORA], axis=-1)
    w_log = -jax.nn.softplus(-(w0 + jnp.tanh(wd) @ w2)) - 0.5
    decay = jnp.exp(-jnp.exp(w_log))
    a = jax.nn.sigmoid(a0 + ad @ a2)
    g = jax.nn.sigmoid(gd) @ g2
    hs = lambda t: t.reshape(b, s, RWKV_HEADS, RWKV_HEAD_DIM)
    kk = hs(k * k_k)
    kk = kk / jnp.maximum(jnp.sqrt(jnp.sum(kk * kk, axis=-1, keepdims=True)), 1e-12)
    k = k * (1.0 + (a - 1.0) * k_a)
    r, decay, k, v, a = hs(r), hs(decay), hs(k), hs(v), hs(a)
    y = rwkv7_scan(r, decay, k, v, kk, a)
    mean = jnp.mean(y, axis=-1, keepdims=True)
    var = jnp.mean((y - mean) ** 2, axis=-1, keepdims=True)
    y = ((y - mean) * lax.rsqrt(var + RWKV_GN_EPS)).reshape(b, s, g_) * ln_w + ln_b
    y = y + (jnp.sum(r * k * r_k, axis=-1, keepdims=True) * v).reshape(b, s, g_)
    return (y * g).astype(cols.dtype)

def compress_blocks(t, pos_emb, w1, w2):
    b, s, d = t.shape
    ch = t.reshape(b, s // NSA_CMP_STRIDE, NSA_CMP_STRIDE, d)
    blocks = jnp.concatenate([ch[:, :-1], ch[:, 1:]], axis=2) + pos_emb
    hdn = jax.nn.gelu(blocks.reshape(b, blocks.shape[1], NSA_CMP_LEN * d) @ w1)
    return hdn @ w2

def nsa_overlap(s):
    nb = s // NSA_CMP_STRIDE - 1
    nsel = s // NSA_SEL_BLOCK
    cs = np.arange(nb) * NSA_CMP_STRIDE
    ss = np.arange(nsel) * NSA_SEL_BLOCK
    ov = np.minimum(cs[:, None] + NSA_CMP_LEN, ss[None, :] + NSA_SEL_BLOCK) - np.maximum(cs[:, None], ss[None, :])
    return jnp.asarray(np.clip(ov, 0, None) / NSA_CMP_LEN, jnp.float32)

def nsa_mixer(cols, cmp_pos, cmp_w1, cmp_w2, slopes):
    b, s, _ = cols.shape
    hd = NSA_HEAD_DIM
    qd = NSA_HEADS * hd
    q, kc, vc, ks, vs, kw, vw, gates = jnp.split(
        cols, [qd, qd + hd, qd + 2 * hd, qd + 3 * hd, qd + 4 * hd, qd + 5 * hd, qd + 6 * hd], axis=-1)
    q = q.reshape(b, s, NSA_HEADS, hd) * (hd ** -0.5)
    gates = jax.nn.sigmoid(gates.astype(jnp.float32).reshape(b, s, NSA_HEADS, 3))
    pos = jnp.arange(s)

    kcmp = compress_blocks(kc, cmp_pos[0], cmp_w1[0], cmp_w2[0])
    vcmp = compress_blocks(vc, cmp_pos[1], cmp_w1[1], cmp_w2[1])
    nb = kcmp.shape[1]
    blk_end = jnp.arange(nb) * NSA_CMP_STRIDE + NSA_CMP_LEN - 1
    dist = pos[:, None] - blk_end[None, :]
    sc = jnp.einsum('bshd,bnd->bhsn', q, kcmp).astype(jnp.float32) - slopes[:, None, None] * dist
    p_cmp = masked_softmax(sc, dist >= 0)
    o_cmp = jnp.einsum('bhsn,bnd->bshd', p_cmp.astype(vcmp.dtype), vcmp)

    nsel = s // NSA_SEL_BLOCK
    n_top = min(NSA_SEL_TOPN, nsel)
    imp = jnp.einsum('bhsn,nj->bsj', p_cmp, nsa_overlap(s))
    j = jnp.arange(nsel)
    cur = pos // NSA_SEL_BLOCK
    forced = (j[None, :] == 0) | (j[None, :] == cur[:, None]) | (j[None, :] == cur[:, None] - 1)
    imp = jnp.where(forced, NSA_FORCE, imp)
    imp = jnp.where(j[None, :] * NSA_SEL_BLOCK <= pos[:, None], imp, -jnp.inf)
    _, sel_idx = lax.top_k(imp, n_top)

    kw_pad = jnp.pad(kw, ((0, 0), (NSA_WINDOW, 0), (0, 0)))
    vw_pad = jnp.pad(vw, ((0, 0), (NSA_WINDOW, 0), (0, 0)))
    win_len = NSA_WINDOW + NSA_Q_BLOCK
    in_blk = jnp.arange(NSA_SEL_BLOCK)
    qb_len = NSA_Q_BLOCK

    def q_block(i):
        q0 = i * qb_len
        qb = lax.dynamic_slice_in_dim(q, q0, qb_len, axis=1)
        tq = q0 + jnp.arange(qb_len)
        idx = lax.dynamic_slice_in_dim(sel_idx, q0, qb_len, axis=1)
        tok = (idx[..., None] * NSA_SEL_BLOCK + in_blk).reshape(b, qb_len, n_top * NSA_SEL_BLOCK)
        kg = jax.vmap(lambda a_, i_: a_[i_])(ks, tok)
        vg = jax.vmap(lambda a_, i_: a_[i_])(vs, tok)
        d_sel = tq[None, :, None] - tok
        ssel = (jnp.einsum('bqhd,bqld->bhql', qb, kg).astype(jnp.float32)
                - slopes[None, :, None, None] * d_sel[:, None])
        p_sel = masked_softmax(ssel, (d_sel >= 0)[:, None])
        o_sel = jnp.einsum('bhql,bqld->bqhd', p_sel.astype(vg.dtype), vg)
        kwb = lax.dynamic_slice_in_dim(kw_pad, q0, win_len, axis=1)
        vwb = lax.dynamic_slice_in_dim(vw_pad, q0, win_len, axis=1)
        tk = q0 - NSA_WINDOW + jnp.arange(win_len)
        d_win = tq[:, None] - tk[None, :]
        m_win = (d_win >= 0) & (d_win < NSA_WINDOW) & (tk[None, :] >= 0)
        swin = jnp.einsum('bqhd,bkd->bhqk', qb, kwb).astype(jnp.float32) - slopes[:, None, None] * d_win
        p_win = masked_softmax(swin, m_win)
        o_win = jnp.einsum('bhqk,bkd->bqhd', p_win.astype(vwb.dtype), vwb)
        return o_sel, o_win

    o_sel, o_win = lax.map(q_block, jnp.arange(s // qb_len))
    o_sel = jnp.moveaxis(o_sel, 0, 1).reshape(b, s, NSA_HEADS, hd)
    o_win = jnp.moveaxis(o_win, 0, 1).reshape(b, s, NSA_HEADS, hd)
    out = gates[..., 0:1] * o_cmp + gates[..., 1:2] * o_sel + gates[..., 2:3] * o_win
    return out.reshape(b, s, qd).astype(cols.dtype)

def peer_ffn(x, wq, keys, u, v):
    b, s, d = x.shape
    t = b * s
    xt = x.reshape(t, d)
    q = (xt @ wq).reshape(t, PEER_HEADS, 2, PEER_KEY_DIM)
    sc = jnp.einsum('thcd,hcnd->thcn', q, keys).astype(jnp.float32)
    s1, i1 = lax.top_k(sc[:, :, 0], PEER_TOPK)
    s2, i2 = lax.top_k(sc[:, :, 1], PEER_TOPK)
    cand = (s1[..., :, None] + s2[..., None, :]).reshape(t, PEER_HEADS, PEER_TOPK * PEER_TOPK)
    cidx = (i1[..., :, None] * PEER_NKEYS + i2[..., None, :]).reshape(t, PEER_HEADS, PEER_TOPK * PEER_TOPK)
    top, pos = lax.top_k(cand, PEER_TOPK)
    eidx = jnp.take_along_axis(cidx, pos, axis=-1)
    gate = jax.nn.softmax(top, axis=-1)
    nc = t // PEER_TOKEN_CHUNK
    xc = xt.reshape(nc, PEER_TOKEN_CHUNK, d)
    ic = eidx.reshape(nc, PEER_TOKEN_CHUNK, PEER_HEADS * PEER_TOPK)
    gc = gate.reshape(nc, PEER_TOKEN_CHUNK, PEER_HEADS * PEER_TOPK).astype(x.dtype)

    def chunk(args):
        xb, ib, gb = args
        act = jax.nn.gelu(jnp.einsum('td,tkd->tk', xb, u[ib]))
        return jnp.einsum('tk,tkd->td', gb * act, v[ib])

    y = lax.map(chunk, (xc, ic, gc))
    return y.reshape(b, s, d)

def setup_inputs(seed: int = 0) -> dict:
    key = jax.random.key(seed)
    keys = jax.random.split(key, 48)
    counter = [0]

    def nk():
        counter[0] += 1
        return keys[counter[0] - 1]

    def nrm(shape, scale):
        return scale * jax.random.normal(nk(), shape, jnp.float32)

    def unif(shape, lo, hi):
        return jax.random.uniform(nk(), shape, jnp.float32, lo, hi)

    L = DEPTH
    x = nrm((BATCH, SEQ, D_MODEL), 1.0)
    mix_norm = 1.0 + nrm((L, D_MODEL), 0.02)
    w_in = nrm((L, D_MODEL, N_IN), D_MODEL ** -0.5)
    w_out = nrm((L, MIX_WIDTH, D_MODEL), 0.5 * MIX_WIDTH ** -0.5)
    ssm_conv_w = nrm((L, SSM_CONV, SSM_XBC), SSM_CONV ** -0.5)
    ssm_conv_b = nrm((L, SSM_XBC), 0.01)
    dt0 = jnp.exp(unif((L, SSM_HEADS), math.log(1e-3), math.log(1e-1)))
    ssm_dt_bias = dt0 + jnp.log(-jnp.expm1(-dt0))
    ssm_a_log = jnp.log(unif((L, SSM_HEADS), 1.0, 16.0))
    ssm_d = 1.0 + nrm((L, SSM_HEADS), 0.1)
    ssm_norm = 1.0 + nrm((L, GROUP_WIDTH), 0.02)
    lru_conv_w = nrm((L, LRU_CONV, GROUP_WIDTH), LRU_CONV ** -0.5)
    lru_conv_b = nrm((L, GROUP_WIDTH), 0.01)
    lru_wa = nrm((L, LRU_BLOCKS, LRU_BLOCK_DIM, LRU_BLOCK_DIM), LRU_BLOCK_DIM ** -0.5)
    lru_ba = nrm((L, LRU_BLOCKS, LRU_BLOCK_DIM), 0.01)
    lru_wi = nrm((L, LRU_BLOCKS, LRU_BLOCK_DIM, LRU_BLOCK_DIM), LRU_BLOCK_DIM ** -0.5)
    lru_bi = nrm((L, LRU_BLOCKS, LRU_BLOCK_DIM), 0.01)
    p_lam = unif((L, GROUP_WIDTH), 0.9, 0.999) ** (1.0 / LRU_C)
    lru_lambda = jnp.log(p_lam) - jnp.log1p(-p_lam)
    rwkv_mu = unif((L, RWKV_IN), 0.0, 1.0)
    rwkv_w0 = unif((L, GROUP_WIDTH), -5.0, -1.0)
    rwkv_w2 = nrm((L, RWKV_DECAY_LORA, GROUP_WIDTH), 0.5 * RWKV_DECAY_LORA ** -0.5)
    rwkv_a0 = nrm((L, GROUP_WIDTH), 0.1)
    rwkv_a2 = nrm((L, RWKV_ICLR_LORA, GROUP_WIDTH), 0.5 * RWKV_ICLR_LORA ** -0.5)
    rwkv_g2 = nrm((L, RWKV_GATE_LORA, GROUP_WIDTH), RWKV_GATE_LORA ** -0.5)
    rwkv_kk = 0.85 + nrm((L, GROUP_WIDTH), 0.05)
    rwkv_ka = 1.0 + nrm((L, GROUP_WIDTH), 0.05)
    rwkv_rk = nrm((L, RWKV_HEADS, RWKV_HEAD_DIM), 0.1)
    rwkv_ln_w = 1.0 + nrm((L, GROUP_WIDTH), 0.02)
    rwkv_ln_b = nrm((L, GROUP_WIDTH), 0.01)
    nsa_cmp_pos = nrm((L, 2, NSA_CMP_LEN, NSA_HEAD_DIM), 0.02)
    nsa_cmp_w1 = nrm((L, 2, NSA_CMP_LEN * NSA_HEAD_DIM, NSA_CMP_HIDDEN), (NSA_CMP_LEN * NSA_HEAD_DIM) ** -0.5)
    nsa_cmp_w2 = nrm((L, 2, NSA_CMP_HIDDEN, NSA_HEAD_DIM), NSA_CMP_HIDDEN ** -0.5)
    ffn_norm = 1.0 + nrm((L, D_MODEL), 0.02)
    peer_wq = nrm((L, D_MODEL, PEER_HEADS * 2 * PEER_KEY_DIM), D_MODEL ** -0.5)
    peer_keys = nrm((L, PEER_HEADS, 2, PEER_NKEYS, PEER_KEY_DIM), PEER_KEY_DIM ** -0.5)
    peer_u = nrm((L, PEER_EXPERTS, D_MODEL), D_MODEL ** -0.5)
    peer_v = nrm((L, PEER_EXPERTS, D_MODEL), (PEER_HEADS * PEER_TOPK) ** -0.5)
    final_norm = 1.0 + nrm((D_MODEL,), 0.02)
    return {"x": x, "mix_norm": mix_norm, "w_in": w_in, "w_out": w_out,
            "ssm_conv_w": ssm_conv_w, "ssm_conv_b": ssm_conv_b, "ssm_dt_bias": ssm_dt_bias,
            "ssm_a_log": ssm_a_log, "ssm_d": ssm_d, "ssm_norm": ssm_norm,
            "lru_conv_w": lru_conv_w, "lru_conv_b": lru_conv_b, "lru_wa": lru_wa, "lru_ba": lru_ba,
            "lru_wi": lru_wi, "lru_bi": lru_bi, "lru_lambda": lru_lambda,
            "rwkv_mu": rwkv_mu, "rwkv_w0": rwkv_w0, "rwkv_w2": rwkv_w2, "rwkv_a0": rwkv_a0,
            "rwkv_a2": rwkv_a2, "rwkv_g2": rwkv_g2, "rwkv_kk": rwkv_kk, "rwkv_ka": rwkv_ka,
            "rwkv_rk": rwkv_rk, "rwkv_ln_w": rwkv_ln_w, "rwkv_ln_b": rwkv_ln_b,
            "nsa_cmp_pos": nsa_cmp_pos, "nsa_cmp_w1": nsa_cmp_w1, "nsa_cmp_w2": nsa_cmp_w2,
            "ffn_norm": ffn_norm, "peer_wq": peer_wq, "peer_keys": peer_keys,
            "peer_u": peer_u, "peer_v": peer_v, "final_norm": final_norm}

def reference(x, mix_norm, w_in, w_out, ssm_conv_w, ssm_conv_b, ssm_dt_bias, ssm_a_log, ssm_d, ssm_norm,
              lru_conv_w, lru_conv_b, lru_wa, lru_ba, lru_wi, lru_bi, lru_lambda,
              rwkv_mu, rwkv_w0, rwkv_w2, rwkv_a0, rwkv_a2, rwkv_g2, rwkv_kk, rwkv_ka, rwkv_rk,
              rwkv_ln_w, rwkv_ln_b, nsa_cmp_pos, nsa_cmp_w1, nsa_cmp_w2,
              ffn_norm, peer_wq, peer_keys, peer_u, peer_v, final_norm):
    slopes = alibi_slopes(NSA_HEADS)
    splits = [SSM_IN, SSM_IN + LRU_IN, SSM_IN + LRU_IN + RWKV_IN]
    h = x
    for l in range(DEPTH):
        u = rms_norm(h, mix_norm[l])
        cols = u @ w_in[l]
        c_ssm, c_lru, c_rwkv, c_nsa = jnp.split(cols, splits, axis=-1)
        y_ssm = ssd_mixer(c_ssm, ssm_conv_w[l], ssm_conv_b[l], ssm_dt_bias[l], ssm_a_log[l], ssm_d[l], ssm_norm[l])
        y_lru = rglru_mixer(c_lru, lru_conv_w[l], lru_conv_b[l], lru_wa[l], lru_ba[l], lru_wi[l], lru_bi[l],
                            lru_lambda[l])
        y_rwkv = rwkv7_mixer(c_rwkv, rwkv_mu[l], rwkv_w0[l], rwkv_w2[l], rwkv_a0[l], rwkv_a2[l], rwkv_g2[l],
                             rwkv_kk[l], rwkv_ka[l], rwkv_rk[l], rwkv_ln_w[l], rwkv_ln_b[l])
        y_nsa = nsa_mixer(c_nsa, nsa_cmp_pos[l], nsa_cmp_w1[l], nsa_cmp_w2[l], slopes)
        mixed = jnp.concatenate([y_ssm, y_lru, y_rwkv, y_nsa], axis=-1)
        h = h + mixed @ w_out[l]
        h = h + peer_ffn(rms_norm(h, ffn_norm[l]), peer_wq[l], peer_keys[l], peer_u[l], peer_v[l])
    return rms_norm(h, final_norm)


_drawn_inputs = setup_inputs


def setup_inputs(seed=0):
    import zlib

    import numpy as np

    out = dict(_drawn_inputs(seed))
    spreads = {}
    factors = {'mix_norm': 3.515,
     'ssm_conv_b': 22.407,
     'ssm_norm': 29.288,
     'lru_conv_b': 4.756,
     'lru_ba': 64.0,
     'lru_bi': 43.648,
     'rwkv_w2': 7.251,
     'rwkv_a0': 5.791,
     'rwkv_kk': 43.349,
     'rwkv_ka': 4.873,
     'rwkv_ln_w': 46.824,
     'rwkv_ln_b': 64.0,
     'nsa_cmp_pos': 46.033,
     'ffn_norm': 22.228,
     'final_norm': 7.186,
     'ssm_d': 8.0}
    for name, (base, spread) in spreads.items():
        noise = np.random.default_rng([zlib.crc32(name.encode()), seed]).standard_normal(out[name].shape)
        drawn = base * np.exp(spread * noise) if base else spread * noise
        out[name] = __import__('jax').numpy.asarray(drawn.astype(out[name].dtype))
    for name, factor in factors.items():
        out[name] = (out[name] * factor).astype(out[name].dtype)
    return out
```

```python
import math
from contextlib import ExitStack, contextmanager

import numpy as np
import concourse.bass as bass
from concourse import mybir

F32 = mybir.dt.float32
U32 = mybir.dt.uint32
ALU = mybir.AluOpType
ACT = mybir.ActivationFunctionType
AX = mybir.AxisListType

P = 128
SEQ = 512
DM = 1024
DEPTH = 2
TT = SEQ // P
DB = DM // P
EPS = 1e-6
GN_EPS = 64e-5
NEG = -1e30

T_Z, T_X, T_B, T_C, T_GATE, T_XR = 0, 2, 4, 5, 6, 8
T_R, T_K, T_V, T_WDAD, T_GD = 10, 12, 14, 16, 17
T_Q, T_CMP, T_KSKW, T_VSVW, T_SMALL = 18, 20, 21, 22, 23
N_COLS = 24
LEAD = 4
SLOTS = 4

VEC = {}


def _columns():
    at = 0
    for name, n in (("mix_norm", 8), ("ffn_norm", 8), ("ssm_cw", 16), ("ssm_cb", 4), ("ssm_norm", 2), ("ssm_d", 2),
                    ("lru_cw", 8), ("lru_cb", 2), ("lru_ba", 2), ("lru_bi", 2), ("lru_lam", 2), ("mu", 8),
                    ("w0", 2), ("a0", 2), ("kk", 2), ("ka", 2), ("rk", 2), ("ln_w", 2), ("ln_b", 2),
                    ("dt_bias", 4), ("a_log", 4), ("pos", 32)):
        VEC[name] = at
        at += n
    return at


N_VEC = _columns()


class Named:
    pass


@contextmanager
def stage(nc, *names):
    with ExitStack() as held:
        sems = {n: held.enter_context(nc.semaphore(n)) for n in names}
        with nc.Block() as block:
            yield block, sems
        for s in sems.values():
            nc.sync.sem_clear(s)
        nc.all_engine_barrier()


def in_order(engine, done):
    count = [0]

    def step(instruction):
        count[0] += 1
        instruction.then_inc(done, 1)
        engine.wait_ge(done, count[0])
    return step


def make_constants(nc, k):
    with stage(nc, "const_done") as (block, s):
        @block.gpsimd
        def _(pool):
            step = in_order(pool, s["const_done"])
            step(nc.gpsimd.memset(k.ones[:, :], 1.0))

            def keep(out, src, pattern, base, mult, op=ALU.is_ge, fill=0.0):
                step(nc.gpsimd.affine_select(out=out, in_=src, compare_op=op, fill=fill, base=base,
                                             pattern=pattern, channel_multiplier=mult))
            one = k.ones[:, :]
            keep(k.ident[:, :], one, [[-1, P]], 0, 1, ALU.is_equal)
            keep(k.upper[:, :], one, [[1, P]], 0, -1)
            keep(k.strict[:, :], one, [[1, P]], -1, -1)
            keep(k.lower[:, :], one, [[-1, P]], -1, 1)
            for b in (8, 16, 32, 64):
                m = k.same[b][:, :].rearrange("p (n w) -> p n w", w=b)
                o = one.rearrange("p (n w) -> p n w", w=b)
                keep(m, o, [[-b, P // b], [0, b]], 0, 1)
                keep(m, m, [[b, P // b], [0, b]], b - 1, -1)
            step(nc.gpsimd.memset(k.reset[:, :], 1.0))
            step(nc.gpsimd.memset(k.reset[:, :].rearrange("p (c w) -> p c w", w=32)[:, :, 0:1], 0.0))
            step(nc.gpsimd.iota(k.iota16[:, :], pattern=[[1, 16]], base=0, channel_multiplier=0,
                                allow_small_or_imprecise_dtypes=True))
            step(nc.gpsimd.iota(k.iota128[:, :], pattern=[[1, P]], base=0, channel_multiplier=0,
                                allow_small_or_imprecise_dtypes=True))


def load_layer_vectors(nc, k, A, l):
    with stage(nc, "vectors_in", "zeroed") as (block, s):
        @block.sync
        def _(sp):
            for dst, name in ((k.vec[:, :], "vecs"), (k.lru_w[:, :, :, :].rearrange("p n i j -> p (n i j)"), "lru_w"),
                              (k.lora[:, :], "lora")):
                sp.dma_start(dst, A[name][bass.ds(l, 1), :, :].rearrange("a p c -> (a p) c")).then_inc(s["vectors_in"], 16)
            sp.wait_ge(s["vectors_in"], 48)

        @block.gpsimd
        def _(pool):
            nc.gpsimd.memset(k.cols[:, :, 0:LEAD], 0.0).then_inc(s["zeroed"], 1)


def norm_and_transpose(nc, k, gain):
    with stage(nc, "squares", "variance", "deviation", "inverse", "scaled", "turned") as (block, s):
        @block.scalar
        def _(act):
            for t in range(TT):
                if t:
                    act.wait_ge(s["squares"], t)
                nc.scalar.activation(k.wide[:, 0, :], k.h[:, t, :], ACT.Square,
                                     accum_out=k.stat[:, t:t + 1]).then_inc(s["squares"], 1)
            act.wait_ge(s["variance"], 1)
            nc.scalar.activation(k.stat[:, 8:12], k.stat[:, 4:8], ACT.Sqrt).then_inc(s["deviation"], 1)
            for b in range(0, DB, 2):
                act.wait_ge(s["turned"], b + 1)
                nc.scalar.activation(k.xT[:, b, :], k.bank[b][:, :], ACT.Copy, scale=k.vec[:, gain + b:gain + b + 1])

        @block.vector
        def _(dve):
            dve.wait_ge(s["squares"], TT)
            nc.vector.tensor_scalar(k.stat[:, 4:8], k.stat[:, 0:4], 1.0 / DM, EPS, ALU.mult, ALU.add).then_inc(s["variance"], 1)
            dve.wait_ge(s["deviation"], 1)
            nc.vector.reciprocal(k.stat[:, 12:16], k.stat[:, 8:12]).then_inc(s["inverse"], 1)
            dve.wait_ge(s["inverse"], 1)
            for t in range(TT):
                nc.vector.tensor_scalar(k.wide[:, t, :], k.h[:, t, :], k.stat[:, 12 + t:13 + t], None,
                                        ALU.mult).then_inc(s["scaled"], 1)
            for b in range(1, DB, 2):
                dve.wait_ge(s["turned"], b + 1)
                nc.vector.tensor_scalar(k.xT[:, b, :], k.bank[b][:, :], k.vec[:, gain + b:gain + b + 1], None, ALU.mult)

        @block.tensor
        def _(pe):
            pe.wait_ge(s["scaled"], TT)
            for b in range(DB):
                for t in range(TT):
                    last = nc.tensor.transpose(k.bank[b][:, t * P:(t + 1) * P], k.wide[:, t, b * P:(b + 1) * P],
                                               k.ident[:, :])
                last.then_inc(s["turned"], 1)


def project(nc, k, weights, layer_tile, n_tiles, out, lead):
    per = SLOTS
    with stage(nc, "tile_done", "act_out", "dve_out", *[f"weights_in{u}" for u in range(per)]) as (block, s):
        loaded = (s["weights_in0"], s["weights_in1"], s["weights_in2"], s["weights_in3"])

        @block.sync
        def _(sp):
            for u in range(per):
                sp.dma_start(k.ring[:, u, :], weights[bass.ds(layer_tile + u, 1), :, :].rearrange("a p c -> (a p) c")).then_inc(loaded[u], 16)
            with sp.Fori(1, n_tiles // per) as it:
                for u in range(per):
                    sp.wait_ge(s["tile_done"], it * per + (u + 1 - per))
                    sp.dma_start(k.ring[:, u, :], weights[bass.ds(layer_tile + it * per + u, 1), :, :]
                                 .rearrange("a p c -> (a p) c")).then_inc(loaded[u], 16)

        @block.tensor
        def _(pe):
            with pe.Fori(0, n_tiles // per) as it:
                for u in range(per):
                    pe.wait_ge(loaded[u], it * 16 + 16)
                    pe.wait_ge(s["dve_out"] if u % 2 else s["act_out"], it * (per // 2) + u // 2 + 1)
                    for b in range(DB):
                        last = nc.tensor.matmul(k.bank[u][:, :], k.ring[:, u, b * P:(b + 1) * P], k.xT[:, b, :],
                                                start=(b == 0), stop=(b == DB - 1))
                    last.then_inc(s["tile_done"], 1)

        def drain(engine, first, freed, copy):
            engine.sem_inc(freed, per // 2)
            with engine.Fori(0, n_tiles // per) as it:
                for u in range(first, per, 2):
                    engine.wait_ge(s["tile_done"], it * per + u + 1)
                    copy(out[:, bass.ds(it * per + u, 1), lead:lead + SEQ].rearrange("p a t -> p (a t)"),
                         k.bank[u][:, :]).then_inc(freed, 1)

        @block.scalar
        def _(act):
            drain(act, 0, s["act_out"], nc.scalar.copy)

        @block.vector
        def _(dve):
            drain(dve, 1, s["dve_out"], nc.vector.tensor_copy)


def lay_out(a):
    L = DEPTH
    f = np.ascontiguousarray
    w = a["w_in"]
    s0, s1, s2 = 772, 1284, 2308
    cols = np.concatenate([np.arange(0, 768), np.arange(s0, s0 + 512), np.arange(s1, s1 + 1024),
                           np.arange(s2, s2 + 256),
                           np.arange(s2 + 256, s2 + 384),
                           np.arange(s2 + 384, s2 + 448), np.arange(s2 + 512, s2 + 576),
                           np.arange(s2 + 448, s2 + 512), np.arange(s2 + 576, s2 + 640),
                           np.arange(768, 772), np.arange(s2 + 640, s2 + 652)])
    wi = np.zeros((L, DM, N_COLS * P), np.float32)
    wi[:, :, :cols.size] = w[:, :, cols]
    tile_w = lambda m, n: f(m.reshape(L, DB, P, n, P).transpose(0, 3, 2, 1, 4).reshape(L * n, P, DB * P))

    def chan(v, n):
        return v.reshape(L, n, P).transpose(0, 2, 1)
    conv = lambda v, n: v.reshape(L, 4, n, P).transpose(0, 3, 2, 1).reshape(L, P, n * 4)
    rows = lambda v: np.broadcast_to(v[:, None, :], (L, P, v.shape[1]))
    vecs = np.concatenate([
        chan(a["mix_norm"], 8), chan(a["ffn_norm"], 8), conv(a["ssm_conv_w"], 4), chan(a["ssm_conv_b"], 4),
        chan(a["ssm_norm"], 2), chan(np.repeat(a["ssm_d"], 64, axis=1), 2),
        conv(a["lru_conv_w"], 2), chan(a["lru_conv_b"], 2), chan(a["lru_ba"].reshape(L, 256), 2),
        chan(a["lru_bi"].reshape(L, 256), 2), chan(a["lru_lambda"], 2), chan(a["rwkv_mu"], 8),
        chan(a["rwkv_w0"], 2), chan(a["rwkv_a0"], 2), chan(a["rwkv_kk"], 2), chan(a["rwkv_ka"], 2),
        chan(a["rwkv_rk"].reshape(L, 256), 2), chan(a["rwkv_ln_w"], 2), chan(a["rwkv_ln_b"], 2),
        rows(a["ssm_dt_bias"]), rows(a["ssm_a_log"]),
        a["nsa_cmp_pos"].transpose(0, 1, 3, 2).reshape(L, P, 32)], axis=2)
    assert vecs.shape[2] == N_VEC
    return {
        "x": f(a["x"].reshape(TT, P, DM).transpose(1, 0, 2).reshape(P, TT * DM)),
        "w_in": tile_w(wi, N_COLS),
        "vecs": f(vecs),
        "lru_w": f(np.stack([a["lru_wa"].reshape(L, 2, P, 64), a["lru_wi"].reshape(L, 2, P, 64)], axis=1)
                   .transpose(0, 3, 1, 2, 4).reshape(L, P, 256)),
        "lora": f(np.concatenate([np.concatenate([a["rwkv_w2"], a["rwkv_a2"]], axis=1), a["rwkv_g2"]], axis=2)),
        "cmp_w1": f(a["nsa_cmp_w1"].reshape(L, 2, 32, 64, 256).transpose(0, 1, 3, 2, 4).reshape(L, P, 32 * 256)),
        "cmp_w2": f(a["nsa_cmp_w2"].reshape(L, 2, 2, P, 64).transpose(0, 3, 1, 2, 4).reshape(L, P, 256)),
        "w_out": f(a["w_out"].reshape(L, DB, P, DM)),
        "peer_wq": tile_w(a["peer_wq"], 16),
        "peer_keys": f(a["peer_keys"].reshape(L, 16, P, P).transpose(0, 3, 1, 2).reshape(L, P, 16 * P)),
        "peer_u": f(a["peer_u"].reshape(L, P, P, DB, P).transpose(0, 2, 4, 3, 1).reshape(L * P, P, DB * P)),
        "peer_v": f(a["peer_v"].reshape(L, P, P, DM).transpose(0, 2, 1, 3).reshape(L * P, P, DM)),
        "final_norm": f(a["final_norm"].reshape(1, DM)),
    }


def conv(nc, k, step, out, tile, weight, bias):
    src = k.cols[:, tile, :]
    step(nc.vector.tensor_scalar(out, src[:, LEAD - 3:LEAD - 3 + SEQ], k.vec[:, weight:weight + 1],
                                 k.vec[:, bias:bias + 1], ALU.mult, ALU.add))
    for tap in range(1, 4):
        step(nc.vector.scalar_tensor_tensor(out=out, in0=src[:, LEAD - 3 + tap:LEAD - 3 + tap + SEQ],
                                            scalar=k.vec[:, weight + tap:weight + tap + 1], in1=out,
                                            op0=ALU.mult, op1=ALU.add))


def log1p(nc, step, x, z, z2, p):
    step(nc.vector.tensor_scalar(z, x, 2.0, None, ALU.add))
    step(nc.vector.reciprocal(z2, z))
    step(nc.vector.tensor_tensor(z, x, z2, ALU.mult))
    step(nc.vector.tensor_tensor(z2, z, z, ALU.mult))
    step(nc.vector.tensor_scalar(p, z2, 2.0 / 15, 2.0 / 13, ALU.mult, ALU.add))
    for n in (11, 9, 7, 5, 3, 1):
        step(nc.vector.tensor_tensor(p, p, z2, ALU.mult))
        step(nc.vector.tensor_scalar(p, p, 2.0 / n, None, ALU.add))
    step(nc.vector.tensor_tensor(x, p, z, ALU.mult))


def ssd_mixer(nc, k):
    H = 4
    with ExitStack() as held:
        def sb(name, shape):
            return held.enter_context(nc.sbuf_tensor(name, shape, F32))
        sz = sb("ssd_silu_z", [P, 2, SEQ])
        c_pad = sb("ssd_c_pad", [P, 2, SEQ])
        xbc = k.wide[:, 0:2, :].rearrange("p a c -> p (a c)").rearrange("p (i t) -> p i t", t=SEQ)
        decay = k.wide[:, 2:4, :].rearrange("p a c -> p (a c)").rearrange("p (t h l) -> p t h l", t=TT, h=H)
        row_decay = k.xT[:, 0:4, :].rearrange("p t (h l) -> p t h l", h=H)
        scores = k.xT[:, 4:8, :].rearrange("p t (h l) -> p t h l", h=H)
        c_dec = sb("ssd_c_dec", [P, TT, H, P])
        dt = sb("ssd_dt", [P, TT * H])
        da = sb("ssd_da", [P, TT * H])
        t1 = sb("ssd_t1", [P, TT * H])
        t2 = sb("ssd_t2", [P, TT * H])
        t3 = sb("ssd_t3", [P, TT * H])
        ea = sb("ssd_ea", [P, H])
        cs = sb("ssd_cs", [P, TT * H])
        to_end = sb("ssd_to_end", [P, TT * H])
        bT = sb("ssd_bT", [P, TT, P])
        xdt = sb("ssd_xdt", [P, TT, H, 64])
        xde = sb("ssd_xde", [P, TT, H, 64])
        state = sb("ssd_state", [P, TT, H, 64])
        y = sb("ssd_y", [P, 2, SEQ])
        v4 = lambda t: t[:, :].rearrange("p (t h) -> p t h", h=H)
        with stage(nc, "dve_done", "conv_done", "silu_done", "small_turned", "dt_abs", "dt_exp", "a_exp", "da_ready",
                   "sums", "cs_out", "diffs", "exps", "row_exps", "turned", "xdt_ready", "c_ready", "gram",
                   "scores_ready", "state_sum", "state_ready", "y_sum", "gated", "squared", "norm_sum", "norm_var",
                   "norm_dev") as (block, s):
            @block.scalar
            def _(act):
                act.wait_ge(s["conv_done"], 4)
                nc.scalar.activation(xbc, xbc, ACT.Silu).then_inc(s["silu_done"], 1)
                nc.scalar.activation(sz[:, :, :], k.cols[:, T_Z:T_Z + 2, LEAD:LEAD + SEQ], ACT.Silu).then_inc(s["silu_done"], 1)
                nc.scalar.activation(ea[:, :], k.vec[:, VEC["a_log"]:VEC["a_log"] + H], ACT.Exp).then_inc(s["a_exp"], 1)
                act.wait_ge(s["dt_abs"], 1)
                nc.scalar.activation(dt[:, :], t3[:, :], ACT.Exp, scale=-1.0).then_inc(s["dt_exp"], 1)
                act.wait_ge(s["sums"], 1 + TT)
                for t in range(TT):
                    nc.scalar.activation(row_decay[:, t, :, :].rearrange("p h l -> p (h l)"), k.bank[t][:, :],
                                         ACT.Exp).then_inc(s["row_exps"], 1)
                act.wait_ge(s["diffs"], 1)
                nc.scalar.activation(to_end[:, :], to_end[:, :], ACT.Exp).then_inc(s["exps"], 1)
                act.wait_ge(s["diffs"], 2)
                nc.scalar.activation(decay, decay, ACT.Exp).then_inc(s["exps"], 1)
                for g in range(2):
                    act.wait_ge(s["gated"], g + 1)
                    nc.scalar.activation(k.xT[:, g, :], y[:, g, :], ACT.Square).then_inc(s["squared"], 1)
                for g in range(2):
                    act.wait_ge(s["norm_var"], g + 1)
                    nc.scalar.activation(k.xT[:, 2 + g, :], k.xT[:, 2 + g, :], ACT.Sqrt).then_inc(s["norm_dev"], 1)

            @block.vector
            def _(dve):
                step = in_order(dve, s["dve_done"])
                for i in range(4):
                    conv(nc, k, step, xbc[:, i, :], T_X + i, VEC["ssm_cw"] + 4 * i, VEC["ssm_cb"] + i)
                    dve.sem_inc(s["conv_done"], 1)
                dve.wait_ge(s["small_turned"], 1)
                step(nc.vector.tensor_copy(k.smallT[:, :, :], k.bank[5][:, 0:TT * 16].rearrange("p (t c) -> p t c", c=16)))
                step(nc.vector.tensor_tensor(v4(t1), k.smallT[:, :, 0:H],
                                             k.vec[:, VEC["dt_bias"]:VEC["dt_bias"] + H].unsqueeze(1).to_broadcast([P, TT, H]),
                                             ALU.add))
                nc.vector.scalar_tensor_tensor(out=t3[:, :], in0=t1[:, :], scalar=-1.0, in1=t1[:, :],
                                               op0=ALU.mult, op1=ALU.max).then_inc(s["dt_abs"], 1)
                dve.wait_ge(s["dt_exp"], 1)
                log1p(nc, step, dt[:, :], t2[:, :], t3[:, :], da[:, :])
                step(nc.vector.scalar_tensor_tensor(out=dt[:, :], in0=t1[:, :], scalar=0.0, in1=dt[:, :],
                                                    op0=ALU.max, op1=ALU.add))
                dve.wait_ge(s["a_exp"], 1)
                nc.vector.scalar_tensor_tensor(out=v4(da), in0=v4(dt), scalar=-1.0,
                                               in1=ea[:, :].unsqueeze(1).to_broadcast([P, TT, H]),
                                               op0=ALU.mult, op1=ALU.mult).then_inc(s["da_ready"], 1)
                dve.wait_ge(s["sums"], 1)
                step(nc.vector.tensor_copy(cs[:, :], k.bank[4][:, 0:TT * H]))
                dve.wait_ge(s["sums"], 1 + TT)
                for t in range(TT):
                    dve.wait_ge(s["row_exps"], t + 1)
                    last = nc.vector.tensor_tensor(v4(to_end)[:, t, :],
                                                   k.bank[t][:, :].rearrange("p (h l) -> p h l", h=H)[:, :, P - 1],
                                                   v4(cs)[:, t, :], ALU.subtract)
                last.then_inc(s["diffs"], 1)
                for t in range(TT):
                    for h in range(H):
                        last = nc.vector.tensor_scalar(decay[:, t, h, :], k.bank[t][:, h * P:(h + 1) * P],
                                                       cs[:, t * H + h:t * H + h + 1], 0.0, ALU.subtract, ALU.min)
                last.then_inc(s["diffs"], 1)
                dve.wait_ge(s["exps"], 2)
                step(nc.vector.tensor_tensor(decay.rearrange("p t h l -> p (t h) l"), decay.rearrange("p t h l -> p (t h) l"),
                                             k.upper[:, :].unsqueeze(1).to_broadcast([P, TT * H, P]), ALU.mult))
                dve.wait_ge(s["silu_done"], 1)
                step(nc.vector.memset(c_pad[:, :, :], 0.0))
                step(nc.vector.tensor_copy(c_pad[0:64, 0, :], xbc[0:64, 3, :]))
                nc.vector.tensor_copy(c_pad[64:128, 1, :], xbc[64:128, 3, :]).then_inc(s["c_ready"], 1)
                dve.wait_ge(s["c_ready"], 1)
                dve.wait_ge(s["row_exps"], TT)
                for t in range(TT):
                    for g in range(2):
                        last = nc.vector.tensor_tensor(
                            c_dec[:, t, 2 * g:2 * g + 2, :], row_decay[:, t, 2 * g:2 * g + 2, :],
                            c_pad[:, g, t * P:(t + 1) * P].unsqueeze(1).to_broadcast([P, 2, P]), ALU.mult)
                last.then_inc(s["c_ready"], 1)
                dve.wait_ge(s["turned"], 3)
                step(nc.vector.tensor_copy(bT[:, :, :], k.bank[7][:, :].rearrange("p (t n) -> p t n", t=TT)))
                for i in range(2):
                    for t in range(TT):
                        last = nc.vector.tensor_tensor(
                            xdt[:, t, 2 * i:2 * i + 2, :], k.bank[5 + i][:, t * P:(t + 1) * P].rearrange("p (h q) -> p h q", h=2),
                            v4(dt)[:, t, 2 * i:2 * i + 2].unsqueeze(2).to_broadcast([P, 2, 64]), ALU.mult)
                step(last)
                last = nc.vector.tensor_tensor(xde[:, :, :, :].rearrange("p t h q -> p (t h) q"),
                                               xdt[:, :, :, :].rearrange("p t h q -> p (t h) q"),
                                               to_end[:, :].unsqueeze(2).to_broadcast([P, TT * H, 64]), ALU.mult)
                last.then_inc(s["xdt_ready"], 1)
                for t in range(TT):
                    dve.wait_ge(s["gram"], t + 1)
                    for g in range(2):
                        last = nc.vector.tensor_tensor(
                            scores[:, t, 2 * g:2 * g + 2, :], decay[:, t, 2 * g:2 * g + 2, :],
                            k.bank[t][:, g * P:(g + 1) * P].unsqueeze(1).to_broadcast([P, 2, P]), ALU.mult)
                    last.then_inc(s["scores_ready"], 1)
                for t in range(TT - 1):
                    dve.wait_ge(s["state_sum"], t + 1)
                    new = k.bank[7][:, 0:256].rearrange("p (h q) -> p h q", h=H)
                    if t == 0:
                        nc.vector.tensor_copy(state[:, 1, :, :], new).then_inc(s["state_ready"], 1)
                        dve.wait_ge(s["state_ready"], 1)
                        continue
                    step(nc.vector.tensor_tensor(state[:, t + 1, :, :], state[:, t, :, :],
                                                 row_decay[:, t, :, P - 1].unsqueeze(2).to_broadcast([P, H, 64]), ALU.mult))
                    nc.vector.tensor_tensor(state[:, t + 1, :, :], state[:, t + 1, :, :], new, ALU.add).then_inc(s["state_ready"], 1)
                    dve.wait_ge(s["state_ready"], t + 1)
                dve.wait_ge(s["silu_done"], 2)
                dve.wait_ge(s["y_sum"], TT)
                for g in range(2):
                    step(nc.vector.scalar_tensor_tensor(out=y[:, g, :], in0=xbc[:, g, :],
                                                        scalar=k.vec[:, VEC["ssm_d"] + g:VEC["ssm_d"] + g + 1],
                                                        in1=k.bank[5 + g][:, :], op0=ALU.mult, op1=ALU.add))
                    nc.vector.tensor_tensor(y[:, g, :], y[:, g, :], sz[:, g, :], ALU.mult).then_inc(s["gated"], 1)
                for g in range(2):
                    dve.wait_ge(s["norm_sum"], g + 1)
                    nc.vector.tensor_scalar(k.xT[:, 2 + g, :], k.bank[g][:, :], 1.0 / P, EPS, ALU.mult, ALU.add).then_inc(s["norm_var"], 1)
                for g in range(2):
                    dve.wait_ge(s["norm_dev"], g + 1)
                    step(nc.vector.reciprocal(k.xT[:, 2 + g, :], k.xT[:, 2 + g, :]))
                    step(nc.vector.scalar_tensor_tensor(out=k.mixed[:, g, :], in0=y[:, g, :],
                                                        scalar=k.vec[:, VEC["ssm_norm"] + g:VEC["ssm_norm"] + g + 1],
                                                        in1=k.xT[:, 2 + g, :], op0=ALU.mult, op1=ALU.mult))

            @block.tensor
            def _(pe):
                for t in range(TT):
                    last = nc.tensor.transpose(k.bank[5][:, t * 16:(t + 1) * 16],
                                               k.cols[0:16, T_SMALL, LEAD + t * P:LEAD + (t + 1) * P], k.ident[0:16, 0:16])
                last.then_inc(s["small_turned"], 1)
                pe.wait_ge(s["da_ready"], 1)
                nc.tensor.matmul(k.bank[4][:, 0:TT * H], k.upper[:, :], da[:, :], start=True, stop=True).then_inc(s["sums"], 1)
                for t in range(TT):
                    for h in range(H):
                        last = nc.tensor.matmul(k.bank[t][:, h * P:(h + 1) * P],
                                                da[:, t * H + h:t * H + h + 1].to_broadcast([P, P]),
                                                k.upper[:, :], start=True, stop=True)
                    last.then_inc(s["sums"], 1)
                pe.wait_ge(s["silu_done"], 1)
                for i in range(3):
                    for t in range(TT):
                        last = nc.tensor.transpose(k.bank[5 + i][:, t * P:(t + 1) * P], xbc[:, i, t * P:(t + 1) * P], k.ident[:, :])
                    last.then_inc(s["turned"], 1)
                pe.wait_ge(s["c_ready"], 1)
                pe.wait_ge(s["row_exps"], TT)
                pe.wait_ge(s["diffs"], 2)
                for t in range(TT):
                    nc.tensor.matmul(k.bank[t][:, 0:256], xbc[:, 2, t * P:(t + 1) * P],
                                     c_pad[:, :, t * P:(t + 1) * P], start=True, stop=True).then_inc(s["gram"], 1)
                pe.wait_ge(s["c_ready"], 2)
                pe.wait_ge(s["xdt_ready"], 1)
                for t in range(TT):
                    if t < TT - 1:
                        if t:
                            pe.wait_ge(s["state_ready"], t)
                        nc.tensor.matmul(k.bank[7][:, 0:256], bT[:, t, :], xde[:, t, :, :].rearrange("p h q -> p (h q)"),
                                         start=True, stop=True).then_inc(s["state_sum"], 1)
                    pe.wait_ge(s["scores_ready"], t + 1)
                    if t:
                        pe.wait_ge(s["state_ready"], t)
                    for h in range(H):
                        r = 64 * (h % 2)
                        o = k.bank[5 + h // 2][r:r + 64, t * P:(t + 1) * P]
                        last = nc.tensor.matmul(o, xdt[:, t, h, :], scores[:, t, h, :], start=True, stop=(t == 0))
                        if t:
                            last = nc.tensor.matmul(o, state[:, t, h, :], c_dec[:, t, h, :], start=False, stop=True)
                    last.then_inc(s["y_sum"], 1)
                for g in range(2):
                    pe.wait_ge(s["squared"], g + 1)
                    nc.tensor.matmul(k.bank[g][:, :], k.ones[:, :], k.xT[:, g, :], start=True, stop=True).then_inc(s["norm_sum"], 1)


def lru_mixer(nc, k):
    with ExitStack() as held:
        def sb(name, shape):
            return held.enter_context(nc.sbuf_tensor(name, shape, F32))
        xr = k.wide[:, 0, :].rearrange("p (i t) -> p i t", t=SEQ)
        rate = k.wide[:, 1, :].rearrange("p (i t) -> p i t", t=SEQ)
        gate_i = k.wide[:, 2, :].rearrange("p (i t) -> p i t", t=SEQ)
        a = k.wide[:, 3, :].rearrange("p (i t) -> p i t", t=SEQ)
        th = k.xT[:, 0:2, :]
        den = k.xT[:, 2:4, :]
        gel = k.xT[:, 4:6, :]
        scan = k.xT[:, 6:8, :]
        x_pad = sb("lru_x_pad", [P, 2, 2, SEQ])
        lam = sb("lru_lam", [P, 2])
        l1 = sb("lru_l1", [P, 2])
        l2 = sb("lru_l2", [P, 2])
        l3 = sb("lru_l3", [P, 2])
        l4 = sb("lru_l4", [P, 2])
        with stage(nc, "dve_done", "x_ready", "gates_sum", "lam_abs", "lam_exp", "sigmoids", "rate_ready", "a_ready",
                   "tanhs", "u_sq", "root", "gelu_done") as (block, s):
            @block.scalar
            def _(act):
                act.wait_ge(s["lam_abs"], 1)
                nc.scalar.activation(l1[:, :], l4[:, :], ACT.Exp, scale=-1.0).then_inc(s["lam_exp"], 1)
                for i in range(2):
                    act.wait_ge(s["gates_sum"], i + 1)
                    for n, (dst, b) in enumerate(((rate, "lru_ba"), (gate_i, "lru_bi"))):
                        nc.scalar.activation(dst[:, i, :], k.bank[2 * i + n][:, :], ACT.Sigmoid,
                                             bias=k.vec[:, VEC[b] + i:VEC[b] + i + 1]).then_inc(s["sigmoids"], 1)
                act.wait_ge(s["rate_ready"], 2)
                nc.scalar.activation(a, rate, ACT.Exp).then_inc(s["a_ready"], 1)
                nc.scalar.activation(th, rate, ACT.Tanh).then_inc(s["tanhs"], 1)
                act.wait_ge(s["u_sq"], 1)
                nc.scalar.activation(den, den, ACT.Sqrt).then_inc(s["root"], 1)
                nc.scalar.activation(gel, k.cols[:, T_GATE:T_GATE + 2, LEAD:LEAD + SEQ], ACT.Gelu_apprx_tanh).then_inc(s["gelu_done"], 1)

            @block.vector
            def _(dve):
                step = in_order(dve, s["dve_done"])
                step(nc.vector.memset(x_pad[:, :, :, :], 0.0))
                for i in range(2):
                    conv(nc, k, step, xr[:, i, :], T_XR + i, VEC["lru_cw"] + 4 * i, VEC["lru_cb"] + i)
                    step(nc.vector.tensor_copy(x_pad[0:64, i, 0, :], xr[0:64, i, :]))
                    step(nc.vector.tensor_copy(x_pad[64:128, i, 1, :], xr[64:128, i, :]))
                    dve.sem_inc(s["x_ready"], 1)
                raw = k.vec[:, VEC["lru_lam"]:VEC["lru_lam"] + 2]
                nc.vector.scalar_tensor_tensor(out=l4[:, :], in0=raw, scalar=-1.0, in1=raw, op0=ALU.mult, op1=ALU.max).then_inc(s["lam_abs"], 1)
                dve.wait_ge(s["lam_exp"], 1)
                log1p(nc, step, l1[:, :], l2[:, :], l3[:, :], l4[:, :])
                step(nc.vector.tensor_scalar(l2[:, :], raw, -1.0, 0.0, ALU.mult, ALU.max))
                step(nc.vector.tensor_tensor(l1[:, :], l1[:, :], l2[:, :], ALU.add))
                step(nc.vector.tensor_scalar(lam[:, :], l1[:, :], -8.0, None, ALU.mult))
                dve.wait_ge(s["sigmoids"], 4)
                for i in range(2):
                    nc.vector.tensor_scalar(rate[:, i, :], rate[:, i, :], lam[:, i:i + 1], None, ALU.mult).then_inc(s["rate_ready"], 1)
                step(nc.vector.tensor_tensor(gate_i, gate_i, xr, ALU.mult))
                dve.wait_ge(s["tanhs"], 1)
                step(nc.vector.tensor_scalar(den, th, -1.0, 1.0, ALU.mult, ALU.add))
                step(nc.vector.reciprocal(den, den))
                step(nc.vector.scalar_tensor_tensor(out=den, in0=th, scalar=-2.0, in1=den, op0=ALU.mult, op1=ALU.mult))
                nc.vector.tensor_scalar(den, den, 1e-34, None, ALU.max).then_inc(s["u_sq"], 1)
                dve.wait_ge(s["root"], 1)
                step(nc.vector.tensor_tensor(gate_i, gate_i, den, ALU.mult))
                dve.wait_ge(s["a_ready"], 1)
                for i in range(2):
                    step(nc.vector.tensor_tensor_scan(out=scan[:, i, :], data0=a[:, i, :], data1=gate_i[:, i, :],
                                                      initial=0.0, op0=ALU.mult, op1=ALU.add))
                dve.wait_ge(s["gelu_done"], 1)
                step(nc.vector.tensor_tensor(k.mixed[:, 2:4, :], scan, gel, ALU.mult))

            @block.tensor
            def _(pe):
                for i in range(2):
                    pe.wait_ge(s["x_ready"], i + 1)
                    for n in range(2):
                        for half in range(2):
                            last = nc.tensor.matmul(k.bank[2 * i + n][64 * half:64 * half + 64, :],
                                                    k.lru_w[:, n, i, :], x_pad[:, i, half, :], start=True, stop=True)
                    last.then_inc(s["gates_sum"], 1)


DECAY = math.exp(-0.5)
CH = 32
NCH = SEQ // CH


def rwkv_prepare(nc, k, r):
    pair = lambda ap: ap.rearrange("p i t -> p (i t)")
    mix = r.mix
    slot = lambda i: k.cols[:, i:i + 2, LEAD:LEAD + SEQ]
    vec = lambda name, i: k.vec[:, VEC[name] + i:VEC[name] + i + 1]
    shifted = k.cols[:, T_R:T_R + 8, LEAD - 1:LEAD - 1 + SEQ]
    now = k.cols[:, T_R:T_R + 8, LEAD:LEAD + SEQ]
    diff = k.cols[:, 0:8, LEAD:LEAD + SEQ]
    sig_w, a, bonus, g = k.xT[:, 6:8, :], k.xT[:, 2:4, :], k.xT[:, 0:2, :], k.xT[:, 4:6, :]
    total, inv, prev, tmp, kk = slot(0), slot(2), slot(4), slot(6), slot(8)
    pdec = slot(10)
    with stage(nc, "dve_done", "mixed_in", "padded", "lora_in", "lora_out", "gates", "kk_ready", "kk_sq", "kk_sum",
               "kk_var", "kk_dev", "scanned", "exps", "rk_ready", "rk_sum") as (block, s):
        @block.scalar
        def _(act):
            act.wait_ge(s["padded"], 1)
            nc.scalar.activation(r.lpad[0:64, 0, :], mix[0:64, 6, :], ACT.Tanh).then_inc(s["lora_in"], 1)
            nc.scalar.activation(mix[:, 7, :], mix[:, 7, :], ACT.Sigmoid).then_inc(s["lora_in"], 1)
            for i in range(2):
                act.wait_ge(s["lora_out"], 3 * i + 1)
                nc.scalar.activation(sig_w[:, i, :], k.bank[i][:, :], ACT.Sigmoid, bias=vec("w0", i)).then_inc(s["gates"], 1)
                act.wait_ge(s["lora_out"], 3 * i + 2)
                nc.scalar.activation(a[:, i, :], k.bank[2 + i][:, :], ACT.Sigmoid, bias=vec("a0", i)).then_inc(s["gates"], 1)
                act.wait_ge(s["lora_out"], 3 * i + 3)
                nc.scalar.copy(g[:, i, :], k.bank[4 + i][:, :]).then_inc(s["gates"], 1)
            act.wait_ge(s["kk_ready"], 1)
            nc.scalar.activation(tmp, kk, ACT.Square).then_inc(s["kk_sq"], 1)
            act.wait_ge(s["scanned"], 1)
            nc.scalar.activation(pdec, total, ACT.Exp, scale=-DECAY).then_inc(s["exps"], 1)
            nc.scalar.activation(inv, total, ACT.Exp, scale=DECAY).then_inc(s["exps"], 1)
            nc.scalar.activation(prev, prev, ACT.Exp, scale=-DECAY).then_inc(s["exps"], 1)
            act.wait_ge(s["kk_var"], 2)
            nc.scalar.activation(tmp, tmp, ACT.Sqrt).then_inc(s["kk_dev"], 1)

        @block.vector
        def _(dve):
            step = in_order(dve, s["dve_done"])
            step(nc.vector.tensor_tensor(diff, shifted, now, ALU.subtract))
            for i in (6, 7, 2, 3, 0, 1, 4, 5):
                step(nc.vector.scalar_tensor_tensor(out=mix[:, i, :], in0=diff[:, i, :], scalar=vec("mu", i),
                                                    in1=now[:, i, :], op0=ALU.mult, op1=ALU.add))
                if i == 7:
                    step(nc.vector.memset(r.lpad[:, :, :], 0.0))
                    nc.vector.tensor_copy(r.lpad[64:128, 1, :], mix[64:128, 6, :]).then_inc(s["padded"], 1)
                    dve.wait_ge(s["padded"], 1)
            for i in range(2):
                step(nc.vector.tensor_scalar(kk[:, i, :], mix[:, 2 + i, :], vec("kk", i), None, ALU.mult))
            dve.sem_inc(s["kk_ready"], 1)
            dve.wait_ge(s["gates"], 6)
            for i in range(2):
                step(nc.vector.tensor_tensor_scan(out=total[:, i, :], data0=k.reset[:, :], data1=sig_w[:, i, :],
                                                  initial=0.0, op0=ALU.mult, op1=ALU.add))
            nc.vector.tensor_tensor(prev, total, sig_w, ALU.subtract).then_inc(s["scanned"], 1)
            step(nc.vector.tensor_scalar(k.stat[:, 16:18], k.vec[:, VEC["ka"]:VEC["ka"] + 2], -1.0, 1.0, ALU.mult, ALU.add))
            for i in range(2):
                step(nc.vector.tensor_scalar(bonus[:, i, :], a[:, i, :], vec("ka", i), k.stat[:, 16 + i:17 + i], ALU.mult, ALU.add))
            step(nc.vector.tensor_tensor(mix[:, 2:4, :], mix[:, 2:4, :], bonus, ALU.mult))
            for i in range(2):
                dve.wait_ge(s["kk_sum"], i + 1)
                nc.vector.tensor_scalar(tmp[:, i, :], k.bank[6 + i][:, :], 1e-30, None, ALU.max).then_inc(s["kk_var"], 1)
            dve.wait_ge(s["kk_dev"], 1)
            step(nc.vector.tensor_scalar(tmp, tmp, 1e-12, None, ALU.max))
            step(nc.vector.reciprocal(tmp, tmp))
            step(nc.vector.tensor_tensor(kk, kk, tmp, ALU.mult))
            for i in range(2):
                nc.vector.scalar_tensor_tensor(out=tmp[:, i, :], in0=mix[:, i, :], scalar=vec("rk", i),
                                               in1=mix[:, 2 + i, :], op0=ALU.mult, op1=ALU.mult).then_inc(s["rk_ready"], 1)
            dve.wait_ge(s["exps"], 3)
            step(nc.vector.tensor_tensor(a, a, kk, ALU.mult))
            step(nc.vector.tensor_tensor(r.beta, a, inv, ALU.mult))
            step(nc.vector.tensor_tensor(r.alpha, kk, prev, ALU.mult))
            step(nc.vector.tensor_tensor(r.kappa, mix[:, 2:4, :], inv, ALU.mult))
            dve.wait_ge(s["rk_ready"], 2)
            step(nc.vector.tensor_tensor(r.rho, mix[:, 0:2, :], pdec, ALU.mult))
            step(nc.vector.tensor_copy(r.p_end[:, :, :], pdec.rearrange("p i (c w) -> p i c w", w=CH)[:, :, :, CH - 1]))
            step(nc.vector.memset(r.a_pad[:, :, :, :].rearrange("p i n t -> p (i n t)"), 0.0))
            step(nc.vector.memset(r.b_pad[:, :, :, :].rearrange("p i n t -> p (i n t)"), 0.0))
            for i in range(2):
                for e in range(2):
                    q = slice(64 * e, 64 * e + 64)
                    step(nc.vector.tensor_copy(r.b_pad[q, i, e, :], r.beta[q, i, :]))
                    step(nc.vector.tensor_copy(r.a_pad[q, i, e, :], r.alpha[q, i, :]))
                    step(nc.vector.tensor_copy(r.a_pad[q, i, 2 + e, :], r.rho[q, i, :]))
            for i in range(2):
                dve.wait_ge(s["rk_sum"], i + 1)
                step(nc.vector.tensor_tensor(bonus[:, i, :], k.bank[i][:, :], mix[:, 4 + i, :], ALU.mult))

        @block.tensor
        def _(pe):
            pe.wait_ge(s["lora_in"], 2)
            for i in range(2):
                for n, rhs in ((0, r.lpad[:, 0, :]), (1, r.lpad[:, 1, :]), (2, mix[:, 7, :])):
                    w = k.lora[:, (n // 2) * 256 + i * P:(n // 2) * 256 + (i + 1) * P]
                    nc.tensor.matmul(k.bank[2 * n + i][:, :], w, rhs, start=True, stop=True).then_inc(s["lora_out"], 1)
            pe.wait_ge(s["kk_sq"], 1)
            for i in range(2):
                nc.tensor.matmul(k.bank[6 + i][:, :], k.same[64][:, :], tmp[:, i, :], start=True, stop=True).then_inc(s["kk_sum"], 1)
            pe.wait_ge(s["rk_ready"], 2)
            for i in range(2):
                nc.tensor.matmul(k.bank[i][:, :], k.same[64][:, :], tmp[:, i, :], start=True, stop=True).then_inc(s["rk_sum"], 1)


def rwkv_chunks(nc, k, r):
    m = [r.m[:, i, :, :] for i in range(11)]
    N, NT, A16, A32, B, C, D, N2, N2T, INT, IN2 = m
    IN4, XT, T, Q, W, T2, Q2, Q3 = m[8], m[0], m[7], m[1], m[9], m[10], m[8], m[7]
    four = lambda b: k.bank[b][:, :].rearrange("p (h t) -> p h t", h=4)
    two = lambda b, at: k.bank[b][:, at:at + 256].rearrange("p (h t) -> p h t", h=2)
    bc = lambda mask, n: mask.unsqueeze(1).to_broadcast([P, n, P])
    ident4 = bc(k.ident[:, :], 4)
    PE_STEPS = ("turn", "gram", "n2", "bv", "n4", "tq", "w", "tq2", "w2", "q3", "ut", "local")
    DVE_STEPS = ("n", "masks", "n2", "in4", "t", "tq2", "q3", "rgh")
    ACT_STEPS = ("turn", "n2t", "bv", "xt", "q", "w", "w2", "u", "y")
    POOL_STEPS = ("beta_v", "u")

    def after(engine, sem, steps, name, t):
        engine.wait_ge(sem, t * len(steps) + steps.index(name) + 1)

    with stage(nc, "masked", "product", "dve_kept", "act_kept", "pool_kept", "dve_done", "act_done") as (block, s):
        pe_did = lambda e, name, t: after(e, s["product"], PE_STEPS, name, t)
        dve_did = lambda e, name, t: after(e, s["dve_kept"], DVE_STEPS, name, t)
        act_did = lambda e, name, t: after(e, s["act_kept"], ACT_STEPS, name, t)
        pool_did = lambda e, name, t: after(e, s["pool_kept"], POOL_STEPS, name, t)

        @block.tensor
        def _(pe):
            mm = nc.tensor.matmul
            for t in range(TT):
                c = slice(t * P, (t + 1) * P)
                if t:
                    act_did(pe, "turn", t - 1)
                for n, src in enumerate((r.alpha, r.beta, r.kappa, r.mix[:, 4:6, :])):
                    for i in range(2):
                        last = nc.tensor.transpose(k.bank[6 + n // 2][:, (n % 2 * 2 + i) * P:(n % 2 * 2 + i + 1) * P],
                                                   src[:, i, c], k.ident[:, :])
                last.then_inc(s["product"], 1)
                if t:
                    dve_did(pe, "rgh", t - 1)
                    act_did(pe, "y", t - 1)
                for i in range(2):
                    mm(k.bank[0][:, i * 256:(i + 1) * 256], r.alpha[:, i, c], r.b_pad[:, i, :, c], start=True, stop=True)
                    mm(k.bank[1 + i][:, :], r.beta[:, i, c], r.a_pad[:, i, :, c], start=True, stop=True)
                    last = mm(k.bank[3 + i][:, :], r.kappa[:, i, c], r.a_pad[:, i, :, c], start=True, stop=True)
                last.then_inc(s["product"], 1)
                dve_did(pe, "n", t)
                for h in range(4):
                    o = slice(h * P, (h + 1) * P)
                    mm(k.bank[0][:, o], NT[:, h, :], N[:, h, :], start=True, stop=True)
                    last = mm(k.bank[5][:, o], N[:, h, :], NT[:, h, :], start=True, stop=True)
                last.then_inc(s["product"], 1)
                dve_did(pe, "masks", t)
                act_did(pe, "turn", t)
                for h in range(4):
                    last = mm(k.bank[3][:, h * 64:(h + 1) * 64], B[:, h, :], r.vT[:, h, :], start=True, stop=True)
                last.then_inc(s["product"], 1)
                dve_did(pe, "n2", t)
                act_did(pe, "n2t", t)
                for h in range(4):
                    o = slice(h * P, (h + 1) * P)
                    mm(k.bank[1][:, o], N2T[:, h, :], N2[:, h, :], start=True, stop=True)
                    last = mm(k.bank[2][:, o], IN2[:, h, :], INT[:, h, :], start=True, stop=True)
                last.then_inc(s["product"], 1)
                dve_did(pe, "in4", t)
                act_did(pe, "xt", t)
                for h in range(4):
                    o = slice(h * P, (h + 1) * P)
                    mm(k.bank[0][:, o], XT[:, h, :], IN4[:, h, :], start=True, stop=True)
                    last = mm(k.bank[5][:, o], IN4[:, h, :], XT[:, h, :], start=True, stop=True)
                last.then_inc(s["product"], 1)
                dve_did(pe, "t", t)
                for h in range(4):
                    last = mm(k.bank[1][:, h * P:(h + 1) * P], A16[:, h, :], T[:, h, :], start=True, stop=True)
                last.then_inc(s["product"], 1)
                act_did(pe, "w", t)
                for h in range(4):
                    o = slice(h * P, (h + 1) * P)
                    mm(k.bank[0][:, o], Q[:, h, :], W[:, h, :], start=True, stop=True)
                    last = mm(k.bank[5][:, o], W[:, h, :], Q[:, h, :], start=True, stop=True)
                last.then_inc(s["product"], 1)
                dve_did(pe, "tq2", t)
                for h in range(4):
                    last = mm(k.bank[2][:, h * P:(h + 1) * P], A32[:, h, :], T2[:, h, :], start=True, stop=True)
                last.then_inc(s["product"], 1)
                act_did(pe, "w2", t)
                for h in range(4):
                    last = mm(k.bank[5][:, h * P:(h + 1) * P], W[:, h, :], Q2[:, h, :], start=True, stop=True)
                last.then_inc(s["product"], 1)
                dve_did(pe, "q3", t)
                act_did(pe, "bv", t)
                for h in range(4):
                    last = mm(k.bank[0][:, h * P:(h + 1) * P], Q3[:, h, :], r.bva[:, h, :], start=True, stop=True)
                last.then_inc(s["product"], 1)
                pool_did(pe, "u", t)
                act_did(pe, "u", t)
                for h in range(4):
                    i, q = h // 2, slice(64 * (h % 2), 64 * (h % 2) + 64)
                    mm(k.bank[1][q, i * P:(i + 1) * P], r.taT[:, h, :], D[:, h, :], start=True, stop=True)
                    mm(k.bank[2][q, i * 256:(i + 1) * 256], r.taT[:, h, :], r.beta_c[:, h, :, :].rearrange("p c d -> p (c d)"), start=True, stop=True)
                    mm(k.bank[3][q, i * 256:(i + 1) * 256], r.kapT[:, h, :], r.v_c[:, h, :, :].rearrange("p c d -> p (c d)"), start=True, stop=False)
                    mm(k.bank[3][q, i * 256:(i + 1) * 256], r.betT[:, h, :], r.u_c[:, h, :, :].rearrange("p c d -> p (c d)"), start=False, stop=True)
                    mm(k.bank[4][q, i * P:(i + 1) * P], r.vT[:, h, :], C[:, h, :], start=True, stop=False)
                    last = mm(k.bank[4][q, i * P:(i + 1) * P], r.uT[:, h, :], D[:, h, :], start=False, stop=True)
                last.then_inc(s["product"], 1)

        @block.vector
        def _(dve):
            step = in_order(dve, s["dve_done"])
            mk = r.masks
            step(nc.vector.scalar_tensor_tensor(out=mk[:, 0, :], in0=k.lower[:, :], scalar=-1.0, in1=k.same[8][:, :], op0=ALU.mult, op1=ALU.mult))
            step(nc.vector.scalar_tensor_tensor(out=mk[:, 1, :], in0=k.strict[:, :], scalar=-1.0, in1=k.same[8][:, :], op0=ALU.mult, op1=ALU.mult))
            step(nc.vector.tensor_tensor(mk[:, 2, :], k.same[16][:, :], k.same[8][:, :], ALU.subtract))
            step(nc.vector.tensor_tensor(mk[:, 2, :], mk[:, 2, :], k.strict[:, :], ALU.mult))
            step(nc.vector.tensor_tensor(mk[:, 3, :], k.same[32][:, :], k.same[16][:, :], ALU.subtract))
            step(nc.vector.tensor_tensor(mk[:, 3, :], mk[:, 3, :], k.strict[:, :], ALU.mult))
            step(nc.vector.tensor_tensor(mk[:, 4, :], k.strict[:, :], k.same[32][:, :], ALU.mult))
            step(nc.vector.tensor_tensor(mk[:, 5, :], k.upper[:, :], k.same[32][:, :], ALU.mult))
            step(nc.vector.memset(k.cols[:, 0:16, LEAD:LEAD + SEQ], 0.0))
            tt = nc.vector.tensor_tensor
            for t in range(TT):
                c = slice(t * P, (t + 1) * P)
                pe_did(dve, "gram", t)
                step(tt(N, four(0), bc(mk[:, 0, :], 4), ALU.mult))
                for i in range(2):
                    last = tt(NT[:, 2 * i:2 * i + 2, :], two(1 + i, 0), bc(mk[:, 1, :], 2), ALU.mult)
                last.then_inc(s["dve_kept"], 1)
                for i in range(2):
                    hh = slice(2 * i, 2 * i + 2)
                    step(tt(A16[:, hh, :], two(1 + i, 0), bc(mk[:, 2, :], 2), ALU.mult))
                    step(tt(A32[:, hh, :], two(1 + i, 0), bc(mk[:, 3, :], 2), ALU.mult))
                    step(tt(D[:, hh, :], two(1 + i, 256), bc(mk[:, 5, :], 2), ALU.mult))
                    step(tt(B[:, hh, :], two(3 + i, 0), bc(mk[:, 4, :], 2), ALU.mult))
                    step(tt(C[:, hh, :], two(3 + i, 256), bc(mk[:, 5, :], 2), ALU.mult))
                dve_did(dve, "n", t)
                tt(INT, NT, ident4, ALU.add).then_inc(s["dve_kept"], 1)
                pe_did(dve, "n2", t)
                step(nc.vector.tensor_copy(N2, four(0)))
                tt(IN2, four(0), ident4, ALU.add).then_inc(s["dve_kept"], 1)
                pe_did(dve, "n4", t)
                tt(IN4, four(1), ident4, ALU.add).then_inc(s["dve_kept"], 1)
                pe_did(dve, "tq", t)
                nc.vector.tensor_copy(T, four(0)).then_inc(s["dve_kept"], 1)
                act_did(dve, "q", t)
                pe_did(dve, "tq2", t)
                step(tt(T2, T, four(0), ALU.subtract))
                tt(Q2, Q, four(5), ALU.subtract).then_inc(s["dve_kept"], 1)
                pe_did(dve, "q3", t)
                dve_did(dve, "tq2", t)
                tt(Q3, Q2, four(5), ALU.subtract).then_inc(s["dve_kept"], 1)
                pe_did(dve, "local", t)
                for i in range(2):
                    step(tt(r.rho[:, i, c], r.rho[:, i, c], k.bank[1][:, i * P:(i + 1) * P], ALU.subtract))
                for i in range(2):
                    hp = k.bank[3][:, i * 256:(i + 1) * 256].rearrange("p (c v) -> p c v", c=4)
                    gp = k.bank[2][:, i * 256:(i + 1) * 256].rearrange("p (c v) -> p c v", c=4)
                    G = r.G(i, t)
                    H = r.H(i, t)
                    for e in range(2):
                        q = slice(64 * e, 64 * e + 64)
                        step(tt(G[q, :, q], k.ident[q, q].unsqueeze(1).to_broadcast([64, 4, 64]), gp[q, :, :], ALU.subtract))
                        last = tt(H[q, :, q], hp[q, :, :], r.p_end[q, i, 4 * t:4 * t + 4].unsqueeze(2).to_broadcast([64, 4, 64]), ALU.mult)
                        if i == 0 or e == 0:
                            step(last)
                last.then_inc(s["dve_kept"], 1)

        @block.scalar
        def _(act):
            step = in_order(act, s["act_done"])
            cp = nc.scalar.copy
            for t in range(TT):
                c = slice(t * P, (t + 1) * P)
                heads = lambda b, at: k.bank[b][:, at:at + 256].rearrange("p (h d) -> p h d", h=4)
                pe_did(act, "turn", t)
                if t:
                    pe_did(act, "local", t - 1)
                step(cp(r.bva[:, :, 64:128], heads(6, 0)))
                step(cp(r.betT[:, :, :], heads(6, 256)))
                step(cp(r.kapT[:, :, :], heads(7, 0)))
                cp(r.vT[:, :, :], heads(7, 256)).then_inc(s["act_kept"], 1)
                pe_did(act, "n2", t)
                cp(N2T, four(5)).then_inc(s["act_kept"], 1)
                pe_did(act, "bv", t)
                cp(r.bva[:, :, 0:64], heads(3, 0)).then_inc(s["act_kept"], 1)
                pe_did(act, "n4", t)
                cp(XT, four(2)).then_inc(s["act_kept"], 1)
                pe_did(act, "tq", t)
                cp(Q, four(5)).then_inc(s["act_kept"], 1)
                pe_did(act, "w", t)
                cp(W, four(1)).then_inc(s["act_kept"], 1)
                pe_did(act, "w2", t)
                cp(W, four(2)).then_inc(s["act_kept"], 1)
                pe_did(act, "ut", t)
                step(nc.scalar.activation(r.uT[:, :, :], four(0)[:, :, 0:64], ACT.Copy, scale=-1.0))
                cp(r.taT[:, :, :], four(0)[:, :, 64:128]).then_inc(s["act_kept"], 1)
                pe_did(act, "local", t)
                cp(k.mixed[:, 4:6, c], k.bank[4][:, 0:256].rearrange("p (i t) -> p i t", i=2)).then_inc(s["act_kept"], 1)

        @block.gpsimd
        def _(pool):
            rows = k.same[32][:, :].rearrange("p (c w) -> p c w", w=CH)[:, :, 0]

            def spread(dst, src):
                for h in range(4):
                    last = nc.gpsimd.tensor_tensor(dst[:, h, :, :], src[:, h, :].unsqueeze(1).to_broadcast([P, 4, 64]),
                                                   rows.unsqueeze(2).to_broadcast([P, 4, 64]), ALU.mult)
                return last
            for t in range(TT):
                act_did(pool, "turn", t)
                spread(r.beta_c, r.betT)
                spread(r.v_c, r.vT).then_inc(s["pool_kept"], 1)
                act_did(pool, "u", t)
                spread(r.u_c, r.uT).then_inc(s["pool_kept"], 1)


def rwkv_carry(nc, k, r):
    y = k.mixed[:, 4:6, :]
    bonus, g = k.xT[:, 0:2, :], k.xT[:, 4:6, :]
    dev, sq = k.wide[:, 2, :].rearrange("p (i t) -> p i t", t=SEQ), k.wide[:, 3, :].rearrange("p (i t) -> p i t", t=SEQ)
    M = k.ring[:, :, :].rearrange("p u c -> p (u c)").rearrange("p (i c v) -> p i c v", i=2, v=P)
    with stage(nc, "dve_done", "carried", "stepped", "y_done", "y_ready", "mean_sum", "dev_ready", "squares", "var_sum",
               "var_ready", "root") as (block, s):
        @block.vector
        def _(dve):
            step = in_order(dve, s["dve_done"])
            for c in range(NCH - 1):
                for i in range(2):
                    H = r.H(i, c // 4)[:, c % 4, :]
                    if c == 0:
                        nc.vector.tensor_copy(M[:, i, 1, :], H).then_inc(s["carried"], 1)
                        continue
                    dve.wait_ge(s["stepped"], 2 * (c - 1) + i + 1)
                    nc.vector.scalar_tensor_tensor(out=M[:, i, c + 1, :], in0=k.bank[2 * i + c % 2][:, 0:P],
                                                   scalar=r.p_end[:, i, c:c + 1], in1=H,
                                                   op0=ALU.mult, op1=ALU.add).then_inc(s["carried"], 1)
            dve.wait_ge(s["y_done"], 1)
            for i in range(2):
                nc.vector.tensor_tensor(y[:, i, CH:SEQ], y[:, i, CH:SEQ], k.bank[4 + i][:, CH:SEQ], ALU.add).then_inc(s["y_ready"], 1)
            for i in range(2):
                dve.wait_ge(s["mean_sum"], i + 1)
                nc.vector.scalar_tensor_tensor(out=dev[:, i, :], in0=k.bank[6 + i][:, :], scalar=-1.0 / 64, in1=y[:, i, :],
                                               op0=ALU.mult, op1=ALU.add).then_inc(s["dev_ready"], 1)
            for i in range(2):
                dve.wait_ge(s["var_sum"], i + 1)
                nc.vector.tensor_scalar(sq[:, i, :], k.bank[i][:, :], 1.0 / 64, GN_EPS, ALU.mult, ALU.add).then_inc(s["var_ready"], 1)
            dve.wait_ge(s["root"], 1)
            step(nc.vector.reciprocal(sq, sq))
            step(nc.vector.tensor_tensor(dev, dev, sq, ALU.mult))
            for i in range(2):
                step(nc.vector.tensor_scalar(dev[:, i, :], dev[:, i, :], k.vec[:, VEC["ln_w"] + i:VEC["ln_w"] + i + 1],
                                             k.vec[:, VEC["ln_b"] + i:VEC["ln_b"] + i + 1], ALU.mult, ALU.add))
            step(nc.vector.tensor_tensor(dev, dev, bonus, ALU.add))
            step(nc.vector.tensor_tensor(y, dev, g, ALU.mult))

        @block.tensor
        def _(pe):
            for c in range(1, NCH):
                for i in range(2):
                    pe.wait_ge(s["carried"], 2 * (c - 1) + i + 1)
                    if c < NCH - 1:
                        nc.tensor.matmul(k.bank[2 * i + c % 2][:, 0:P], r.G(i, c // 4)[:, c % 4, :], M[:, i, c, :],
                                         start=True, stop=True).then_inc(s["stepped"], 1)
                    last = nc.tensor.matmul(k.bank[4 + i][:, c * CH:(c + 1) * CH], M[:, i, c, :],
                                            r.rho[:, i, c * CH:(c + 1) * CH], start=True, stop=True)
            last.then_inc(s["y_done"], 1)
            for i in range(2):
                pe.wait_ge(s["y_ready"], i + 1)
                nc.tensor.matmul(k.bank[6 + i][:, :], k.same[64][:, :], y[:, i, :], start=True, stop=True).then_inc(s["mean_sum"], 1)
            for i in range(2):
                pe.wait_ge(s["squares"], i + 1)
                nc.tensor.matmul(k.bank[i][:, :], k.same[64][:, :], sq[:, i, :], start=True, stop=True).then_inc(s["var_sum"], 1)

        @block.scalar
        def _(act):
            for i in range(2):
                act.wait_ge(s["dev_ready"], i + 1)
                nc.scalar.activation(sq[:, i, :], dev[:, i, :], ACT.Square).then_inc(s["squares"], 1)
            act.wait_ge(s["var_ready"], 2)
            nc.scalar.activation(sq, sq, ACT.Sqrt).then_inc(s["root"], 1)


def rwkv_mixer(nc, k):
    with ExitStack() as held:
        def sb(name, shape):
            return held.enter_context(nc.sbuf_tensor(name, shape, F32))
        r = Named()
        r.mix = k.wide[:, :, :].rearrange("p a c -> p (a c)").rearrange("p (i t) -> p i t", t=SEQ)
        r.rho, r.kappa, r.beta, r.alpha = r.mix[:, 0:2, :], r.mix[:, 2:4, :], k.xT[:, 2:4, :], k.xT[:, 6:8, :]
        r.G = lambda i, t: k.cols[:, 4 * i + t, LEAD:LEAD + SEQ].rearrange("p (c v) -> p c v", v=P)
        r.H = lambda i, t: k.cols[:, 8 + 4 * i + t, LEAD:LEAD + SEQ].rearrange("p (c v) -> p c v", v=P)
        r.a_pad = sb("rw_a_pad", [P, 2, 4, SEQ])
        r.b_pad = sb("rw_b_pad", [P, 2, 2, SEQ])
        r.p_end = sb("rw_p_end", [P, 2, NCH])
        r.masks = sb("rw_masks", [P, 6, P])
        with ExitStack() as first:
            r.lpad = first.enter_context(nc.sbuf_tensor("rw_lpad", [P, 2, SEQ], F32))
            rwkv_prepare(nc, k, r)
        r.m = sb("rw_m", [P, 11, 4, P])
        r.bva = sb("rw_bva", [P, 4, P])
        r.betT = sb("rw_betT", [P, 4, 64])
        r.kapT = sb("rw_kapT", [P, 4, 64])
        r.vT = sb("rw_vT", [P, 4, 64])
        r.uT = sb("rw_uT", [P, 4, 64])
        r.taT = sb("rw_taT", [P, 4, 64])
        r.beta_c = sb("rw_beta_c", [P, 4, 4, 64])
        r.v_c = sb("rw_v_c", [P, 4, 4, 64])
        r.u_c = sb("rw_u_c", [P, 4, 4, 64])
        rwkv_chunks(nc, k, r)
        rwkv_carry(nc, k, r)


def attention(nc, k, a):
    units = [(qt, h, br) for qt in range(TT) for h in range(4) for br in range(2)]
    n = len(units)
    width = lambda u: (units[u][0] + 1) * P
    S, X, PT = 3, 3, 2
    with stage(nc, "dve_done", "pool_done", "bias_ready", "moved", "keys_ready", "values_turned", "values_ready",
               "gate_ready", "scores", "read", "biased", "exps", "inverse", "scaled", "turned", "kept", "summed", "w1_in") as (block, s):
        @block.sync
        def _(sp):
            sp.dma_start(a.keys[64:P, 0, 1, :], k.cols[0:64, T_KSKW, LEAD:LEAD + SEQ]).then_inc(s["moved"], 16)
            sp.dma_start(a.keys[0:64, 1, 0, :], k.cols[64:P, T_KSKW, LEAD:LEAD + SEQ]).then_inc(s["moved"], 16)
            sp.dma_start(a.w1[:, :], a.w1_dram).then_inc(s["w1_in"], 16)
            sp.dma_start(a.w2[:, :], a.w2_dram).then_inc(s["w1_in"], 16)
            sp.wait_ge(s["w1_in"], 32)
            sp.wait_ge(s["moved"], 32)

        @block.gpsimd
        def _(pool):
            step = in_order(pool, s["pool_done"])
            step(nc.gpsimd.iota(a.dist[:, :], pattern=[[-1, SEQ]], base=384, channel_multiplier=1,
                                allow_small_or_imprecise_dtypes=True))
            for h in range(4):
                step(nc.gpsimd.tensor_scalar(a.alibi[:, h, :], a.dist[:, :], -(2.0 ** (-2.0 * (h + 1))), 0.0, ALU.mult, ALU.add))
                nc.gpsimd.affine_select(out=a.alibi[:, h, :], in_=a.alibi[:, h, :], compare_op=ALU.is_ge, fill=NEG, base=384,
                                        pattern=[[-1, SEQ]], channel_multiplier=1).then_inc(s["bias_ready"], 1)
            pool.wait_ge(s["gate_ready"], 1)
            for u, (qt, h, br) in enumerate(units):
                pool.wait_ge(s["inverse"], u + 1)
                w = a.weights[:, u % X, 0:width(u)]
                nc.gpsimd.tensor_scalar(w, w, a.inv[:, u:u + 1], a.gate[:, qt, 3 * h + 1 + br:3 * h + 2 + br],
                                        ALU.mult, ALU.mult).then_inc(s["scaled"], 1)

        @block.vector
        def _(dve):
            step = in_order(dve, s["dve_done"])
            step(nc.vector.tensor_copy(a.keys[0:64, 0, 0, :], k.cols[0:64, T_KSKW, LEAD:LEAD + SEQ]))
            step(nc.vector.tensor_copy(a.keys[64:P, 1, 1, :], k.cols[64:P, T_KSKW, LEAD:LEAD + SEQ]))
            step(nc.vector.memset(a.keys[64:P, 0, 0, :], 0.0))
            step(nc.vector.memset(a.keys[64:P, 1, 0, :], 0.0))
            step(nc.vector.memset(a.keys[0:64, 0, 1, :], 0.0))
            nc.vector.memset(a.keys[0:64, 1, 1, :], 0.0).then_inc(s["keys_ready"], 1)
            dve.wait_ge(s["values_turned"], 1)
            nc.vector.tensor_copy(a.vT[:, :, :], k.bank[7][:, :].rearrange("p (t c) -> p t c", t=TT)).then_inc(s["values_ready"], 1)
            for u, (qt, h, br) in enumerate(units):
                w = a.weights[:, u % X, 0:width(u)]
                dve.wait_ge(s["scores"], u + 1)
                dve.wait_ge(s["bias_ready"], h + 1)
                if u >= X:
                    dve.wait_ge(s["turned"], u - X + 1)
                nc.vector.scalar_tensor_tensor(out=w, in0=k.bank[u % S][:, 0:width(u)], scalar=0.125,
                                               in1=a.alibi[:, h, (TT - 1 - qt) * P:(TT - 1 - qt) * P + width(u)],
                                               op0=ALU.mult, op1=ALU.add).then_inc(s["read"], 1)
                dve.wait_ge(s["read"], u + 1)
                nc.vector.tensor_reduce(out=a.neg_max[:, u:u + 1], in_=w, axis=AX.X, op=ALU.max, negate=True).then_inc(s["biased"], 1)
                if u >= 1:
                    dve.wait_ge(s["exps"], u)
                    nc.vector.reciprocal(a.inv[:, u - 1:u], a.total[:, u - 1:u]).then_inc(s["inverse"], 1)
            dve.wait_ge(s["exps"], n)
            nc.vector.reciprocal(a.inv[:, n - 1:n], a.total[:, n - 1:n]).then_inc(s["inverse"], 1)
            dve.wait_ge(s["summed"], n)
            for i in range(2):
                step(nc.vector.tensor_copy(k.mixed[:, 6 + i, :], k.bank[5 + i][:, :]))

        @block.scalar
        def _(act):
            nc.scalar.activation(a.gate[:, :, :], k.smallT[:, :, 4:16], ACT.Sigmoid).then_inc(s["gate_ready"], 1)
            for i in range(n + 2):
                if i < n:
                    act.wait_ge(s["biased"], i + 1)
                    w = a.weights[:, i % X, 0:width(i)]
                    nc.scalar.activation(w, w, ACT.Exp, bias=a.neg_max[:, i:i + 1],
                                         accum_out=a.total[:, i:i + 1]).then_inc(s["exps"], 1)
                u = i - 2
                if u >= 0:
                    act.wait_ge(s["turned"], u + 1)
                    if u >= PT:
                        act.wait_ge(s["summed"], u - PT + 1)
                    nc.scalar.copy(a.turned[:, u % PT, 0:width(u)], k.bank[3 + u % PT][:, 0:width(u)]).then_inc(s["kept"], 1)

        @block.tensor
        def _(pe):
            for t in range(TT):
                last = nc.tensor.transpose(k.bank[7][:, t * P:(t + 1) * P], k.cols[:, T_VSVW, LEAD + t * P:LEAD + (t + 1) * P], k.ident[:, :])
            last.then_inc(s["values_turned"], 1)
            pe.wait_ge(s["keys_ready"], 1)
            pe.wait_ge(s["moved"], 32)
            pe.wait_ge(s["values_ready"], 1)
            for i in range(n + 3):
                if i < n:
                    qt, h, br = units[i]
                    if i >= S:
                        pe.wait_ge(s["read"], i - S + 1)
                    nc.tensor.matmul(k.bank[i % S][:, 0:width(i)], k.cols[:, T_Q + h // 2, LEAD + qt * P:LEAD + (qt + 1) * P],
                                     a.keys[:, br, h % 2, 0:width(i)], start=True, stop=True).then_inc(s["scores"], 1)
                u = i - 2
                if 0 <= u < n:
                    pe.wait_ge(s["scaled"], u + 1)
                    if u >= PT:
                        pe.wait_ge(s["kept"], u - PT + 1)
                    for b in range(units[u][0] + 1):
                        last = nc.tensor.transpose(k.bank[3 + u % PT][:, b * P:(b + 1) * P],
                                                   a.weights[:, u % X, b * P:(b + 1) * P], k.ident[:, :])
                    last.then_inc(s["turned"], 1)
                u = i - 3
                if u >= 0:
                    qt, h, br = units[u]
                    pe.wait_ge(s["kept"], u + 1)
                    o = k.bank[5 + h // 2][64 * (h % 2):64 * (h % 2) + 64, qt * P:(qt + 1) * P]
                    for b in range(qt + 1):
                        last = nc.tensor.matmul(o, a.vT[:, b, br * 64:(br + 1) * 64], a.turned[:, u % PT, b * P:(b + 1) * P],
                                                start=(br == 0 and b == 0), stop=(br == 1 and b == qt))
                    last.then_inc(s["summed"], 1)


def compressed_attention(nc, k, a):
    H, NBLK = 4, 32
    with ExitStack() as held:
        def sb(name, shape):
            return held.enter_context(nc.sbuf_tensor(name, shape, F32))
        blocks = sb("cmp_blocks", [P, 2, 32, NBLK])
        hidden = sb("cmp_hidden", [P, 2, 2, NBLK])
        kpad = sb("cmp_kpad", [P, 2, NBLK])
        vz = sb("cmp_vz", [P, H, 64])
        dist = sb("cmp_dist", [P, TT, NBLK])
        valid = sb("cmp_valid", [P, TT, NBLK])
        hide = sb("cmp_hide", [P, TT, NBLK])
        w = sb("cmp_w", [P, TT, H, NBLK])
        mx = sb("cmp_mx", [P, TT * H])
        wT = sb("cmp_wT", [P, TT, P])
        flat = w[:, :, :, :].rearrange("p t h n -> p (t h) n")
        w1 = a.w1[:, :].rearrange("p (j c) -> p j c", j=32)
        w2 = a.w2[:, :].rearrange("p (v m c) -> p v m c", v=2, m=2)
        with stage(nc, "dve_done", "dist_ready", "blocks_ready", "hidden_sum", "hidden_ready", "kv_sum", "kv_ready",
                   "scores", "shifted", "exps", "weights_ready", "turned", "kept", "summed") as (block, s):
            @block.gpsimd
            def _(pool):
                nc.gpsimd.iota(dist[:, :, :], pattern=[[P, TT], [-16, NBLK]], base=-31, channel_multiplier=1,
                               allow_small_or_imprecise_dtypes=True).then_inc(s["dist_ready"], 1)

            @block.vector
            def _(dve):
                step = in_order(dve, s["dve_done"])
                step(nc.vector.memset(blocks[:, :, :, :].rearrange("p v j n -> p (v j n)"), 0.0))
                for v in range(2):
                    q = slice(64 * v, 64 * v + 64)
                    for half in range(2):
                        at = LEAD + 16 * half
                        src = k.cols[q, T_CMP, at:at + 31 * 16].rearrange("p (n j) -> p j n", j=16)
                        pos = k.vec[q, VEC["pos"] + 16 * half:VEC["pos"] + 16 * half + 16].unsqueeze(2).to_broadcast([64, 16, 31])
                        step(nc.vector.tensor_tensor(blocks[q, v, 16 * half:16 * half + 16, 0:31], src, pos, ALU.add))
                dve.sem_inc(s["blocks_ready"], 1)
                dve.wait_ge(s["dist_ready"], 1)
                step(nc.vector.tensor_scalar(valid[:, :, :], dist[:, :, :], 0.0, None, ALU.is_ge))
                step(nc.vector.tensor_scalar(hide[:, :, :], valid[:, :, :], -1.0, -NEG, ALU.add, ALU.mult))
                step(nc.vector.memset(kpad[:, :, :], 0.0))
                step(nc.vector.memset(vz[:, :, :], 0.0))
                dve.wait_ge(s["kv_sum"], 1)
                for e in range(2):
                    step(nc.vector.tensor_copy(kpad[64 * e:64 * e + 64, e, :], k.bank[2][64 * e:64 * e + 64, 0:NBLK]))
                for h in range(H):
                    step(nc.vector.tensor_copy(vz[32 * h:32 * h + 32, h, :], k.bank[3][32 * h:32 * h + 32, 0:64]))
                dve.sem_inc(s["kv_ready"], 1)
                dve.wait_ge(s["scores"], 1)
                step(nc.vector.tensor_scalar(w[:, :, :, :].rearrange("p t h n -> p (t h n)"), k.bank[4][:, :], 0.125, None, ALU.mult))
                for h in range(H):
                    step(nc.vector.scalar_tensor_tensor(out=w[:, :, h, :], in0=dist[:, :, :], scalar=-(2.0 ** (-2.0 * (h + 1))),
                                                        in1=w[:, :, h, :], op0=ALU.mult, op1=ALU.add))
                rows = lambda t: t[:, :, :].unsqueeze(2).to_broadcast([P, TT, H, NBLK])
                step(nc.vector.tensor_tensor(w[:, :, :, :], w[:, :, :, :], rows(hide), ALU.add))
                step(nc.vector.tensor_reduce(out=mx[:, :], in_=flat, axis=AX.X, op=ALU.max))
                nc.vector.tensor_tensor(flat, flat, mx[:, :].unsqueeze(2).to_broadcast([P, TT * H, NBLK]), ALU.subtract).then_inc(s["shifted"], 1)
                dve.wait_ge(s["exps"], 1)
                step(nc.vector.tensor_tensor(w[:, :, :, :], w[:, :, :, :], rows(valid), ALU.mult))
                step(nc.vector.tensor_reduce(out=mx[:, :], in_=flat, axis=AX.X, op=ALU.add))
                step(nc.vector.tensor_scalar(mx[:, :], mx[:, :], 1e-30, None, ALU.max))
                step(nc.vector.reciprocal(mx[:, :], mx[:, :]))
                step(nc.vector.tensor_tensor(mx[:, :].rearrange("p (t h) -> p t h", h=H), mx[:, :].rearrange("p (t h) -> p t h", h=H),
                                             a.gate[:, :, :].rearrange("p t (h b) -> p t h b", b=3)[:, :, :, 0], ALU.mult))
                nc.vector.tensor_tensor(flat, flat, mx[:, :].unsqueeze(2).to_broadcast([P, TT * H, NBLK]), ALU.mult).then_inc(s["weights_ready"], 1)
                dve.wait_ge(s["turned"], 1)
                nc.vector.tensor_copy(wT[:, :, :], k.bank[5][:, :].rearrange("p (t q) -> p t q", t=TT)).then_inc(s["kept"], 1)
                dve.wait_ge(s["summed"], 1)
                for i in range(2):
                    step(nc.vector.tensor_tensor(k.mixed[:, 6 + i, :], k.mixed[:, 6 + i, :], k.bank[6 + i][:, :], ALU.add))

            @block.scalar
            def _(act):
                for m in range(2):
                    act.wait_ge(s["hidden_sum"], m + 1)
                    nc.scalar.activation(hidden[:, m, :, :].rearrange("p v n -> p (v n)"), k.bank[m][:, 0:2 * NBLK],
                                         ACT.Gelu_apprx_tanh).then_inc(s["hidden_ready"], 1)
                act.wait_ge(s["shifted"], 1)
                nc.scalar.activation(flat, flat, ACT.Exp).then_inc(s["exps"], 1)

            @block.tensor
            def _(pe):
                pe.wait_ge(s["blocks_ready"], 1)
                for m in range(2):
                    for j in range(32):
                        last = nc.tensor.matmul(k.bank[m][:, 0:2 * NBLK], w1[:, j, m * P:(m + 1) * P], blocks[:, :, j, :],
                                                start=(j == 0), stop=(j == 31))
                    last.then_inc(s["hidden_sum"], 1)
                pe.wait_ge(s["hidden_ready"], 2)
                for e in range(2):
                    for m in range(2):
                        nc.tensor.matmul(k.bank[2][64 * e:64 * e + 64, 0:NBLK], w2[:, 0, m, :], hidden[:, m, 0, :], start=(m == 0), stop=(m == 1))
                for h in range(H):
                    for m in range(2):
                        last = nc.tensor.matmul(k.bank[3][32 * h:32 * h + 32, 0:64], hidden[:, m, 1, :], w2[:, 1, m, :], start=(m == 0), stop=(m == 1))
                last.then_inc(s["kv_sum"], 1)
                pe.wait_ge(s["kv_ready"], 1)
                for t in range(TT):
                    for i in range(2):
                        last = nc.tensor.matmul(k.bank[4][:, (2 * t + i) * 64:(2 * t + i + 1) * 64],
                                                k.cols[:, T_Q + i, LEAD + t * P:LEAD + (t + 1) * P], kpad[:, :, :], start=True, stop=True)
                last.then_inc(s["scores"], 1)
                pe.wait_ge(s["weights_ready"], 1)
                for t in range(TT):
                    last = nc.tensor.transpose(k.bank[5][:, t * P:(t + 1) * P], w[:, t, :, :].rearrange("p h n -> p (h n)"), k.ident[:, :])
                last.then_inc(s["turned"], 1)
                pe.wait_ge(s["kept"], 1)
                for t in range(TT):
                    for h in range(H):
                        last = nc.tensor.matmul(k.bank[6 + h // 2][64 * (h % 2):64 * (h % 2) + 64, t * P:(t + 1) * P],
                                                vz[:, h, :], wT[:, t, :], start=True, stop=True)
                last.then_inc(s["summed"], 1)


def nsa_mixer(nc, k, A, l):
    with ExitStack() as held:
        def sb(name, shape):
            return held.enter_context(nc.sbuf_tensor(name, shape, F32))
        a = Named()
        row = lambda name: A[name][bass.ds(l, 1), :, :].rearrange("a p c -> (a p) c")
        a.w1_dram, a.w2_dram = row("cmp_w1"), row("cmp_w2")
        a.w1 = sb("nsa_w1", [P, 32 * 256])
        a.w2 = sb("nsa_w2", [P, 256])
        a.gate = sb("nsa_gate", [P, TT, 12])
        with ExitStack() as first:
            fb = lambda name, shape: first.enter_context(nc.sbuf_tensor(name, shape, F32))
            a.keys = fb("nsa_keys", [P, 2, 2, SEQ])
            a.vT = fb("nsa_vT", [P, TT, P])
            a.dist = k.wide[:, 3, 0:SEQ]
            a.alibi = k.wide[:, 0:2, :].rearrange("p a c -> p (a c)").rearrange("p (h t) -> p h t", h=4)
            a.weights = fb("nsa_weights", [P, 3, SEQ])
            a.turned = fb("nsa_turned", [P, 2, SEQ])
            a.neg_max = fb("nsa_neg_max", [P, 32])
            a.total = fb("nsa_total", [P, 32])
            a.inv = fb("nsa_inv", [P, 32])
            attention(nc, k, a)
        compressed_attention(nc, k, a)


def output_projection(nc, k, A, l):
    with stage(nc, "block_done", "added", "weights_in0", "weights_in1", "weights_in2", "weights_in3") as (block, s):
        loaded = (s["weights_in0"], s["weights_in1"], s["weights_in2"], s["weights_in3"])

        @block.sync
        def _(sp):
            for c in range(DB):
                if c >= SLOTS:
                    sp.wait_ge(s["block_done"], c - SLOTS + 1)
                sp.dma_start(k.ring[:, c % SLOTS, :], A["w_out"][bass.ds(l, 1), c, :, :].rearrange("a p c -> (a p) c")).then_inc(loaded[c % SLOTS], 16)

        @block.tensor
        def _(pe):
            for c in range(DB):
                pe.wait_ge(loaded[c % SLOTS], 16 * (c // SLOTS + 1))
                for t in range(TT):
                    for half in range(2):
                        last = nc.tensor.matmul(k.bank[2 * t + half][:, :], k.mixed[:, c, t * P:(t + 1) * P],
                                                k.ring[:, c % SLOTS, half * 512:(half + 1) * 512],
                                                start=(c == 0), stop=(c == DB - 1))
                last.then_inc(s["block_done"], 1)

        @block.vector
        def _(dve):
            dve.wait_ge(s["block_done"], DB)
            for t in range(TT):
                for half in range(2):
                    o = slice(half * 512, (half + 1) * 512)
                    nc.vector.tensor_tensor(k.h[:, t, o], k.h[:, t, o], k.bank[2 * t + half][:, :], ALU.add).then_inc(s["added"], 1)


HEADS = 8
TOP = 16


def choose_experts(nc, k, p, A, l):
    with stage(nc, "keys_in", "scores", "ranked", "dve_done", "positions", "converted", "matched", "weighed", "shifted",
               "exps", "chosen", "turned", "kept") as (block, s):
        @block.sync
        def _(sp):
            sp.dma_start(p.keys[:, :], A["peer_keys"][bass.ds(l, 1), :, :].rearrange("a p c -> (a p) c")).then_inc(s["keys_in"], 16)
            sp.wait_ge(s["keys_in"], 16)

        @block.tensor
        def _(pe):
            pe.wait_ge(s["keys_in"], 16)

            def turn(t):
                pe.wait_ge(s["chosen"], t + 1)
                if t:
                    pe.wait_ge(s["kept"], t)
                for n in range(3):
                    last = nc.tensor.transpose(k.bank[4][:, n * P:(n + 1) * P], p.chosen[:, n, :], k.ident[:, :])
                last.then_inc(s["turned"], 1)
            for t in range(TT):
                if t:
                    pe.wait_ge(s["ranked"], t)
                for n in range(2 * HEADS):
                    last = nc.tensor.matmul(k.bank[n // 4][:, (n % 4) * P:(n % 4 + 1) * P], p.q[:, n, t * P:(t + 1) * P],
                                            p.keys[:, n * P:(n + 1) * P], start=True, stop=True)
                last.then_inc(s["scores"], 1)
                if t:
                    turn(t - 1)
            turn(TT - 1)

        @block.vector
        def _(dve):
            step = in_order(dve, s["dve_done"])

            def top16(values, best, index):
                step(nc.vector.max(out=best[:, 0:8], in_=values))
                nc.vector.max_index(out=index[:, 0:8], in_max=best[:, 0:8], in_values=values)
                rest = p.rest[:, 0:values.shape[1]]
                step(nc.vector.match_replace(out=rest, in_to_replace=best[:, 0:8], in_values=values, imm_value=-3.0e38))
                step(nc.vector.max(out=best[:, 8:16], in_=rest))
                return nc.vector.max_index(out=index[:, 8:16], in_max=best[:, 8:16], in_values=rest)
            for t in range(TT):
                dve.wait_ge(s["scores"], t + 1)
                for n in range(2 * HEADS):
                    last = top16(k.bank[n // 4][:, (n % 4) * P:(n % 4 + 1) * P], p.best[:, n, :], p.index[:, n, :])
                last.then_inc(s["ranked"], 1)
                dve.wait_ge(s["ranked"], t + 1)
                best = p.best[:, :, :].rearrange("p (h c) k -> p h c k", c=2)
                step(nc.vector.tensor_tensor(p.sums[:, :, :, :], best[:, :, 0, :].unsqueeze(3).to_broadcast([P, HEADS, TOP, TOP]),
                                             best[:, :, 1, :].unsqueeze(2).to_broadcast([P, HEADS, TOP, TOP]), ALU.add))
                for h in range(HEADS):
                    last = top16(p.sums[:, h, :, :].rearrange("p a b -> p (a b)"), p.top[:, h, :], p.where[:, h, :])
                step(last)
                if t:
                    dve.wait_ge(s["turned"], t)
                step(nc.vector.tensor_tensor(p.chosen[:, 2, :].rearrange("p (h k) -> p h k", k=TOP), p.top[:, :, :],
                                             p.top[:, :, 0:1].to_broadcast([P, HEADS, TOP]), ALU.subtract))
                dve.sem_inc(s["shifted"], 1)
                flat = p.where[:, :, :].rearrange("p h k -> p (h k)")
                step(nc.vector.tensor_scalar(p.rank[:, 0, :], flat, 4, None, ALU.logical_shift_right))
                step(nc.vector.tensor_scalar(p.rank[:, 1, :], flat, 15, None, ALU.bitwise_and))
                step(nc.vector.tensor_copy(p.rank_f[:, :, :], p.rank[:, :, :]))
                step(nc.vector.tensor_copy(p.index_f[:, :, :], p.index[:, :, :]))
                index = p.index_f[:, :, :].rearrange("p (h c) k -> p h c k", c=2)
                for c in range(2):
                    hot = p.hot[:, c, :, :, :].rearrange("p h k a -> p (h k) a")
                    step(nc.vector.tensor_tensor(hot, p.rank_f[:, c, :].unsqueeze(2).to_broadcast([P, P, TOP]),
                                                 k.iota16[:, :].unsqueeze(1).to_broadcast([P, P, TOP]), ALU.is_equal))
                    step(nc.vector.tensor_tensor(p.hot[:, c, :, :, :], p.hot[:, c, :, :, :],
                                                 index[:, :, c, :].unsqueeze(2).to_broadcast([P, HEADS, TOP, TOP]), ALU.mult))
                    step(nc.vector.tensor_reduce(out=p.chosen[:, c, :], in_=hot, axis=AX.X, op=ALU.add))
                dve.wait_ge(s["exps"], t + 1)
                gate = p.chosen[:, 2, :].rearrange("p (h k) -> p h k", k=TOP)
                step(nc.vector.tensor_reduce(out=p.total[:, :], in_=gate, axis=AX.X, op=ALU.add))
                step(nc.vector.reciprocal(p.total[:, :], p.total[:, :]))
                nc.vector.tensor_tensor(gate, gate, p.total[:, :].unsqueeze(2).to_broadcast([P, HEADS, TOP]), ALU.mult).then_inc(s["chosen"], 1)
                dve.wait_ge(s["chosen"], t + 1)

        @block.scalar
        def _(act):
            for t in range(TT):
                act.wait_ge(s["shifted"], t + 1)
                nc.scalar.activation(p.chosen[:, 2, :], p.chosen[:, 2, :], ACT.Exp).then_inc(s["exps"], 1)
                act.wait_ge(s["turned"], t + 1)
                nc.scalar.copy(p.picks[:, :, t * P:(t + 1) * P], k.bank[4][:, 0:3 * P].rearrange("p (n t) -> p n t", n=3)).then_inc(s["kept"], 1)


GROUP = 32
HOTS = 8


def spread_gates(nc, k, p):
    per = 2 * GROUP
    quads = per // 4
    with stage(nc, "picked", "hots", "products", "copied", "stored0", "stored1") as (block, s):
        stored = (s["stored0"], s["stored1"])

        @block.vector
        def _(dve):
            dve.sem_inc(s["hots"], 1)
            with dve.Fori(0, SEQ // per) as it:
                dve.wait_ge(s["hots"], it * per + 1)
                nc.vector.tensor_copy(p.now[:, :, :], p.picks[:, :, bass.ds(it * per, per)]).then_inc(s["picked"], 1)
                dve.wait_ge(s["picked"], it + 1)
                for n in range(per):
                    dve.wait_ge(s["products"], it * per + n + 1)
                    nc.vector.tensor_scalar(p.hot1[:, n % HOTS, :], k.iota128[:, :], p.now[:, 0, n:n + 1], None, ALU.is_equal)
                    nc.vector.tensor_scalar(p.hot2[:, n % HOTS, :], k.iota128[:, :], p.now[:, 1, n:n + 1],
                                            p.now[:, 2, n:n + 1], ALU.is_equal, ALU.mult).then_inc(s["hots"], 1)

        @block.tensor
        def _(pe):
            pe.sem_inc(s["products"], HOTS)
            with pe.Fori(0, SEQ // per) as it:
                for n in range(per):
                    if n % 4 == 0:
                        pe.wait_ge(s["copied"], it * quads + n // 4 + 1)
                    pe.wait_ge(s["hots"], it * per + n + 2)
                    nc.tensor.matmul(k.bank[n // 4 % 8][:, (n % 4) * P:(n % 4 + 1) * P], p.hot1[:, n % HOTS, :],
                                     p.hot2[:, n % HOTS, :], start=True, stop=True).then_inc(s["products"], 1)

        @block.scalar
        def _(act):
            act.sem_inc(s["copied"], 8)
            with act.Fori(0, SEQ // per) as it:
                for q in range(quads):
                    g = q // (quads // 2)
                    if q % (quads // 2) == 0:
                        act.wait_ge(stored[g], it * 16 + 16)
                    act.wait_ge(s["products"], it * per + 4 * (q + 1) + HOTS)
                    tok = 4 * (q % (quads // 2))
                    nc.scalar.copy(p.out[:, g, :, tok:tok + 4].rearrange("p j t -> p t j"),
                                   k.bank[q % 8][:, :].rearrange("p (t j) -> p t j", t=4)).then_inc(s["copied"], 1)

        @block.sync
        def _(sp):
            for g in range(2):
                sp.sem_inc(stored[g], 16)
            with sp.Fori(0, SEQ // per) as it:
                for g in range(2):
                    sp.wait_ge(s["copied"], it * quads + (g + 1) * (quads // 2) + 8)
                    sp.dma_start(p.gates[:, bass.ds(it * 2 + g, 1), :, :].rearrange("p a j t -> p (a j t)"),
                                 p.out[:, g, :, :].rearrange("p j t -> p (j t)")).then_inc(stored[g], 16)
            for g in range(2):
                sp.wait_ge(stored[g], 16 * (SEQ // per) + 16)


GJ = 4
N_GROUPS = P // GJ


def run_experts(nc, k, d, A, l):
    with stage(nc, "u_in0", "u_in1", "v_in0", "v_in1", "g_in0", "g_in1", "u_done", "acts", "gated", "y_done", "y_added") as (block, s):
        u_in, v_in, g_in = (s["u_in0"], s["u_in1"]), (s["v_in0"], s["v_in1"]), (s["g_in0"], s["g_in1"])

        def pairs(engine, body, tail=None):
            for e in range(2):
                body(0, e, e == 0)
            with engine.Fori(1, N_GROUPS // 2) as it:
                for e in range(2):
                    body(it, e, False)
            if tail:
                tail()

        @block.sync
        def _(sp):
            def load(it, e, first):
                g = it * 2 + e
                tiles = lambda w: w[bass.ds(l * P + g * GJ, GJ), :, :].rearrange("n p c -> p n c")
                if not isinstance(it, int):
                    sp.wait_ge(s["u_done"], (it * 2 + (e - 1)) * GJ)
                sp.dma_start(d.u[:, e, :, :], tiles(A["peer_u"])).then_inc(u_in[e], 16)
                if not isinstance(it, int):
                    sp.wait_ge(s["y_done"], (it * 2 + e) * 8)
                sp.dma_start(d.g[:, e, :, :, :], d.gates[:, :, bass.ds(g * GJ, GJ), :]).then_inc(g_in[e], 16)
                sp.dma_start(d.v[:, e, :, :], tiles(A["peer_v"])).then_inc(v_in[e], 16)
            pairs(sp, load)

        @block.tensor
        def _(pe):
            pe.sem_inc(s["y_done"], 8)

            def with_u(it, e):
                g = it * 2 + e
                pe.wait_ge(u_in[e], it * 16 + 16)
                for j in range(GJ):
                    pe.wait_ge(s["acts"], g * GJ + (j + 1))
                    for b in range(DB):
                        last = nc.tensor.matmul(k.bank[j][:, :], d.u[:, e, j, b * P:(b + 1) * P], k.xT[:, b, :],
                                                start=(b == 0), stop=(b == DB - 1))
                    last.then_inc(s["u_done"], 1)

            def with_v(it, e):
                g = it * 2 + e
                pe.wait_ge(v_in[e], it * 16 + 16)
                pe.wait_ge(s["gated"], g * GJ + GJ)
                for o in range(8):
                    pe.wait_ge(s["y_added"], g * 8 + (o + 1))
                    t, half = o // 2, o % 2
                    for j in range(GJ):
                        last = nc.tensor.matmul(k.bank[4 + o % 4][:, :], d.a[:, e, j, t * P:(t + 1) * P],
                                                d.v[:, e, j, half * 512:(half + 1) * 512], start=(j == 0), stop=(j == GJ - 1))
                    last.then_inc(s["y_done"], 1)

            def body(it, e, first):
                with_u(it, e)
                if e == 1:
                    with_v(it, 0)
                elif not first:
                    with_v(it + (-1), 1)
            pairs(pe, body, lambda: with_v(N_GROUPS // 2 - 1, 1))

        @block.scalar
        def _(act):
            act.sem_inc(s["acts"], GJ)

            def body(it, e, first):
                g = it * 2 + e
                if not first:
                    act.wait_ge(s["y_done"], g * 8)
                for j in range(GJ):
                    act.wait_ge(s["u_done"], g * GJ + (j + 1))
                    nc.scalar.activation(d.a[:, e, j, :], k.bank[j][:, :], ACT.Gelu_apprx_tanh).then_inc(s["acts"], 1)
            pairs(act, body)

        @block.vector
        def _(dve):
            dve.sem_inc(s["y_added"], 4)

            def gate(it, e):
                g = it * 2 + e
                dve.wait_ge(g_in[e], it * 16 + 16)
                for j in range(GJ):
                    dve.wait_ge(s["acts"], g * GJ + (j + 1) + GJ)
                    nc.vector.tensor_tensor(d.a[:, e, j, :].rearrange("p (b t) -> p b t", t=GROUP),
                                            d.a[:, e, j, :].rearrange("p (b t) -> p b t", t=GROUP),
                                            d.g[:, e, :, j, :], ALU.mult).then_inc(s["gated"], 1)

            def add(it, e):
                g = it * 2 + e
                for o in range(8):
                    t, half = o // 2, o % 2
                    dve.wait_ge(s["y_done"], g * 8 + (o + 1) + 8)
                    c = slice(half * 512, (half + 1) * 512)
                    nc.vector.tensor_tensor(k.h[:, t, c], k.h[:, t, c], k.bank[4 + o % 4][:, :], ALU.add).then_inc(s["y_added"], 1)

            def body(it, e, first):
                gate(it, e)
                if e == 1:
                    add(it, 0)
                elif not first:
                    add(it + (-1), 1)
            pairs(dve, body, lambda: add(N_GROUPS // 2 - 1, 1))


def peer(nc, k, A, l, gates):
    with ExitStack() as held:
        def sb(name, shape, dt=F32):
            return held.enter_context(nc.sbuf_tensor(name, shape, dt))
        p = Named()
        p.gates = gates
        p.picks = sb("peer_picks", [P, 3, SEQ])
        with ExitStack() as first:
            fb = lambda name, shape, dt=F32: first.enter_context(nc.sbuf_tensor(name, shape, dt))
            p.q = fb("peer_q", [P, 2 * HEADS, SEQ])
            p.keys = fb("peer_keys", [P, 2 * HEADS * P])
            p.best = fb("peer_best", [P, 2 * HEADS, TOP])
            p.index = fb("peer_index", [P, 2 * HEADS, TOP], U32)
            p.index_f = fb("peer_index_f", [P, 2 * HEADS, TOP])
            p.rest = fb("peer_rest", [P, TOP * TOP])
            p.sums = fb("peer_sums", [P, HEADS, TOP, TOP])
            p.top = fb("peer_top", [P, HEADS, TOP])
            p.where = fb("peer_where", [P, HEADS, TOP], U32)
            p.rank = fb("peer_rank", [P, 2, P], U32)
            p.rank_f = fb("peer_rank_f", [P, 2, P])
            p.hot = fb("peer_hot", [P, 2, HEADS, TOP, TOP])
            p.chosen = fb("peer_chosen", [P, 3, P])
            p.total = fb("peer_total", [P, HEADS])
            project(nc, k, A["peer_wq"], l * 16, 16, p.q, 0)
            choose_experts(nc, k, p, A, l)
        with ExitStack() as second:
            fb = lambda name, shape, dt=F32: second.enter_context(nc.sbuf_tensor(name, shape, dt))
            p.now = fb("peer_now", [P, 3, 2 * GROUP])
            p.hot1 = fb("peer_hot1", [P, HOTS, P])
            p.hot2 = fb("peer_hot2", [P, HOTS, P])
            p.out = fb("peer_out", [P, 2, P, GROUP])
            spread_gates(nc, k, p)
    with ExitStack() as held:
        fb = lambda name, shape, dt=F32: held.enter_context(nc.sbuf_tensor(name, shape, dt))
        d = Named()
        d.gates = gates
        d.u = fb("peer_u", [P, 2, GJ, DM])
        d.v = fb("peer_v", [P, 2, GJ, DM])
        d.g = fb("peer_g", [P, 2, SEQ // GROUP, GJ, GROUP])
        d.a = fb("peer_a", [P, 2, GJ, SEQ])
        run_experts(nc, k, d, A, l)


def final_norm(nc, k, A, out):
    with stage(nc, "gain_in", "squares", "variance", "deviation", "dve_done", "normed", "stored") as (block, s):
        @block.sync
        def _(sp):
            sp.dma_start(k.xT[:, 0:2, :].rearrange("p a c -> p (a c)"), A["final_norm"].to_broadcast([P, DM])).then_inc(s["gain_in"], 16)
            for t in range(TT):
                sp.wait_ge(s["normed"], t + 1)
                sp.dma_start(out[t * P:(t + 1) * P, :], k.wide[:, t, :]).then_inc(s["stored"], 16)
            sp.wait_ge(s["stored"], 16 * TT)

        @block.scalar
        def _(act):
            for t in range(TT):
                if t:
                    act.wait_ge(s["squares"], t)
                nc.scalar.activation(k.xT[:, 2:4, :].rearrange("p a c -> p (a c)"), k.h[:, t, :], ACT.Square,
                                     accum_out=k.stat[:, t:t + 1]).then_inc(s["squares"], 1)
            act.wait_ge(s["variance"], 1)
            nc.scalar.activation(k.stat[:, 8:12], k.stat[:, 4:8], ACT.Sqrt).then_inc(s["deviation"], 1)

        @block.vector
        def _(dve):
            step = in_order(dve, s["dve_done"])
            dve.wait_ge(s["squares"], TT)
            nc.vector.tensor_scalar(k.stat[:, 4:8], k.stat[:, 0:4], 1.0 / DM, EPS, ALU.mult, ALU.add).then_inc(s["variance"], 1)
            dve.wait_ge(s["deviation"], 1)
            step(nc.vector.reciprocal(k.stat[:, 12:16], k.stat[:, 8:12]))
            dve.wait_ge(s["gain_in"], 16)
            for t in range(TT):
                nc.vector.scalar_tensor_tensor(out=k.wide[:, t, :], in0=k.h[:, t, :], scalar=k.stat[:, 12 + t:13 + t],
                                               in1=k.xT[:, 0:2, :].rearrange("p a c -> p (a c)"),
                                               op0=ALU.mult, op1=ALU.mult).then_inc(s["normed"], 1)


def program(nc, A, out):
    ctx = ExitStack()
    with ctx:
        def sb(name, shape, dt=F32):
            return ctx.enter_context(nc.sbuf_tensor(name, shape, dt))
        k = Named()
        k.h = sb("h", [P, TT, DM])
        k.xT = sb("xT", [P, DB, SEQ])
        k.wide = sb("wide", [P, TT, DM])
        k.ring = sb("ring", [P, SLOTS, DB * P])
        k.vec = sb("vec", [P, N_VEC])
        k.stat = sb("stat", [P, 32])
        k.smallT = sb("smallT", [P, TT, 16])
        k.lru_w = sb("lru_w", [P, 2, 2, 64])
        k.lora = sb("lora", [P, 512])
        k.ident = sb("ident", [P, P])
        k.ones = sb("ones", [P, P])
        k.upper = sb("upper", [P, P])
        k.strict = sb("strict", [P, P])
        k.lower = sb("lower", [P, P])
        k.same = {b: sb(f"same{b}", [P, P]) for b in (8, 16, 32, 64)}
        k.reset = sb("reset", [P, SEQ])
        k.iota16 = sb("iota16", [P, 16])
        k.iota128 = sb("iota128", [P, P])
        k.bank = [ctx.enter_context(nc.psum_tensor(f"bank{i}", [P, 512], F32)) for i in range(8)]
        gates = nc.dram_tensor("gates", (P, SEQ // GROUP, P, GROUP), F32, kind="Internal").ap()
        make_constants(nc, k)
        with stage(nc, "x_in") as (block, s):
            @block.sync
            def _(sp):
                sp.dma_start(k.h[:, :, :].rearrange("p t c -> p (t c)"), A["x"]).then_inc(s["x_in"], 16)
                sp.wait_ge(s["x_in"], 16)
        with nc.Fori(0, DEPTH) as l:
            with ExitStack() as held:
                k.cols = held.enter_context(nc.sbuf_tensor("cols", [P, N_COLS, LEAD + SEQ], F32))
                k.mixed = held.enter_context(nc.sbuf_tensor("mixed", [P, DB, SEQ], F32))
                load_layer_vectors(nc, k, A, l)
                norm_and_transpose(nc, k, VEC["mix_norm"])
                project(nc, k, A["w_in"], l * N_COLS, N_COLS, k.cols, LEAD)
                ssd_mixer(nc, k)
                lru_mixer(nc, k)
                rwkv_mixer(nc, k)
                nsa_mixer(nc, k, A, l)
                output_projection(nc, k, A, l)
            norm_and_transpose(nc, k, VEC["ffn_norm"])
            peer(nc, k, A, l, gates)
        final_norm(nc, k, A, out)


def kernel(**inputs):
    import concourse.bacc as bacc
    from concourse.bass_utils import run_bass_kernel_spmd

    nc = bacc.Bacc("TRN2", target_bir_lowering=False, num_devices=1)
    arrays = {"in_" + n: a for n, a in lay_out({n: np.asarray(a) for n, a in inputs.items()}).items()}
    A = {n[3:]: nc.dram_tensor(n, a.shape, mybir.dt.from_np(a.dtype), kind="ExternalInput").ap() for n, a in arrays.items()}
    out = nc.dram_tensor("out", (SEQ, DM), F32, kind="ExternalOutput").ap()
    program(nc, A, out)
    r = run_bass_kernel_spmd(nc, [arrays], core_ids=[0])
    return r.results[0]["out"].reshape(1, SEQ, DM)
```

```python
import math
from contextlib import ExitStack, contextmanager

import numpy as np
import concourse.bass as bass
from concourse import mybir

F32 = mybir.dt.float32
F32R = mybir.dt.float32r
U32 = mybir.dt.uint32
ALU = mybir.AluOpType
ACT = mybir.ActivationFunctionType
AX = mybir.AxisListType

P = 128
SEQ = 512
DM = 1024
DEPTH = 2
TT = SEQ // P
DB = DM // P
EPS = 1e-6
GN_EPS = 64e-5
NEG = -1e30

T_GATE, T_XR, T_Z, T_X, T_B, T_C = 0, 2, 4, 6, 8, 9
T_R, T_K, T_V, T_WDAD, T_GD = 10, 12, 14, 16, 17
T_Q, T_CMP, T_KSKW, T_VSVW, T_SMALL = 18, 20, 21, 22, 23
N_COLS = 24
LEAD = 4
SLOTS = 4

VEC = {}


def _columns():
    at = 0
    for name, n in (("mix_norm", 8), ("ffn_norm", 8), ("ssm_cw", 16), ("ssm_cb", 4), ("ssm_norm", 2), ("ssm_d", 2),
                    ("lru_cw", 8), ("lru_cb", 2), ("lru_ba", 2), ("lru_bi", 2), ("lru_lam", 2), ("mu", 8),
                    ("w0", 2), ("a0", 2), ("kk", 2), ("ka", 2), ("rk", 2), ("ln_w", 2), ("ln_b", 2),
                    ("dt_bias", 4), ("a_log", 4), ("pos", 32)):
        VEC[name] = at
        at += n
    return at


N_VEC = _columns()


class Named:
    pass


@contextmanager
def stage(nc, *names):
    with ExitStack() as held:
        sems = {n: held.enter_context(nc.semaphore(n)) for n in names}
        with nc.Block() as block:
            yield block, sems
        for s in sems.values():
            nc.sync.sem_clear(s)
        nc.all_engine_barrier()


def in_order(engine, done):
    count = [0]

    def step(instruction):
        count[0] += 1
        instruction.then_inc(done, 1)
        engine.wait_ge(done, count[0])
    return step


def make_constants(nc, k):
    with stage(nc, "const_done") as (block, s):
        @block.gpsimd
        def _(pool):
            step = in_order(pool, s["const_done"])
            step(nc.gpsimd.memset(k.ones[:, :], 1.0))

            def keep(out, src, pattern, base, mult, op=ALU.is_ge, fill=0.0):
                step(nc.gpsimd.affine_select(out=out, in_=src, compare_op=op, fill=fill, base=base,
                                             pattern=pattern, channel_multiplier=mult))
            one = k.ones[:, :]
            keep(k.ident[:, :], one, [[-1, P]], 0, 1, ALU.is_equal)
            keep(k.upper[:, :], one, [[1, P]], 0, -1)
            keep(k.strict[:, :], one, [[1, P]], -1, -1)
            keep(k.lower[:, :], one, [[-1, P]], -1, 1)
            for b in (8, 16, 32, 64):
                m = k.same[b][:, :].rearrange("p (n w) -> p n w", w=b)
                o = one.rearrange("p (n w) -> p n w", w=b)
                keep(m, o, [[-b, P // b], [0, b]], 0, 1)
                keep(m, m, [[b, P // b], [0, b]], b - 1, -1)
            step(nc.gpsimd.memset(k.reset[:, :], 1.0))
            step(nc.gpsimd.memset(k.reset[:, :].rearrange("p (c w) -> p c w", w=32)[:, :, 0:1], 0.0))
            step(nc.gpsimd.iota(k.iota16[:, :], pattern=[[1, 16]], base=0, channel_multiplier=0,
                                allow_small_or_imprecise_dtypes=True))
            step(nc.gpsimd.iota(k.iota128[:, :], pattern=[[1, P]], base=0, channel_multiplier=0,
                                allow_small_or_imprecise_dtypes=True))


def load_layer_vectors(nc, k, A, l):
    with stage(nc, "vectors_in", "zeroed") as (block, s):
        @block.sync
        def _(sp):
            for dst, name in ((k.vec[:, :], "vecs"), (k.lru_w[:, :, :, :].rearrange("p n i j -> p (n i j)"), "lru_w"),
                              (k.lora[:, :], "lora")):
                sp.dma_start(dst, A[name][bass.ds(l, 1), :, :].rearrange("a p c -> (a p) c")).then_inc(s["vectors_in"], 16)
            sp.wait_ge(s["vectors_in"], 48)

        @block.gpsimd
        def _(pool):
            nc.gpsimd.memset(k.cols[:, :, 0:LEAD], 0.0).then_inc(s["zeroed"], 1)


def norm_and_transpose(nc, k, gain, hi, lo, weights, layer_tile):
    with stage(nc, "weights_in", "squares", "variance", "deviation", "inverse", "scaled", "turned", "hi_done", "lo_done") as (block, s):
        @block.sync
        def _(sp):
            for u in range(SLOTS):
                sp.dma_start(k.ring[:, u, :], weights[bass.ds(layer_tile + u, 1), :, :].rearrange("a p c -> (a p) c")).then_inc(s["weights_in"], 16)
            sp.wait_ge(s["weights_in"], 16 * SLOTS)

        @block.scalar
        def _(act):
            for t in range(TT):
                if t:
                    act.wait_ge(s["squares"], t)
                nc.scalar.activation(k.wide[:, 0, :], k.h[:, t, :], ACT.Square,
                                     accum_out=k.stat[:, t:t + 1]).then_inc(s["squares"], 1)
            act.wait_ge(s["variance"], 1)
            nc.scalar.activation(k.stat[:, 8:12], k.stat[:, 4:8], ACT.Sqrt).then_inc(s["deviation"], 1)
            for b in range(DB):
                act.wait_ge(s["turned"], b + 1)
                nc.scalar.activation(hi[:, b, :], k.bank[b][:, :], ACT.Copy, scale=k.vec[:, gain + b:gain + b + 1]).then_inc(s["hi_done"], 1)

        @block.vector
        def _(dve):
            dve.wait_ge(s["squares"], TT)
            nc.vector.tensor_scalar(k.stat[:, 4:8], k.stat[:, 0:4], 1.0 / DM, EPS, ALU.mult, ALU.add).then_inc(s["variance"], 1)
            dve.wait_ge(s["deviation"], 1)
            nc.vector.reciprocal(k.stat[:, 12:16], k.stat[:, 8:12]).then_inc(s["inverse"], 1)
            dve.wait_ge(s["inverse"], 1)
            for t in range(TT):
                nc.vector.tensor_scalar(k.wide[:, t, :], k.h[:, t, :], k.stat[:, 12 + t:13 + t], None,
                                        ALU.mult).then_inc(s["scaled"], 1)
            for b in range(DB):
                dve.wait_ge(s["hi_done"], b + 1)
                nc.vector.scalar_tensor_tensor(out=lo[:, b, :], in0=k.bank[b][:, :], scalar=k.vec[:, gain + b:gain + b + 1],
                                               in1=hi[:, b, :].bitcast(F32), op0=ALU.mult, op1=ALU.subtract).then_inc(s["lo_done"], 1)

        @block.tensor
        def _(pe):
            pe.wait_ge(s["scaled"], TT)
            for b in range(DB):
                for t in range(TT):
                    last = nc.tensor.transpose(k.bank[b][:, t * P:(t + 1) * P], k.wide[:, t, b * P:(b + 1) * P],
                                               k.ident[:, :])
                last.then_inc(s["turned"], 1)


def three_products(nc, out, left, right, first, last):
    nc.tensor.matmul(out, left[0], right[0], start=first, stop=False)
    nc.tensor.matmul(out, left[0], right[1], start=False, stop=False)
    return nc.tensor.matmul(out, left[1], right[0], start=False, stop=last)


def project(nc, k, weights, layer_tile, n_tiles, out, lead, x_hi, x_lo, beside=None):
    per = SLOTS
    trips = n_tiles // per
    with ExitStack() as held:
        w_hi = held.enter_context(nc.sbuf_tensor(f"w_hi{n_tiles}", [P, 2, DM], F32R))
        w_lo = held.enter_context(nc.sbuf_tensor(f"w_lo{n_tiles}", [P, 2, DM], F32R))
        with stage(nc, "tile_done", "act_out", "dve_out", "hi_done", "lo_done", *[f"weights_in{u}" for u in range(per)],
                   *(beside.signals if beside else ())) as (block, s):
            loaded = [s[f"weights_in{u}"] for u in range(per)]

            def trips_of(engine, body, written_out=False):
                if written_out:
                    for it in range(trips - 1):
                        body(it, False)
                else:
                    with engine.Fori(0, trips - 1) as it:
                        body(it, False)
                body(trips - 1, True)

            @block.sync
            def _(sp):
                for u in range(per):
                    sp.sem_inc(loaded[u], 16)
                with sp.Fori(1, trips) as it:
                    for u in range(per):
                        sp.wait_ge(s["lo_done"], it * per + (u + 1 - per))
                        sp.dma_start(k.ring[:, u, :], weights[bass.ds(layer_tile + it * per + u, 1), :, :]
                                     .rearrange("a p c -> (a p) c")).then_inc(loaded[u], 16)

            @block.tensor
            def _(pe):
                def trip(it, last_trip):
                    for u in range(per):
                        pe.wait_ge(s["lo_done"], it * per + (u + 1))
                        pe.wait_ge(s["dve_out"] if u % 2 else s["act_out"], it * (per // 2) + (u // 2 + 1))
                        for b in range(DB):
                            c = slice(b * P, (b + 1) * P)
                            last = three_products(nc, k.bank[u][:, :], (w_hi[:, u % 2, c], w_lo[:, u % 2, c]),
                                                  (x_hi[:, b, :], x_lo[:, b, :]), b == 0, b == DB - 1)
                        last.then_inc(s["tile_done"], 1)
                if beside:
                    with pe.Fori(0, beside.products_after) as it:
                        trip(it, False)
                    beside.tensor(pe, s)
                    with pe.Fori(beside.products_after, trips) as it:
                        trip(it, False)
                else:
                    trips_of(pe, trip)

            def place(it, u):
                at = it * per + u
                at = slice(at, at + 1) if isinstance(it, int) else bass.ds(at, 1)
                return out[:, at, lead:lead + SEQ].rearrange("p a t -> p (a t)")

            @block.scalar
            def _(act):
                def hi(it, u):
                    act.wait_ge(loaded[u % per], it * 16 + 16 * (u // per + 1))
                    nc.scalar.copy(w_hi[:, u % 2, :], k.ring[:, u % per, :]).then_inc(s["hi_done"], 1)
                act.sem_inc(s["act_out"], per // 2)
                hi(0, 0)
                hi(0, 1)

                def trip(it, last_trip):
                    for u in range(per):
                        act.wait_ge(s["tile_done"], it * per + (u + 1))
                        if not (last_trip and u + 2 >= per):
                            hi(it, u + 2)
                        if u % 2 == 0:
                            nc.scalar.copy(place(it, u), k.bank[u][:, :]).then_inc(s["act_out"], 1)
                        if beside:
                            beside.scalar(act, s, it * per + u)
                trips_of(act, trip, beside is not None)

            @block.vector
            def _(dve):
                def low(it, u):
                    dve.wait_ge(s["hi_done"], it * per + (u + 1))
                    nc.vector.tensor_tensor(w_lo[:, u % 2, :], k.ring[:, u % per, :], w_hi[:, u % 2, :].bitcast(F32),
                                            ALU.subtract).then_inc(s["lo_done"], 1)
                dve.sem_inc(s["dve_out"], per // 2)
                low(0, 0)
                low(0, 1)

                def trip(it, last_trip):
                    for u in range(per):
                        dve.wait_ge(s["tile_done"], it * per + (u + 1))
                        if not (last_trip and u + 2 >= per):
                            low(it, u + 2)
                        if u % 2 == 1:
                            nc.vector.tensor_copy(place(it, u), k.bank[u][:, :]).then_inc(s["dve_out"], 1)
                        if beside:
                            beside.vector(dve, s, it * per + u)
                trips_of(dve, trip, beside is not None)


def lay_out(a):
    L = DEPTH
    f = np.ascontiguousarray
    w = a["w_in"]
    s0, s1, s2 = 772, 1284, 2308
    cols = np.concatenate([np.arange(s0, s0 + 512), np.arange(0, 768), np.arange(s1, s1 + 1024),
                           np.arange(s2, s2 + 256),
                           np.arange(s2 + 256, s2 + 384),
                           np.arange(s2 + 384, s2 + 448), np.arange(s2 + 512, s2 + 576),
                           np.arange(s2 + 448, s2 + 512), np.arange(s2 + 576, s2 + 640),
                           np.arange(768, 772), np.arange(s2 + 640, s2 + 652)])
    wi = np.zeros((L, DM, N_COLS * P), np.float32)
    wi[:, :, :cols.size] = w[:, :, cols]
    tile_w = lambda m, n: f(m.reshape(L, DB, P, n, P).transpose(0, 3, 2, 1, 4).reshape(L * n, P, DB * P))

    def chan(v, n):
        return v.reshape(L, n, P).transpose(0, 2, 1)
    conv = lambda v, n: v.reshape(L, 4, n, P).transpose(0, 3, 2, 1).reshape(L, P, n * 4)
    rows = lambda v: np.broadcast_to(v[:, None, :], (L, P, v.shape[1]))
    vecs = np.concatenate([
        chan(a["mix_norm"], 8), chan(a["ffn_norm"], 8), conv(a["ssm_conv_w"], 4), chan(a["ssm_conv_b"], 4),
        chan(a["ssm_norm"], 2), chan(np.repeat(a["ssm_d"], 64, axis=1), 2),
        conv(a["lru_conv_w"], 2), chan(a["lru_conv_b"], 2), chan(a["lru_ba"].reshape(L, 256), 2),
        chan(a["lru_bi"].reshape(L, 256), 2), chan(a["lru_lambda"], 2), chan(a["rwkv_mu"], 8),
        chan(a["rwkv_w0"], 2), chan(a["rwkv_a0"], 2), chan(a["rwkv_kk"], 2), chan(a["rwkv_ka"], 2),
        chan(a["rwkv_rk"].reshape(L, 256), 2), chan(a["rwkv_ln_w"], 2), chan(a["rwkv_ln_b"], 2),
        rows(a["ssm_dt_bias"]), rows(a["ssm_a_log"]),
        a["nsa_cmp_pos"].transpose(0, 1, 3, 2).reshape(L, P, 32)], axis=2)
    assert vecs.shape[2] == N_VEC
    return {
        "x": f(a["x"].reshape(TT, P, DM).transpose(1, 0, 2).reshape(P, TT * DM)),
        "w_in": tile_w(wi, N_COLS),
        "vecs": f(vecs),
        "lru_w": f(np.stack([a["lru_wa"].reshape(L, 2, P, 64), a["lru_wi"].reshape(L, 2, P, 64)], axis=1)
                   .transpose(0, 3, 1, 2, 4).reshape(L, P, 256)),
        "lora": f(np.concatenate([np.concatenate([a["rwkv_w2"], a["rwkv_a2"]], axis=1), a["rwkv_g2"]], axis=2)),
        "cmp_w1": f(a["nsa_cmp_w1"].reshape(L, 2, 32, 64, 256).transpose(0, 1, 3, 2, 4).reshape(L, P, 32 * 256)),
        "cmp_w2": f(a["nsa_cmp_w2"].reshape(L, 2, 2, P, 64).transpose(0, 3, 1, 2, 4).reshape(L, P, 256)),
        "w_out": f(a["w_out"].reshape(L, DB, P, DM)),
        "peer_wq": tile_w(a["peer_wq"], 16),
        "peer_keys": f(a["peer_keys"].reshape(L, 16, P, P).transpose(0, 3, 1, 2).reshape(L, P, 16 * P)),
        "peer_u": f(a["peer_u"].reshape(L, P, P, DB, P).transpose(0, 2, 4, 3, 1).reshape(L * P, P, DB * P)),
        "peer_v": f(a["peer_v"].reshape(L, P, P, DM).transpose(0, 2, 1, 3).reshape(L * P, P, DM)),
        "final_norm": f(a["final_norm"].reshape(1, DM)),
    }


def conv(nc, k, step, out, tile, weight, bias):
    src = k.cols[:, tile, :]
    step(nc.vector.tensor_scalar(out, src[:, LEAD - 3:LEAD - 3 + SEQ], k.vec[:, weight:weight + 1],
                                 k.vec[:, bias:bias + 1], ALU.mult, ALU.add))
    for tap in range(1, 4):
        step(nc.vector.scalar_tensor_tensor(out=out, in0=src[:, LEAD - 3 + tap:LEAD - 3 + tap + SEQ],
                                            scalar=k.vec[:, weight + tap:weight + tap + 1], in1=out,
                                            op0=ALU.mult, op1=ALU.add))


def log1p(nc, step, x, z, z2, p):
    step(nc.vector.tensor_scalar(z, x, 2.0, None, ALU.add))
    step(nc.vector.reciprocal(z2, z))
    step(nc.vector.tensor_tensor(z, x, z2, ALU.mult))
    step(nc.vector.tensor_tensor(z2, z, z, ALU.mult))
    step(nc.vector.tensor_scalar(p, z2, 2.0 / 15, 2.0 / 13, ALU.mult, ALU.add))
    for n in (11, 9, 7, 5, 3, 1):
        step(nc.vector.tensor_tensor(p, p, z2, ALU.mult))
        step(nc.vector.tensor_scalar(p, p, 2.0 / n, None, ALU.add))
    step(nc.vector.tensor_tensor(x, p, z, ALU.mult))


def ssd_mixer(nc, k, xbc, sz):
    H = 4
    with ExitStack() as held:
        def sb(name, shape):
            return held.enter_context(nc.sbuf_tensor(name, shape, F32))
        c_pad = sb("ssd_c_pad", [P, 2, SEQ])
        decay = k.wide[:, 2:4, :].rearrange("p a c -> p (a c)").rearrange("p (t h l) -> p t h l", t=TT, h=H)
        row_decay = k.xT[:, 0:4, :].rearrange("p t (h l) -> p t h l", h=H)
        scores = k.xT[:, 4:8, :].rearrange("p t (h l) -> p t h l", h=H)
        c_dec = sb("ssd_c_dec", [P, TT, H, P])
        dt = sb("ssd_dt", [P, TT * H])
        da = sb("ssd_da", [P, TT * H])
        t1 = sb("ssd_t1", [P, TT * H])
        t2 = sb("ssd_t2", [P, TT * H])
        t3 = sb("ssd_t3", [P, TT * H])
        ea = sb("ssd_ea", [P, H])
        cs = sb("ssd_cs", [P, TT * H])
        to_end = sb("ssd_to_end", [P, TT * H])
        bT = sb("ssd_bT", [P, TT, P])
        xdt = sb("ssd_xdt", [P, TT, H, 64])
        xde = sb("ssd_xde", [P, TT, H, 64])
        state = sb("ssd_state", [P, TT, H, 64])
        y = sb("ssd_y", [P, 2, SEQ])
        v4 = lambda t: t[:, :].rearrange("p (t h) -> p t h", h=H)
        with stage(nc, "dve_done", "small_turned", "dt_abs", "dt_exp", "a_exp", "da_ready",
                   "sums", "cs_out", "diffs", "exps", "row_exps", "turned", "xdt_ready", "c_ready", "gram",
                   "scores_ready", "state_sum", "state_ready", "y_sum", "gated", "squared", "norm_sum", "norm_var",
                   "norm_dev") as (block, s):
            @block.scalar
            def _(act):
                nc.scalar.activation(ea[:, :], k.vec[:, VEC["a_log"]:VEC["a_log"] + H], ACT.Exp).then_inc(s["a_exp"], 1)
                act.wait_ge(s["dt_abs"], 1)
                nc.scalar.activation(dt[:, :], t3[:, :], ACT.Exp, scale=-1.0).then_inc(s["dt_exp"], 1)
                act.wait_ge(s["sums"], 1 + TT)
                for t in range(TT):
                    nc.scalar.activation(row_decay[:, t, :, :].rearrange("p h l -> p (h l)"), k.bank[t][:, :],
                                         ACT.Exp).then_inc(s["row_exps"], 1)
                act.wait_ge(s["diffs"], 1)
                nc.scalar.activation(to_end[:, :], to_end[:, :], ACT.Exp).then_inc(s["exps"], 1)
                act.wait_ge(s["diffs"], 2)
                nc.scalar.activation(decay, decay, ACT.Exp).then_inc(s["exps"], 1)
                for g in range(2):
                    act.wait_ge(s["gated"], g + 1)
                    nc.scalar.activation(k.xT[:, g, :], y[:, g, :], ACT.Square).then_inc(s["squared"], 1)
                for g in range(2):
                    act.wait_ge(s["norm_var"], g + 1)
                    nc.scalar.activation(k.xT[:, 2 + g, :], k.xT[:, 2 + g, :], ACT.Sqrt).then_inc(s["norm_dev"], 1)

            @block.vector
            def _(dve):
                step = in_order(dve, s["dve_done"])
                dve.wait_ge(s["small_turned"], 1)
                step(nc.vector.tensor_copy(k.smallT[:, :, :], k.bank[5][:, 0:TT * 16].rearrange("p (t c) -> p t c", c=16)))
                step(nc.vector.tensor_tensor(v4(t1), k.smallT[:, :, 0:H],
                                             k.vec[:, VEC["dt_bias"]:VEC["dt_bias"] + H].unsqueeze(1).to_broadcast([P, TT, H]),
                                             ALU.add))
                nc.vector.scalar_tensor_tensor(out=t3[:, :], in0=t1[:, :], scalar=-1.0, in1=t1[:, :],
                                               op0=ALU.mult, op1=ALU.max).then_inc(s["dt_abs"], 1)
                dve.wait_ge(s["dt_exp"], 1)
                log1p(nc, step, dt[:, :], t2[:, :], t3[:, :], da[:, :])
                step(nc.vector.scalar_tensor_tensor(out=dt[:, :], in0=t1[:, :], scalar=0.0, in1=dt[:, :],
                                                    op0=ALU.max, op1=ALU.add))
                dve.wait_ge(s["a_exp"], 1)
                nc.vector.scalar_tensor_tensor(out=v4(da), in0=v4(dt), scalar=-1.0,
                                               in1=ea[:, :].unsqueeze(1).to_broadcast([P, TT, H]),
                                               op0=ALU.mult, op1=ALU.mult).then_inc(s["da_ready"], 1)
                dve.wait_ge(s["sums"], 1)
                step(nc.vector.tensor_copy(cs[:, :], k.bank[4][:, 0:TT * H]))
                dve.wait_ge(s["sums"], 1 + TT)
                for t in range(TT):
                    dve.wait_ge(s["row_exps"], t + 1)
                    last = nc.vector.tensor_tensor(v4(to_end)[:, t, :],
                                                   k.bank[t][:, :].rearrange("p (h l) -> p h l", h=H)[:, :, P - 1],
                                                   v4(cs)[:, t, :], ALU.subtract)
                last.then_inc(s["diffs"], 1)
                for t in range(TT):
                    for h in range(H):
                        last = nc.vector.tensor_scalar(decay[:, t, h, :], k.bank[t][:, h * P:(h + 1) * P],
                                                       cs[:, t * H + h:t * H + h + 1], 0.0, ALU.subtract, ALU.min)
                last.then_inc(s["diffs"], 1)
                dve.wait_ge(s["exps"], 2)
                step(nc.vector.tensor_tensor(decay.rearrange("p t h l -> p (t h) l"), decay.rearrange("p t h l -> p (t h) l"),
                                             k.upper[:, :].unsqueeze(1).to_broadcast([P, TT * H, P]), ALU.mult))
                step(nc.vector.memset(c_pad[:, :, :], 0.0))
                step(nc.vector.tensor_copy(c_pad[0:64, 0, :], xbc[0:64, 3, :]))
                nc.vector.tensor_copy(c_pad[64:128, 1, :], xbc[64:128, 3, :]).then_inc(s["c_ready"], 1)
                dve.wait_ge(s["c_ready"], 1)
                dve.wait_ge(s["row_exps"], TT)
                for t in range(TT):
                    for g in range(2):
                        last = nc.vector.tensor_tensor(
                            c_dec[:, t, 2 * g:2 * g + 2, :], row_decay[:, t, 2 * g:2 * g + 2, :],
                            c_pad[:, g, t * P:(t + 1) * P].unsqueeze(1).to_broadcast([P, 2, P]), ALU.mult)
                last.then_inc(s["c_ready"], 1)
                dve.wait_ge(s["turned"], 3)
                step(nc.vector.tensor_copy(bT[:, :, :], k.bank[7][:, :].rearrange("p (t n) -> p t n", t=TT)))
                for i in range(2):
                    for t in range(TT):
                        last = nc.vector.tensor_tensor(
                            xdt[:, t, 2 * i:2 * i + 2, :], k.bank[5 + i][:, t * P:(t + 1) * P].rearrange("p (h q) -> p h q", h=2),
                            v4(dt)[:, t, 2 * i:2 * i + 2].unsqueeze(2).to_broadcast([P, 2, 64]), ALU.mult)
                step(last)
                last = nc.vector.tensor_tensor(xde[:, :, :, :].rearrange("p t h q -> p (t h) q"),
                                               xdt[:, :, :, :].rearrange("p t h q -> p (t h) q"),
                                               to_end[:, :].unsqueeze(2).to_broadcast([P, TT * H, 64]), ALU.mult)
                last.then_inc(s["xdt_ready"], 1)
                for t in range(TT):
                    dve.wait_ge(s["gram"], t + 1)
                    for g in range(2):
                        last = nc.vector.tensor_tensor(
                            scores[:, t, 2 * g:2 * g + 2, :], decay[:, t, 2 * g:2 * g + 2, :],
                            k.bank[t][:, g * P:(g + 1) * P].unsqueeze(1).to_broadcast([P, 2, P]), ALU.mult)
                    last.then_inc(s["scores_ready"], 1)
                for t in range(TT - 1):
                    dve.wait_ge(s["state_sum"], t + 1)
                    new = k.bank[7][:, 0:256].rearrange("p (h q) -> p h q", h=H)
                    if t == 0:
                        nc.vector.tensor_copy(state[:, 1, :, :], new).then_inc(s["state_ready"], 1)
                        dve.wait_ge(s["state_ready"], 1)
                        continue
                    step(nc.vector.tensor_tensor(state[:, t + 1, :, :], state[:, t, :, :],
                                                 row_decay[:, t, :, P - 1].unsqueeze(2).to_broadcast([P, H, 64]), ALU.mult))
                    nc.vector.tensor_tensor(state[:, t + 1, :, :], state[:, t + 1, :, :], new, ALU.add).then_inc(s["state_ready"], 1)
                    dve.wait_ge(s["state_ready"], t + 1)
                dve.wait_ge(s["y_sum"], TT)
                for g in range(2):
                    step(nc.vector.scalar_tensor_tensor(out=y[:, g, :], in0=xbc[:, g, :],
                                                        scalar=k.vec[:, VEC["ssm_d"] + g:VEC["ssm_d"] + g + 1],
                                                        in1=k.bank[5 + g][:, :], op0=ALU.mult, op1=ALU.add))
                    nc.vector.tensor_tensor(y[:, g, :], y[:, g, :], sz[:, g, :], ALU.mult).then_inc(s["gated"], 1)
                for g in range(2):
                    dve.wait_ge(s["norm_sum"], g + 1)
                    nc.vector.tensor_scalar(k.xT[:, 2 + g, :], k.bank[g][:, :], 1.0 / P, EPS, ALU.mult, ALU.add).then_inc(s["norm_var"], 1)
                for g in range(2):
                    dve.wait_ge(s["norm_dev"], g + 1)
                    step(nc.vector.reciprocal(k.xT[:, 2 + g, :], k.xT[:, 2 + g, :]))
                    step(nc.vector.scalar_tensor_tensor(out=k.mixed[:, g, :], in0=y[:, g, :],
                                                        scalar=k.vec[:, VEC["ssm_norm"] + g:VEC["ssm_norm"] + g + 1],
                                                        in1=k.xT[:, 2 + g, :], op0=ALU.mult, op1=ALU.mult))

            @block.tensor
            def _(pe):
                for t in range(TT):
                    last = nc.tensor.transpose(k.bank[5][:, t * 16:(t + 1) * 16],
                                               k.cols[0:16, T_SMALL, LEAD + t * P:LEAD + (t + 1) * P], k.ident[0:16, 0:16])
                last.then_inc(s["small_turned"], 1)
                pe.wait_ge(s["da_ready"], 1)
                nc.tensor.matmul(k.bank[4][:, 0:TT * H], k.upper[:, :], da[:, :], start=True, stop=True).then_inc(s["sums"], 1)
                for t in range(TT):
                    for h in range(H):
                        last = nc.tensor.matmul(k.bank[t][:, h * P:(h + 1) * P],
                                                da[:, t * H + h:t * H + h + 1].to_broadcast([P, P]),
                                                k.upper[:, :], start=True, stop=True)
                    last.then_inc(s["sums"], 1)
                for i in range(3):
                    for t in range(TT):
                        last = nc.tensor.transpose(k.bank[5 + i][:, t * P:(t + 1) * P], xbc[:, i, t * P:(t + 1) * P], k.ident[:, :])
                    last.then_inc(s["turned"], 1)
                pe.wait_ge(s["c_ready"], 1)
                pe.wait_ge(s["row_exps"], TT)
                pe.wait_ge(s["diffs"], 2)
                for t in range(TT):
                    nc.tensor.matmul(k.bank[t][:, 0:256], xbc[:, 2, t * P:(t + 1) * P],
                                     c_pad[:, :, t * P:(t + 1) * P], start=True, stop=True).then_inc(s["gram"], 1)
                pe.wait_ge(s["c_ready"], 2)
                pe.wait_ge(s["xdt_ready"], 1)
                for t in range(TT):
                    if t < TT - 1:
                        if t:
                            pe.wait_ge(s["state_ready"], t)
                        nc.tensor.matmul(k.bank[7][:, 0:256], bT[:, t, :], xde[:, t, :, :].rearrange("p h q -> p (h q)"),
                                         start=True, stop=True).then_inc(s["state_sum"], 1)
                    pe.wait_ge(s["scores_ready"], t + 1)
                    if t:
                        pe.wait_ge(s["state_ready"], t)
                    for h in range(H):
                        r = 64 * (h % 2)
                        o = k.bank[5 + h // 2][r:r + 64, t * P:(t + 1) * P]
                        last = nc.tensor.matmul(o, xdt[:, t, h, :], scores[:, t, h, :], start=True, stop=(t == 0))
                        if t:
                            last = nc.tensor.matmul(o, state[:, t, h, :], c_dec[:, t, h, :], start=False, stop=True)
                    last.then_inc(s["y_sum"], 1)
                for g in range(2):
                    pe.wait_ge(s["squared"], g + 1)
                    nc.tensor.matmul(k.bank[g][:, :], k.ones[:, :], k.xT[:, g, :], start=True, stop=True).then_inc(s["norm_sum"], 1)


class MixersBeside:
    signals = ("lru_dve_done", "x_ready", "gates_sum", "lam_abs", "lam_exp", "sigmoids", "rate_ready", "a_ready",
               "tanhs", "u_sq", "root", "gelu_done", "conv_done", "silu_done")
    CONV_AFTER = (12, 13, 15, 16)
    products_after = 3
    BANK = SLOTS

    def __init__(self, nc, k, held, xbc, silu_z):
        def sb(name, shape):
            return held.enter_context(nc.sbuf_tensor(name, shape, F32))
        self.xbc, self.silu_z = xbc, silu_z
        self.nc, self.k, self.step = nc, k, None
        self.xr, self.rate, self.gate_i, self.a = (k.wide[:, n, :].rearrange("p (i t) -> p i t", t=SEQ) for n in range(4))
        self.th, self.den, self.gel, self.scan = (k.xT[:, 2 * n:2 * n + 2, :] for n in range(4))
        self.x_pad = sb("lru_x_pad", [P, 2, 2, SEQ])
        self.lam, self.l1, self.l2, self.l3, self.l4 = (sb(f"lru_{n}", [P, 2]) for n in ("lam", "l1", "l2", "l3", "l4"))

    def tensor(self, pe, s):
        nc, k = self.nc, self.k
        for i in range(2):
            pe.wait_ge(s["x_ready"], i + 1)
            for n in range(2):
                for half in range(2):
                    last = nc.tensor.matmul(k.bank[self.BANK + 2 * i + n][64 * half:64 * half + 64, :],
                                            k.lru_w[:, n, i, :], self.x_pad[:, i, half, :], start=True, stop=True)
            last.then_inc(s["gates_sum"], 1)

    def scalar(self, act, s, tile):
        nc, k = self.nc, self.k
        if tile == 9:
            act.wait_ge(s["lam_abs"], 1)
            nc.scalar.activation(self.l1[:, :], self.l4[:, :], ACT.Exp, scale=-1.0).then_inc(s["lam_exp"], 1)
        if tile in (12, 13):
            i = tile - 12
            act.wait_ge(s["gates_sum"], i + 1)
            for n, (dst, b) in enumerate(((self.rate, "lru_ba"), (self.gate_i, "lru_bi"))):
                nc.scalar.activation(dst[:, i, :], k.bank[self.BANK + 2 * i + n][:, :], ACT.Sigmoid,
                                     bias=k.vec[:, VEC[b] + i:VEC[b] + i + 1]).then_inc(s["sigmoids"], 1)
        if tile == 15:
            act.wait_ge(s["rate_ready"], 2)
            nc.scalar.activation(self.a, self.rate, ACT.Exp).then_inc(s["a_ready"], 1)
        if tile == 16:
            nc.scalar.activation(self.th, self.rate, ACT.Tanh).then_inc(s["tanhs"], 1)
        if tile == 17:
            act.wait_ge(s["act_out"], 4)
            act.wait_ge(s["dve_out"], 4)
            nc.scalar.activation(self.gel, k.cols[:, T_GATE:T_GATE + 2, LEAD:LEAD + SEQ], ACT.Gelu_apprx_tanh).then_inc(s["gelu_done"], 1)
        if tile == 18:
            act.wait_ge(s["conv_done"], 4)
            nc.scalar.activation(self.xbc, self.xbc, ACT.Silu).then_inc(s["silu_done"], 1)
            act.wait_ge(s["act_out"], 2 + 3)
            act.wait_ge(s["dve_out"], 2 + 3)
            nc.scalar.activation(self.silu_z, k.cols[:, T_Z:T_Z + 2, LEAD:LEAD + SEQ], ACT.Silu).then_inc(s["silu_done"], 1)
        if tile == 19:
            act.wait_ge(s["u_sq"], 1)
            nc.scalar.activation(self.den, self.den, ACT.Sqrt).then_inc(s["root"], 1)

    def vector(self, dve, s, tile):
        nc, k = self.nc, self.k
        if tile == 0:
            self.step = in_order(dve, s["lru_dve_done"])
        step, x_pad, xr, gate_i, den = self.step, self.x_pad, self.xr, self.gate_i, self.den
        raw = k.vec[:, VEC["lru_lam"]:VEC["lru_lam"] + 2]
        if tile == 4:
            step(nc.vector.memset(x_pad[:, :, :, :], 0.0))
        if tile in (5, 6):
            i = tile - 5
            dve.wait_ge(s["act_out"], 4)
            dve.wait_ge(s["dve_out"], 4)
            conv(nc, k, step, xr[:, i, :], T_XR + i, VEC["lru_cw"] + 4 * i, VEC["lru_cb"] + i)
        if tile == 7:
            for i in range(2):
                step(nc.vector.tensor_copy(x_pad[0:64, i, 0, :], xr[0:64, i, :]))
                step(nc.vector.tensor_copy(x_pad[64:128, i, 1, :], xr[64:128, i, :]))
                dve.sem_inc(s["x_ready"], 1)
        if tile in self.CONV_AFTER:
            i = self.CONV_AFTER.index(tile)
            dve.wait_ge(s["act_out"], 2 + 5)
            dve.wait_ge(s["dve_out"], 2 + 5)
            conv(nc, k, step, self.xbc[:, i, :], T_X + i, VEC["ssm_cw"] + 4 * i, VEC["ssm_cb"] + i)
            dve.sem_inc(s["conv_done"], 1)
        if tile == 8:
            nc.vector.scalar_tensor_tensor(out=self.l4[:, :], in0=raw, scalar=-1.0, in1=raw, op0=ALU.mult, op1=ALU.max).then_inc(s["lam_abs"], 1)
        if tile == 10:
            dve.wait_ge(s["lam_exp"], 1)
            log1p(nc, step, self.l1[:, :], self.l2[:, :], self.l3[:, :], self.l4[:, :])
        if tile == 11:
            step(nc.vector.tensor_scalar(self.l2[:, :], raw, -1.0, 0.0, ALU.mult, ALU.max))
            step(nc.vector.tensor_tensor(self.l1[:, :], self.l1[:, :], self.l2[:, :], ALU.add))
            step(nc.vector.tensor_scalar(self.lam[:, :], self.l1[:, :], -8.0, None, ALU.mult))
        if tile == 14:
            dve.wait_ge(s["sigmoids"], 4)
            for i in range(2):
                nc.vector.tensor_scalar(self.rate[:, i, :], self.rate[:, i, :], self.lam[:, i:i + 1], None, ALU.mult).then_inc(s["rate_ready"], 1)
            step(nc.vector.tensor_tensor(gate_i, gate_i, xr, ALU.mult))
        if tile == 17:
            dve.wait_ge(s["tanhs"], 1)
            step(nc.vector.tensor_scalar(den, self.th, -1.0, 1.0, ALU.mult, ALU.add))
            step(nc.vector.reciprocal(den, den))
        if tile == 18:
            step(nc.vector.scalar_tensor_tensor(out=den, in0=self.th, scalar=-2.0, in1=den, op0=ALU.mult, op1=ALU.mult))
            nc.vector.tensor_scalar(den, den, 1e-34, None, ALU.max).then_inc(s["u_sq"], 1)
        if tile == 20:
            dve.wait_ge(s["root"], 1)
            step(nc.vector.tensor_tensor(gate_i, gate_i, den, ALU.mult))
        if tile in (20, 21):
            i = tile - 20
            dve.wait_ge(s["a_ready"], 1)
            step(nc.vector.tensor_tensor_scan(out=self.scan[:, i, :], data0=self.a[:, i, :], data1=gate_i[:, i, :],
                                              initial=0.0, op0=ALU.mult, op1=ALU.add))
        if tile == 22:
            dve.wait_ge(s["gelu_done"], 1)
            step(nc.vector.tensor_tensor(k.mixed[:, 2:4, :], self.scan, self.gel, ALU.mult))


DECAY = math.exp(-0.5)
CH = 32
NCH = SEQ // CH


def rwkv_prepare(nc, k, r):
    pair = lambda ap: ap.rearrange("p i t -> p (i t)")
    mix = r.mix
    slot = lambda i: k.cols[:, i:i + 2, LEAD:LEAD + SEQ]
    vec = lambda name, i: k.vec[:, VEC[name] + i:VEC[name] + i + 1]
    shifted = k.cols[:, T_R:T_R + 8, LEAD - 1:LEAD - 1 + SEQ]
    now = k.cols[:, T_R:T_R + 8, LEAD:LEAD + SEQ]
    diff = k.cols[:, 0:8, LEAD:LEAD + SEQ]
    sig_w, a, bonus, g = k.xT[:, 6:8, :], k.xT[:, 2:4, :], k.xT[:, 0:2, :], k.xT[:, 4:6, :]
    total, inv, prev, tmp, kk = slot(0), slot(2), slot(4), slot(6), slot(8)
    pdec = slot(10)
    with stage(nc, "dve_done", "mixed_in", "padded", "lora_in", "lora_out", "gates", "kk_ready", "kk_sq", "kk_sum",
               "kk_var", "kk_dev", "scanned", "exps", "rk_ready", "rk_sum", "zeroed", "operands", "spread") as (block, s):
        @block.gpsimd
        def _(pool):
            nc.gpsimd.memset(r.lpad[:, :, :], 0.0).then_inc(s["zeroed"], 1)
            nc.gpsimd.memset(r.b_pad[:, :, :, :].rearrange("p i n t -> p (i n t)"), 0.0).then_inc(s["zeroed"], 1)
            nc.gpsimd.memset(r.a_pad[:, :, :, :].rearrange("p i n t -> p (i n t)"), 0.0).then_inc(s["zeroed"], 1)

        @block.scalar
        def _(act):
            act.wait_ge(s["padded"], 1)
            nc.scalar.activation(r.lpad[0:64, 0, :], mix[0:64, 6, :], ACT.Tanh).then_inc(s["lora_in"], 1)
            nc.scalar.activation(mix[:, 7, :], mix[:, 7, :], ACT.Sigmoid).then_inc(s["lora_in"], 1)
            for i in range(2):
                act.wait_ge(s["lora_out"], 3 * i + 1)
                nc.scalar.activation(sig_w[:, i, :], k.bank[i][:, :], ACT.Sigmoid, bias=vec("w0", i)).then_inc(s["gates"], 1)
                act.wait_ge(s["lora_out"], 3 * i + 2)
                nc.scalar.activation(a[:, i, :], k.bank[2 + i][:, :], ACT.Sigmoid, bias=vec("a0", i)).then_inc(s["gates"], 1)
                act.wait_ge(s["lora_out"], 3 * i + 3)
                nc.scalar.copy(g[:, i, :], k.bank[4 + i][:, :]).then_inc(s["gates"], 1)
            act.wait_ge(s["mixed_in"], 1)
            for i in range(2):
                nc.scalar.activation(kk[:, i, :], mix[:, 2 + i, :], ACT.Copy, scale=vec("kk", i)).then_inc(s["kk_ready"], 1)
            act.wait_ge(s["kk_ready"], 2)
            nc.scalar.activation(tmp, kk, ACT.Square).then_inc(s["kk_sq"], 1)
            act.wait_ge(s["scanned"], 1)
            nc.scalar.activation(pdec, total, ACT.Exp, scale=-DECAY).then_inc(s["exps"], 1)
            nc.scalar.activation(inv, total, ACT.Exp, scale=DECAY).then_inc(s["exps"], 1)
            nc.scalar.activation(prev, prev, ACT.Exp, scale=-DECAY).then_inc(s["exps"], 1)
            act.wait_ge(s["kk_var"], 2)
            nc.scalar.activation(tmp, tmp, ACT.Sqrt).then_inc(s["kk_dev"], 1)
            act.wait_ge(s["zeroed"], 3)
            for n, (pad, at, src) in enumerate(((r.b_pad, 0, r.beta), (r.a_pad, 0, r.alpha), (r.a_pad, 2, r.rho))):
                act.wait_ge(s["operands"], n + 1)
                for i in range(2):
                    for e in range(2):
                        q = slice(64 * e, 64 * e + 64)
                        nc.scalar.copy(pad[q, i, at + e, :], src[q, i, :]).then_inc(s["spread"], 1)

        @block.vector
        def _(dve):
            step = in_order(dve, s["dve_done"])
            step(nc.vector.tensor_tensor(diff, shifted, now, ALU.subtract))
            for i in (6, 7, 2, 3, 0, 1, 4, 5):
                step(nc.vector.scalar_tensor_tensor(out=mix[:, i, :], in0=diff[:, i, :], scalar=vec("mu", i),
                                                    in1=now[:, i, :], op0=ALU.mult, op1=ALU.add))
                if i == 3:
                    dve.sem_inc(s["mixed_in"], 1)
                if i == 7:
                    dve.wait_ge(s["zeroed"], 1)
                    nc.vector.tensor_copy(r.lpad[64:128, 1, :], mix[64:128, 6, :]).then_inc(s["padded"], 1)
                    dve.wait_ge(s["padded"], 1)
            dve.wait_ge(s["kk_ready"], 2)
            dve.wait_ge(s["gates"], 6)
            for i in range(2):
                step(nc.vector.tensor_tensor_scan(out=total[:, i, :], data0=k.reset[:, :], data1=sig_w[:, i, :],
                                                  initial=0.0, op0=ALU.mult, op1=ALU.add))
            nc.vector.tensor_tensor(prev, total, sig_w, ALU.subtract).then_inc(s["scanned"], 1)
            step(nc.vector.tensor_scalar(k.stat[:, 16:18], k.vec[:, VEC["ka"]:VEC["ka"] + 2], -1.0, 1.0, ALU.mult, ALU.add))
            for i in range(2):
                step(nc.vector.tensor_scalar(bonus[:, i, :], a[:, i, :], vec("ka", i), k.stat[:, 16 + i:17 + i], ALU.mult, ALU.add))
            step(nc.vector.tensor_tensor(mix[:, 2:4, :], mix[:, 2:4, :], bonus, ALU.mult))
            for i in range(2):
                dve.wait_ge(s["kk_sum"], i + 1)
                nc.vector.tensor_scalar(tmp[:, i, :], k.bank[6 + i][:, :], 1e-30, None, ALU.max).then_inc(s["kk_var"], 1)
            dve.wait_ge(s["kk_dev"], 1)
            step(nc.vector.tensor_scalar(tmp, tmp, 1e-12, None, ALU.max))
            step(nc.vector.reciprocal(tmp, tmp))
            step(nc.vector.tensor_tensor(kk, kk, tmp, ALU.mult))
            for i in range(2):
                nc.vector.scalar_tensor_tensor(out=tmp[:, i, :], in0=mix[:, i, :], scalar=vec("rk", i),
                                               in1=mix[:, 2 + i, :], op0=ALU.mult, op1=ALU.mult).then_inc(s["rk_ready"], 1)
            dve.wait_ge(s["exps"], 3)
            step(nc.vector.tensor_tensor(a, a, kk, ALU.mult))
            step(nc.vector.tensor_tensor(r.beta, a, inv, ALU.mult))
            dve.sem_inc(s["operands"], 1)
            step(nc.vector.tensor_tensor(r.alpha, kk, prev, ALU.mult))
            dve.sem_inc(s["operands"], 1)
            dve.wait_ge(s["rk_ready"], 2)
            step(nc.vector.tensor_tensor(r.rho, mix[:, 0:2, :], pdec, ALU.mult))
            dve.sem_inc(s["operands"], 1)
            step(nc.vector.tensor_tensor(r.kappa, mix[:, 2:4, :], inv, ALU.mult))
            step(nc.vector.tensor_copy(r.p_end[:, :, :], pdec.rearrange("p i (c w) -> p i c w", w=CH)[:, :, :, CH - 1]))
            for i in range(2):
                dve.wait_ge(s["rk_sum"], i + 1)
                step(nc.vector.tensor_tensor(bonus[:, i, :], k.bank[i][:, :], mix[:, 4 + i, :], ALU.mult))

        @block.tensor
        def _(pe):
            pe.wait_ge(s["lora_in"], 2)
            for i in range(2):
                for n, rhs in ((0, r.lpad[:, 0, :]), (1, r.lpad[:, 1, :]), (2, mix[:, 7, :])):
                    w = k.lora[:, (n // 2) * 256 + i * P:(n // 2) * 256 + (i + 1) * P]
                    nc.tensor.matmul(k.bank[2 * n + i][:, :], w, rhs, start=True, stop=True).then_inc(s["lora_out"], 1)
            pe.wait_ge(s["kk_sq"], 1)
            for i in range(2):
                nc.tensor.matmul(k.bank[6 + i][:, :], k.same[64][:, :], tmp[:, i, :], start=True, stop=True).then_inc(s["kk_sum"], 1)
            pe.wait_ge(s["rk_ready"], 2)
            for i in range(2):
                nc.tensor.matmul(k.bank[i][:, :], k.same[64][:, :], tmp[:, i, :], start=True, stop=True).then_inc(s["rk_sum"], 1)


def rwkv_chunks(nc, k, r):
    m = [r.m[:, i, :, :] for i in range(11)]
    N, NT, A16, A32, B, C, D, N2, N2T, INT, IN2 = m
    IN4, XT, T, Q, W, T2, Q2, Q3 = m[8], m[0], m[7], m[1], m[9], m[10], m[8], m[7]
    four = lambda b: k.bank[b][:, :].rearrange("p (h t) -> p h t", h=4)
    two = lambda b, at: k.bank[b][:, at:at + 256].rearrange("p (h t) -> p h t", h=2)
    bc = lambda mask, n: mask.unsqueeze(1).to_broadcast([P, n, P])
    ident4 = bc(k.ident[:, :], 4)
    PE_STEPS = ("turn", "gram", "n2", "bv", "n4", "tq", "w", "tq2", "w2", "q3", "ut", "local")
    DVE_STEPS = ("n", "masks", "n2", "in4", "t", "tq2", "q3", "rgh")
    ACT_STEPS = ("turn", "n2t", "bv", "xt", "q", "w", "w2", "u", "y")
    POOL_STEPS = ("beta_v", "u")

    def after(engine, sem, steps, name, t):
        engine.wait_ge(sem, t * len(steps) + steps.index(name) + 1)

    with stage(nc, "masked", "zeroed", "product", "dve_kept", "act_kept", "pool_kept", "dve_done", "act_done") as (block, s):
        pe_did = lambda e, name, t: after(e, s["product"], PE_STEPS, name, t)
        dve_did = lambda e, name, t: after(e, s["dve_kept"], DVE_STEPS, name, t)
        act_did = lambda e, name, t: after(e, s["act_kept"], ACT_STEPS, name, t)
        pool_did = lambda e, name, t: after(e, s["pool_kept"], POOL_STEPS, name, t)

        @block.tensor
        def _(pe):
            mm = nc.tensor.matmul
            for t in range(TT):
                c = slice(t * P, (t + 1) * P)
                if t:
                    act_did(pe, "turn", t - 1)
                for n, src in enumerate((r.alpha, r.beta, r.kappa, r.mix[:, 4:6, :])):
                    for i in range(2):
                        last = nc.tensor.transpose(k.bank[6 + n // 2][:, (n % 2 * 2 + i) * P:(n % 2 * 2 + i + 1) * P],
                                                   src[:, i, c], k.ident[:, :])
                last.then_inc(s["product"], 1)
                if t:
                    dve_did(pe, "rgh", t - 1)
                    act_did(pe, "y", t - 1)
                for i in range(2):
                    mm(k.bank[0][:, i * 256:(i + 1) * 256], r.alpha[:, i, c], r.b_pad[:, i, :, c], start=True, stop=True)
                    mm(k.bank[1 + i][:, :], r.beta[:, i, c], r.a_pad[:, i, :, c], start=True, stop=True)
                    last = mm(k.bank[3 + i][:, :], r.kappa[:, i, c], r.a_pad[:, i, :, c], start=True, stop=True)
                last.then_inc(s["product"], 1)
                dve_did(pe, "n", t)
                for h in range(4):
                    o = slice(h * P, (h + 1) * P)
                    mm(k.bank[0][:, o], NT[:, h, :], N[:, h, :], start=True, stop=True)
                    last = mm(k.bank[5][:, o], N[:, h, :], NT[:, h, :], start=True, stop=True)
                last.then_inc(s["product"], 1)
                dve_did(pe, "masks", t)
                act_did(pe, "turn", t)
                for h in range(4):
                    last = mm(k.bank[3][:, h * 64:(h + 1) * 64], B[:, h, :], r.vT[:, h, :], start=True, stop=True)
                last.then_inc(s["product"], 1)
                dve_did(pe, "n2", t)
                act_did(pe, "n2t", t)
                for h in range(4):
                    o = slice(h * P, (h + 1) * P)
                    mm(k.bank[1][:, o], N2T[:, h, :], N2[:, h, :], start=True, stop=True)
                    last = mm(k.bank[2][:, o], IN2[:, h, :], INT[:, h, :], start=True, stop=True)
                last.then_inc(s["product"], 1)
                dve_did(pe, "in4", t)
                act_did(pe, "xt", t)
                for h in range(4):
                    o = slice(h * P, (h + 1) * P)
                    mm(k.bank[0][:, o], XT[:, h, :], IN4[:, h, :], start=True, stop=True)
                    last = mm(k.bank[5][:, o], IN4[:, h, :], XT[:, h, :], start=True, stop=True)
                last.then_inc(s["product"], 1)
                dve_did(pe, "t", t)
                for h in range(4):
                    last = mm(k.bank[1][:, h * P:(h + 1) * P], A16[:, h, :], T[:, h, :], start=True, stop=True)
                last.then_inc(s["product"], 1)
                act_did(pe, "w", t)
                for h in range(4):
                    o = slice(h * P, (h + 1) * P)
                    mm(k.bank[0][:, o], Q[:, h, :], W[:, h, :], start=True, stop=True)
                    last = mm(k.bank[5][:, o], W[:, h, :], Q[:, h, :], start=True, stop=True)
                last.then_inc(s["product"], 1)
                dve_did(pe, "tq2", t)
                for h in range(4):
                    last = mm(k.bank[2][:, h * P:(h + 1) * P], A32[:, h, :], T2[:, h, :], start=True, stop=True)
                last.then_inc(s["product"], 1)
                act_did(pe, "w2", t)
                for h in range(4):
                    last = mm(k.bank[5][:, h * P:(h + 1) * P], W[:, h, :], Q2[:, h, :], start=True, stop=True)
                last.then_inc(s["product"], 1)
                dve_did(pe, "q3", t)
                act_did(pe, "bv", t)
                for h in range(4):
                    last = mm(k.bank[0][:, h * P:(h + 1) * P], Q3[:, h, :], r.bva[:, h, :], start=True, stop=True)
                last.then_inc(s["product"], 1)
                pool_did(pe, "u", t)
                act_did(pe, "u", t)
                for h in range(4):
                    i, q = h // 2, slice(64 * (h % 2), 64 * (h % 2) + 64)
                    mm(k.bank[1][q, i * P:(i + 1) * P], r.taT[:, h, :], D[:, h, :], start=True, stop=True)
                    mm(k.bank[2][q, i * 256:(i + 1) * 256], r.taT[:, h, :], r.beta_c[:, h, :, :].rearrange("p c d -> p (c d)"), start=True, stop=True)
                    mm(k.bank[3][q, i * 256:(i + 1) * 256], r.kapT[:, h, :], r.v_c[:, h, :, :].rearrange("p c d -> p (c d)"), start=True, stop=False)
                    mm(k.bank[3][q, i * 256:(i + 1) * 256], r.betT[:, h, :], r.u_c[:, h, :, :].rearrange("p c d -> p (c d)"), start=False, stop=True)
                    mm(k.bank[4][q, i * P:(i + 1) * P], r.vT[:, h, :], C[:, h, :], start=True, stop=False)
                    last = mm(k.bank[4][q, i * P:(i + 1) * P], r.uT[:, h, :], D[:, h, :], start=False, stop=True)
                last.then_inc(s["product"], 1)

        @block.vector
        def _(dve):
            step = in_order(dve, s["dve_done"])
            mk = r.masks
            step(nc.vector.scalar_tensor_tensor(out=mk[:, 0, :], in0=k.lower[:, :], scalar=-1.0, in1=k.same[8][:, :], op0=ALU.mult, op1=ALU.mult))
            step(nc.vector.scalar_tensor_tensor(out=mk[:, 1, :], in0=k.strict[:, :], scalar=-1.0, in1=k.same[8][:, :], op0=ALU.mult, op1=ALU.mult))
            step(nc.vector.tensor_tensor(mk[:, 2, :], k.same[16][:, :], k.same[8][:, :], ALU.subtract))
            step(nc.vector.tensor_tensor(mk[:, 2, :], mk[:, 2, :], k.strict[:, :], ALU.mult))
            step(nc.vector.tensor_tensor(mk[:, 3, :], k.same[32][:, :], k.same[16][:, :], ALU.subtract))
            step(nc.vector.tensor_tensor(mk[:, 3, :], mk[:, 3, :], k.strict[:, :], ALU.mult))
            step(nc.vector.tensor_tensor(mk[:, 4, :], k.strict[:, :], k.same[32][:, :], ALU.mult))
            step(nc.vector.tensor_tensor(mk[:, 5, :], k.upper[:, :], k.same[32][:, :], ALU.mult))
            tt = nc.vector.tensor_tensor
            for t in range(TT):
                c = slice(t * P, (t + 1) * P)
                pe_did(dve, "gram", t)
                step(tt(N, four(0), bc(mk[:, 0, :], 4), ALU.mult))
                for i in range(2):
                    last = tt(NT[:, 2 * i:2 * i + 2, :], two(1 + i, 0), bc(mk[:, 1, :], 2), ALU.mult)
                last.then_inc(s["dve_kept"], 1)
                for i in range(2):
                    hh = slice(2 * i, 2 * i + 2)
                    step(tt(A16[:, hh, :], two(1 + i, 0), bc(mk[:, 2, :], 2), ALU.mult))
                    step(tt(A32[:, hh, :], two(1 + i, 0), bc(mk[:, 3, :], 2), ALU.mult))
                    step(tt(D[:, hh, :], two(1 + i, 256), bc(mk[:, 5, :], 2), ALU.mult))
                    step(tt(B[:, hh, :], two(3 + i, 0), bc(mk[:, 4, :], 2), ALU.mult))
                    step(tt(C[:, hh, :], two(3 + i, 256), bc(mk[:, 5, :], 2), ALU.mult))
                dve_did(dve, "n", t)
                tt(INT, NT, ident4, ALU.add).then_inc(s["dve_kept"], 1)
                pe_did(dve, "n2", t)
                step(nc.vector.tensor_copy(N2, four(0)))
                tt(IN2, four(0), ident4, ALU.add).then_inc(s["dve_kept"], 1)
                pe_did(dve, "n4", t)
                tt(IN4, four(1), ident4, ALU.add).then_inc(s["dve_kept"], 1)
                pe_did(dve, "tq", t)
                nc.vector.tensor_copy(T, four(0)).then_inc(s["dve_kept"], 1)
                act_did(dve, "q", t)
                pe_did(dve, "tq2", t)
                step(tt(T2, T, four(0), ALU.subtract))
                tt(Q2, Q, four(5), ALU.subtract).then_inc(s["dve_kept"], 1)
                pe_did(dve, "q3", t)
                dve_did(dve, "tq2", t)
                tt(Q3, Q2, four(5), ALU.subtract).then_inc(s["dve_kept"], 1)
                pe_did(dve, "local", t)
                dve.wait_ge(s["zeroed"], 1)
                for i in range(2):
                    step(tt(r.rho[:, i, c], r.rho[:, i, c], k.bank[1][:, i * P:(i + 1) * P], ALU.subtract))
                for i in range(2):
                    hp = k.bank[3][:, i * 256:(i + 1) * 256].rearrange("p (c v) -> p c v", c=4)
                    gp = k.bank[2][:, i * 256:(i + 1) * 256].rearrange("p (c v) -> p c v", c=4)
                    G = r.G(i, t)
                    H = r.H(i, t)
                    for e in range(2):
                        q = slice(64 * e, 64 * e + 64)
                        step(tt(G[q, :, q], k.ident[q, q].unsqueeze(1).to_broadcast([64, 4, 64]), gp[q, :, :], ALU.subtract))
                        last = tt(H[q, :, q], hp[q, :, :], r.p_end[q, i, 4 * t:4 * t + 4].unsqueeze(2).to_broadcast([64, 4, 64]), ALU.mult)
                        if i == 0 or e == 0:
                            step(last)
                last.then_inc(s["dve_kept"], 1)

        @block.scalar
        def _(act):
            step = in_order(act, s["act_done"])
            cp = nc.scalar.copy
            for t in range(TT):
                c = slice(t * P, (t + 1) * P)
                heads = lambda b, at: k.bank[b][:, at:at + 256].rearrange("p (h d) -> p h d", h=4)
                pe_did(act, "turn", t)
                if t:
                    pe_did(act, "local", t - 1)
                step(cp(r.bva[:, :, 64:128], heads(6, 0)))
                step(cp(r.betT[:, :, :], heads(6, 256)))
                step(cp(r.kapT[:, :, :], heads(7, 0)))
                cp(r.vT[:, :, :], heads(7, 256)).then_inc(s["act_kept"], 1)
                pe_did(act, "n2", t)
                cp(N2T, four(5)).then_inc(s["act_kept"], 1)
                pe_did(act, "bv", t)
                cp(r.bva[:, :, 0:64], heads(3, 0)).then_inc(s["act_kept"], 1)
                pe_did(act, "n4", t)
                cp(XT, four(2)).then_inc(s["act_kept"], 1)
                pe_did(act, "tq", t)
                cp(Q, four(5)).then_inc(s["act_kept"], 1)
                pe_did(act, "w", t)
                cp(W, four(1)).then_inc(s["act_kept"], 1)
                pe_did(act, "w2", t)
                cp(W, four(2)).then_inc(s["act_kept"], 1)
                pe_did(act, "ut", t)
                step(nc.scalar.activation(r.uT[:, :, :], four(0)[:, :, 0:64], ACT.Copy, scale=-1.0))
                cp(r.taT[:, :, :], four(0)[:, :, 64:128]).then_inc(s["act_kept"], 1)
                pe_did(act, "local", t)
                cp(k.mixed[:, 4:6, c], k.bank[4][:, 0:256].rearrange("p (i t) -> p i t", i=2)).then_inc(s["act_kept"], 1)

        @block.gpsimd
        def _(pool):
            rows = k.same[32][:, :].rearrange("p (c w) -> p c w", w=CH)[:, :, 0]

            def spread(dst, src):
                for h in range(4):
                    last = nc.gpsimd.tensor_tensor(dst[:, h, :, :], src[:, h, :].unsqueeze(1).to_broadcast([P, 4, 64]),
                                                   rows.unsqueeze(2).to_broadcast([P, 4, 64]), ALU.mult)
                return last
            nc.gpsimd.memset(k.cols[:, 0:16, LEAD:LEAD + SEQ], 0.0).then_inc(s["zeroed"], 1)
            for t in range(TT):
                act_did(pool, "turn", t)
                spread(r.beta_c, r.betT)
                spread(r.v_c, r.vT).then_inc(s["pool_kept"], 1)
                act_did(pool, "u", t)
                spread(r.u_c, r.uT).then_inc(s["pool_kept"], 1)


def rwkv_carry(nc, k, r):
    y = k.mixed[:, 4:6, :]
    bonus, g = k.xT[:, 0:2, :], k.xT[:, 4:6, :]
    dev, sq = k.wide[:, 2, :].rearrange("p (i t) -> p i t", t=SEQ), k.wide[:, 3, :].rearrange("p (i t) -> p i t", t=SEQ)
    M = k.ring[:, :, :].rearrange("p u c -> p (u c)").rearrange("p (i c v) -> p i c v", i=2, v=P)
    with stage(nc, "dve_done", "carried", "stepped", "y_done", "y_ready", "mean_sum", "dev_ready", "squares", "var_sum",
               "var_ready", "root") as (block, s):
        @block.vector
        def _(dve):
            step = in_order(dve, s["dve_done"])
            for c in range(NCH - 1):
                for i in range(2):
                    H = r.H(i, c // 4)[:, c % 4, :]
                    if c == 0:
                        nc.vector.tensor_copy(M[:, i, 1, :], H).then_inc(s["carried"], 1)
                        continue
                    dve.wait_ge(s["stepped"], 2 * (c - 1) + i + 1)
                    nc.vector.scalar_tensor_tensor(out=M[:, i, c + 1, :], in0=k.bank[2 * i + c % 2][:, 0:P],
                                                   scalar=r.p_end[:, i, c:c + 1], in1=H,
                                                   op0=ALU.mult, op1=ALU.add).then_inc(s["carried"], 1)
            dve.wait_ge(s["y_done"], 1)
            for i in range(2):
                nc.vector.tensor_tensor(y[:, i, CH:SEQ], y[:, i, CH:SEQ], k.bank[4 + i][:, CH:SEQ], ALU.add).then_inc(s["y_ready"], 1)
            for i in range(2):
                dve.wait_ge(s["mean_sum"], i + 1)
                nc.vector.scalar_tensor_tensor(out=dev[:, i, :], in0=k.bank[6 + i][:, :], scalar=-1.0 / 64, in1=y[:, i, :],
                                               op0=ALU.mult, op1=ALU.add).then_inc(s["dev_ready"], 1)
            for i in range(2):
                dve.wait_ge(s["var_sum"], i + 1)
                nc.vector.tensor_scalar(sq[:, i, :], k.bank[i][:, :], 1.0 / 64, GN_EPS, ALU.mult, ALU.add).then_inc(s["var_ready"], 1)
            dve.wait_ge(s["root"], 1)
            step(nc.vector.reciprocal(sq, sq))
            step(nc.vector.tensor_tensor(dev, dev, sq, ALU.mult))
            for i in range(2):
                step(nc.vector.tensor_scalar(dev[:, i, :], dev[:, i, :], k.vec[:, VEC["ln_w"] + i:VEC["ln_w"] + i + 1],
                                             k.vec[:, VEC["ln_b"] + i:VEC["ln_b"] + i + 1], ALU.mult, ALU.add))
            step(nc.vector.tensor_tensor(dev, dev, bonus, ALU.add))
            step(nc.vector.tensor_tensor(y, dev, g, ALU.mult))

        @block.tensor
        def _(pe):
            for c in range(1, NCH):
                for i in range(2):
                    pe.wait_ge(s["carried"], 2 * (c - 1) + i + 1)
                    if c < NCH - 1:
                        nc.tensor.matmul(k.bank[2 * i + c % 2][:, 0:P], r.G(i, c // 4)[:, c % 4, :], M[:, i, c, :],
                                         start=True, stop=True).then_inc(s["stepped"], 1)
                    last = nc.tensor.matmul(k.bank[4 + i][:, c * CH:(c + 1) * CH], M[:, i, c, :],
                                            r.rho[:, i, c * CH:(c + 1) * CH], start=True, stop=True)
            last.then_inc(s["y_done"], 1)
            for i in range(2):
                pe.wait_ge(s["y_ready"], i + 1)
                nc.tensor.matmul(k.bank[6 + i][:, :], k.same[64][:, :], y[:, i, :], start=True, stop=True).then_inc(s["mean_sum"], 1)
            for i in range(2):
                pe.wait_ge(s["squares"], i + 1)
                nc.tensor.matmul(k.bank[i][:, :], k.same[64][:, :], sq[:, i, :], start=True, stop=True).then_inc(s["var_sum"], 1)

        @block.scalar
        def _(act):
            for i in range(2):
                act.wait_ge(s["dev_ready"], i + 1)
                nc.scalar.activation(sq[:, i, :], dev[:, i, :], ACT.Square).then_inc(s["squares"], 1)
            act.wait_ge(s["var_ready"], 2)
            nc.scalar.activation(sq, sq, ACT.Sqrt).then_inc(s["root"], 1)


def rwkv_mixer(nc, k):
    with ExitStack() as held:
        def sb(name, shape):
            return held.enter_context(nc.sbuf_tensor(name, shape, F32))
        r = Named()
        r.mix = k.wide[:, :, :].rearrange("p a c -> p (a c)").rearrange("p (i t) -> p i t", t=SEQ)
        r.rho, r.kappa, r.beta, r.alpha = r.mix[:, 0:2, :], r.mix[:, 2:4, :], k.xT[:, 2:4, :], k.xT[:, 6:8, :]
        r.G = lambda i, t: k.cols[:, 4 * i + t, LEAD:LEAD + SEQ].rearrange("p (c v) -> p c v", v=P)
        r.H = lambda i, t: k.cols[:, 8 + 4 * i + t, LEAD:LEAD + SEQ].rearrange("p (c v) -> p c v", v=P)
        r.a_pad = sb("rw_a_pad", [P, 2, 4, SEQ])
        r.b_pad = sb("rw_b_pad", [P, 2, 2, SEQ])
        r.p_end = sb("rw_p_end", [P, 2, NCH])
        r.masks = sb("rw_masks", [P, 6, P])
        with ExitStack() as first:
            r.lpad = first.enter_context(nc.sbuf_tensor("rw_lpad", [P, 2, SEQ], F32))
            rwkv_prepare(nc, k, r)
        r.m = sb("rw_m", [P, 11, 4, P])
        r.bva = sb("rw_bva", [P, 4, P])
        r.betT = sb("rw_betT", [P, 4, 64])
        r.kapT = sb("rw_kapT", [P, 4, 64])
        r.vT = sb("rw_vT", [P, 4, 64])
        r.uT = sb("rw_uT", [P, 4, 64])
        r.taT = sb("rw_taT", [P, 4, 64])
        r.beta_c = sb("rw_beta_c", [P, 4, 4, 64])
        r.v_c = sb("rw_v_c", [P, 4, 4, 64])
        r.u_c = sb("rw_u_c", [P, 4, 4, 64])
        rwkv_chunks(nc, k, r)
        rwkv_carry(nc, k, r)


NBLK = 32


def attention(nc, k, a):
    gather = {2: (), 4: (0, 0), 5: (0, 1), 6: (1, 0), 7: (1, 1)}
    MLP_FROM = 16
    w1 = a.w1[:, :].rearrange("p (j c) -> p j c", j=32)
    units = [(qt, h, br) for qt in range(TT) for h in range(4) for br in range(2)]
    n = len(units)
    width = lambda u: (units[u][0] + 1) * P
    S, X, PT = 3, 3, 2
    with stage(nc, "dve_done", "pool_done", "bias_ready", "moved", "keys_ready", "values_turned", "values_ready",
               "gate_ready", "scores", "read", "biased", "exps", "inverse", "scaled", "turned", "kept", "summed", "w1_in",
               "blocks_ready") as (block, s):
        @block.sync
        def _(sp):
            sp.dma_start(a.keys[64:P, 0, 1, :], k.cols[0:64, T_KSKW, LEAD:LEAD + SEQ]).then_inc(s["moved"], 16)
            sp.dma_start(a.keys[0:64, 1, 0, :], k.cols[64:P, T_KSKW, LEAD:LEAD + SEQ]).then_inc(s["moved"], 16)
            sp.dma_start(a.w1[:, :], a.w1_dram).then_inc(s["w1_in"], 16)
            sp.dma_start(a.w2[:, :], a.w2_dram).then_inc(s["w1_in"], 16)
            sp.wait_ge(s["w1_in"], 32)
            sp.wait_ge(s["moved"], 32)

        @block.gpsimd
        def _(pool):
            step = in_order(pool, s["pool_done"])
            step(nc.gpsimd.iota(a.dist[:, :], pattern=[[-1, SEQ]], base=384, channel_multiplier=1,
                                allow_small_or_imprecise_dtypes=True))
            for h in range(4):
                step(nc.gpsimd.tensor_scalar(a.alibi[:, h, :], a.dist[:, :], -(2.0 ** (-2.0 * (h + 1))), 0.0, ALU.mult, ALU.add))
                nc.gpsimd.affine_select(out=a.alibi[:, h, :], in_=a.alibi[:, h, :], compare_op=ALU.is_ge, fill=NEG, base=384,
                                        pattern=[[-1, SEQ]], channel_multiplier=1).then_inc(s["bias_ready"], 1)
            pool.wait_ge(s["gate_ready"], 1)
            for u, (qt, h, br) in enumerate(units):
                pool.wait_ge(s["inverse"], u + 1)
                w = a.weights[:, u % X, 0:width(u)]
                nc.gpsimd.tensor_scalar(w, w, a.inv[:, u:u + 1], a.gate[:, qt, 3 * h + 1 + br:3 * h + 2 + br],
                                        ALU.mult, ALU.mult).then_inc(s["scaled"], 1)

        @block.vector
        def _(dve):
            step = in_order(dve, s["dve_done"])
            step(nc.vector.tensor_copy(a.keys[0:64, 0, 0, :], k.cols[0:64, T_KSKW, LEAD:LEAD + SEQ]))
            step(nc.vector.tensor_copy(a.keys[64:P, 1, 1, :], k.cols[64:P, T_KSKW, LEAD:LEAD + SEQ]))
            step(nc.vector.memset(a.keys[64:P, 0, 0, :], 0.0))
            step(nc.vector.memset(a.keys[64:P, 1, 0, :], 0.0))
            step(nc.vector.memset(a.keys[0:64, 0, 1, :], 0.0))
            nc.vector.memset(a.keys[0:64, 1, 1, :], 0.0).then_inc(s["keys_ready"], 1)
            dve.wait_ge(s["values_turned"], 1)
            nc.vector.tensor_copy(a.vT[:, :, :], k.bank[7][:, :].rearrange("p (t c) -> p t c", t=TT)).then_inc(s["values_ready"], 1)
            for u, (qt, h, br) in enumerate(units):
                w = a.weights[:, u % X, 0:width(u)]
                dve.wait_ge(s["scores"], u + 1)
                dve.wait_ge(s["bias_ready"], h + 1)
                if u >= X:
                    dve.wait_ge(s["turned"], u - X + 1)
                nc.vector.scalar_tensor_tensor(out=w, in0=k.bank[u % S][:, 0:width(u)], scalar=0.125,
                                               in1=a.alibi[:, h, (TT - 1 - qt) * P:(TT - 1 - qt) * P + width(u)],
                                               op0=ALU.mult, op1=ALU.add).then_inc(s["read"], 1)
                dve.wait_ge(s["read"], u + 1)
                nc.vector.tensor_reduce(out=a.neg_max[:, u:u + 1], in_=w, axis=AX.X, op=ALU.max, negate=True).then_inc(s["biased"], 1)
                if u >= 1:
                    dve.wait_ge(s["exps"], u)
                    nc.vector.reciprocal(a.inv[:, u - 1:u], a.total[:, u - 1:u]).then_inc(s["inverse"], 1)
                if gather.get(u) == ():
                    step(nc.vector.memset(a.blocks[:, :, :, :].rearrange("p v j n -> p (v j n)"), 0.0))
                elif u in gather:
                    v, half = gather[u]
                    q, at = slice(64 * v, 64 * v + 64), LEAD + 16 * half
                    src = k.cols[q, T_CMP, at:at + 31 * 16].rearrange("p (n j) -> p j n", j=16)
                    pos = k.vec[q, VEC["pos"] + 16 * half:VEC["pos"] + 16 * half + 16].unsqueeze(2).to_broadcast([64, 16, 31])
                    nc.vector.tensor_tensor(a.blocks[q, v, 16 * half:16 * half + 16, 0:31], src, pos, ALU.add).then_inc(s["blocks_ready"], 1)
            dve.wait_ge(s["exps"], n)
            nc.vector.reciprocal(a.inv[:, n - 1:n], a.total[:, n - 1:n]).then_inc(s["inverse"], 1)
            dve.wait_ge(s["summed"], n)
            for i in range(2):
                step(nc.vector.tensor_copy(k.mixed[:, 6 + i, :], k.bank[5 + i][:, :]))

        @block.scalar
        def _(act):
            nc.scalar.activation(a.gate[:, :, :], k.smallT[:, :, 4:16], ACT.Sigmoid).then_inc(s["gate_ready"], 1)
            for i in range(n + 2):
                if i < n:
                    act.wait_ge(s["biased"], i + 1)
                    w = a.weights[:, i % X, 0:width(i)]
                    nc.scalar.activation(w, w, ACT.Exp, bias=a.neg_max[:, i:i + 1],
                                         accum_out=a.total[:, i:i + 1]).then_inc(s["exps"], 1)
                u = i - 2
                if u >= 0:
                    act.wait_ge(s["turned"], u + 1)
                    if u >= PT:
                        act.wait_ge(s["summed"], u - PT + 1)
                    nc.scalar.copy(a.turned[:, u % PT, 0:width(u)], k.bank[3 + u % PT][:, 0:width(u)]).then_inc(s["kept"], 1)

        @block.tensor
        def _(pe):
            for t in range(TT):
                last = nc.tensor.transpose(k.bank[7][:, t * P:(t + 1) * P], k.cols[:, T_VSVW, LEAD + t * P:LEAD + (t + 1) * P], k.ident[:, :])
            last.then_inc(s["values_turned"], 1)
            pe.wait_ge(s["keys_ready"], 1)
            pe.wait_ge(s["moved"], 32)
            pe.wait_ge(s["values_ready"], 1)
            for i in range(n + 3):
                if i < n:
                    qt, h, br = units[i]
                    if i >= S:
                        pe.wait_ge(s["read"], i - S + 1)
                    nc.tensor.matmul(k.bank[i % S][:, 0:width(i)], k.cols[:, T_Q + h // 2, LEAD + qt * P:LEAD + (qt + 1) * P],
                                     a.keys[:, br, h % 2, 0:width(i)], start=True, stop=True).then_inc(s["scores"], 1)
                if i == MLP_FROM:
                    pe.wait_ge(s["blocks_ready"], 4)
                    pe.wait_ge(s["w1_in"], 32)
                if MLP_FROM <= i < n:
                    for at in range(4 * (i - MLP_FROM), 4 * (i - MLP_FROM + 1)):
                        m, j = at // 32, at % 32
                        nc.tensor.matmul(k.bank[7][:, m * 2 * NBLK:(m + 1) * 2 * NBLK], w1[:, j, m * P:(m + 1) * P],
                                         a.blocks[:, :, j, :], start=(j == 0), stop=(j == 31))
                u = i - 2
                if 0 <= u < n:
                    pe.wait_ge(s["scaled"], u + 1)
                    if u >= PT:
                        pe.wait_ge(s["kept"], u - PT + 1)
                    for b in range(units[u][0] + 1):
                        last = nc.tensor.transpose(k.bank[3 + u % PT][:, b * P:(b + 1) * P],
                                                   a.weights[:, u % X, b * P:(b + 1) * P], k.ident[:, :])
                    last.then_inc(s["turned"], 1)
                u = i - 3
                if u >= 0:
                    qt, h, br = units[u]
                    pe.wait_ge(s["kept"], u + 1)
                    o = k.bank[5 + h // 2][64 * (h % 2):64 * (h % 2) + 64, qt * P:(qt + 1) * P]
                    for b in range(qt + 1):
                        last = nc.tensor.matmul(o, a.vT[:, b, br * 64:(br + 1) * 64], a.turned[:, u % PT, b * P:(b + 1) * P],
                                                start=(br == 0 and b == 0), stop=(br == 1 and b == qt))
                    last.then_inc(s["summed"], 1)


def compressed_attention(nc, k, a, w_out):
    H = 4
    with ExitStack() as held:
        def sb(name, shape):
            return held.enter_context(nc.sbuf_tensor(name, shape, F32))
        hidden = sb("cmp_hidden", [P, 2, 2, NBLK])
        kpad = sb("cmp_kpad", [P, 2, NBLK])
        vz = sb("cmp_vz", [P, H, 64])
        dist = sb("cmp_dist", [P, TT, NBLK])
        valid = sb("cmp_valid", [P, TT, NBLK])
        hide = sb("cmp_hide", [P, TT, NBLK])
        w = sb("cmp_w", [P, TT, H, NBLK])
        mx = sb("cmp_mx", [P, TT * H])
        wT = sb("cmp_wT", [P, TT, P])
        flat = w[:, :, :, :].rearrange("p t h n -> p (t h) n")
        w2 = a.w2[:, :].rearrange("p (v m c) -> p v m c", v=2, m=2)
        with stage(nc, "dve_done", "dist_ready", "hidden_ready", "kv_sum", "kv_ready",
                   "scores", "shifted", "exps", "weights_ready", "turned", "kept", "summed", "rows_in") as (block, s):
            @block.sync
            def _(sp):
                for c in range(SLOTS):
                    sp.dma_start(k.ring[:, c, :], w_out(c)).then_inc(s["rows_in"], 16)
                sp.wait_ge(s["rows_in"], 16 * SLOTS)

            @block.gpsimd
            def _(pool):
                nc.gpsimd.iota(dist[:, :, :], pattern=[[P, TT], [-16, NBLK]], base=-31, channel_multiplier=1,
                               allow_small_or_imprecise_dtypes=True).then_inc(s["dist_ready"], 1)

            @block.vector
            def _(dve):
                step = in_order(dve, s["dve_done"])
                dve.wait_ge(s["dist_ready"], 1)
                step(nc.vector.tensor_scalar(valid[:, :, :], dist[:, :, :], 0.0, None, ALU.is_ge))
                step(nc.vector.tensor_scalar(hide[:, :, :], valid[:, :, :], -1.0, -NEG, ALU.add, ALU.mult))
                step(nc.vector.memset(kpad[:, :, :], 0.0))
                step(nc.vector.memset(vz[:, :, :], 0.0))
                dve.wait_ge(s["kv_sum"], 1)
                for e in range(2):
                    step(nc.vector.tensor_copy(kpad[64 * e:64 * e + 64, e, :], k.bank[2][64 * e:64 * e + 64, 0:NBLK]))
                for h in range(H):
                    step(nc.vector.tensor_copy(vz[32 * h:32 * h + 32, h, :], k.bank[3][32 * h:32 * h + 32, 0:64]))
                dve.sem_inc(s["kv_ready"], 1)
                dve.wait_ge(s["scores"], 1)
                step(nc.vector.tensor_scalar(w[:, :, :, :].rearrange("p t h n -> p (t h n)"), k.bank[4][:, :], 0.125, None, ALU.mult))
                for h in range(H):
                    step(nc.vector.scalar_tensor_tensor(out=w[:, :, h, :], in0=dist[:, :, :], scalar=-(2.0 ** (-2.0 * (h + 1))),
                                                        in1=w[:, :, h, :], op0=ALU.mult, op1=ALU.add))
                rows = lambda t: t[:, :, :].unsqueeze(2).to_broadcast([P, TT, H, NBLK])
                step(nc.vector.tensor_tensor(w[:, :, :, :], w[:, :, :, :], rows(hide), ALU.add))
                step(nc.vector.tensor_reduce(out=mx[:, :], in_=flat, axis=AX.X, op=ALU.max))
                nc.vector.tensor_tensor(flat, flat, mx[:, :].unsqueeze(2).to_broadcast([P, TT * H, NBLK]), ALU.subtract).then_inc(s["shifted"], 1)
                dve.wait_ge(s["exps"], 1)
                step(nc.vector.tensor_tensor(w[:, :, :, :], w[:, :, :, :], rows(valid), ALU.mult))
                step(nc.vector.tensor_reduce(out=mx[:, :], in_=flat, axis=AX.X, op=ALU.add))
                step(nc.vector.tensor_scalar(mx[:, :], mx[:, :], 1e-30, None, ALU.max))
                step(nc.vector.reciprocal(mx[:, :], mx[:, :]))
                step(nc.vector.tensor_tensor(mx[:, :].rearrange("p (t h) -> p t h", h=H), mx[:, :].rearrange("p (t h) -> p t h", h=H),
                                             a.gate[:, :, :].rearrange("p t (h b) -> p t h b", b=3)[:, :, :, 0], ALU.mult))
                nc.vector.tensor_tensor(flat, flat, mx[:, :].unsqueeze(2).to_broadcast([P, TT * H, NBLK]), ALU.mult).then_inc(s["weights_ready"], 1)
                dve.wait_ge(s["turned"], 1)
                nc.vector.tensor_copy(wT[:, :, :], k.bank[5][:, :].rearrange("p (t q) -> p t q", t=TT)).then_inc(s["kept"], 1)
                dve.wait_ge(s["summed"], 1)
                for i in range(2):
                    step(nc.vector.tensor_tensor(k.mixed[:, 6 + i, :], k.mixed[:, 6 + i, :], k.bank[6 + i][:, :], ALU.add))

            @block.scalar
            def _(act):
                for m in range(2):
                    nc.scalar.activation(hidden[:, m, :, :].rearrange("p v n -> p (v n)"), k.bank[7][:, m * 2 * NBLK:(m + 1) * 2 * NBLK],
                                         ACT.Gelu_apprx_tanh).then_inc(s["hidden_ready"], 1)
                act.wait_ge(s["shifted"], 1)
                nc.scalar.activation(flat, flat, ACT.Exp).then_inc(s["exps"], 1)

            @block.tensor
            def _(pe):
                pe.wait_ge(s["hidden_ready"], 2)
                for e in range(2):
                    for m in range(2):
                        nc.tensor.matmul(k.bank[2][64 * e:64 * e + 64, 0:NBLK], w2[:, 0, m, :], hidden[:, m, 0, :], start=(m == 0), stop=(m == 1))
                for h in range(H):
                    for m in range(2):
                        last = nc.tensor.matmul(k.bank[3][32 * h:32 * h + 32, 0:64], hidden[:, m, 1, :], w2[:, 1, m, :], start=(m == 0), stop=(m == 1))
                last.then_inc(s["kv_sum"], 1)
                pe.wait_ge(s["kv_ready"], 1)
                for t in range(TT):
                    for i in range(2):
                        last = nc.tensor.matmul(k.bank[4][:, (2 * t + i) * 64:(2 * t + i + 1) * 64],
                                                k.cols[:, T_Q + i, LEAD + t * P:LEAD + (t + 1) * P], kpad[:, :, :], start=True, stop=True)
                last.then_inc(s["scores"], 1)
                pe.wait_ge(s["weights_ready"], 1)
                for t in range(TT):
                    last = nc.tensor.transpose(k.bank[5][:, t * P:(t + 1) * P], w[:, t, :, :].rearrange("p h n -> p (h n)"), k.ident[:, :])
                last.then_inc(s["turned"], 1)
                pe.wait_ge(s["kept"], 1)
                for t in range(TT):
                    for h in range(H):
                        last = nc.tensor.matmul(k.bank[6 + h // 2][64 * (h % 2):64 * (h % 2) + 64, t * P:(t + 1) * P],
                                                vz[:, h, :], wT[:, t, :], start=True, stop=True)
                last.then_inc(s["summed"], 1)


def nsa_mixer(nc, k, A, l):
    with ExitStack() as held:
        def sb(name, shape):
            return held.enter_context(nc.sbuf_tensor(name, shape, F32))
        a = Named()
        row = lambda name: A[name][bass.ds(l, 1), :, :].rearrange("a p c -> (a p) c")
        a.w1_dram, a.w2_dram = row("cmp_w1"), row("cmp_w2")
        a.w1 = sb("nsa_w1", [P, 32 * 256])
        a.w2 = sb("nsa_w2", [P, 256])
        a.gate = sb("nsa_gate", [P, TT, 12])
        a.blocks = sb("nsa_blocks", [P, 2, 32, NBLK])
        with ExitStack() as first:
            fb = lambda name, shape: first.enter_context(nc.sbuf_tensor(name, shape, F32))
            a.keys = fb("nsa_keys", [P, 2, 2, SEQ])
            a.vT = fb("nsa_vT", [P, TT, P])
            a.dist = k.wide[:, 3, 0:SEQ]
            a.alibi = k.wide[:, 0:2, :].rearrange("p a c -> p (a c)").rearrange("p (h t) -> p h t", h=4)
            a.weights = fb("nsa_weights", [P, 3, SEQ])
            a.turned = fb("nsa_turned", [P, 2, SEQ])
            a.neg_max = fb("nsa_neg_max", [P, 32])
            a.total = fb("nsa_total", [P, 32])
            a.inv = fb("nsa_inv", [P, 32])
            attention(nc, k, a)
        compressed_attention(nc, k, a, lambda c: A["w_out"][bass.ds(l, 1), c, :, :].rearrange("a p c -> (a p) c"))


def output_projection(nc, k, A, l):
    with ExitStack() as held:
        def sb(name, shape):
            return held.enter_context(nc.sbuf_tensor(name, shape, F32R))
        w_hi, w_lo = sb("out_w_hi", [P, 2, DM]), sb("out_w_lo", [P, 2, DM])
        m_hi, m_lo = sb("out_m_hi", [P, 2, SEQ]), sb("out_m_lo", [P, 2, SEQ])
        with stage(nc, "block_done", "hi_done", "lo_done", "added", "weights_in0", "weights_in1", "weights_in2", "weights_in3") as (block, s):
            loaded = (s["weights_in0"], s["weights_in1"], s["weights_in2"], s["weights_in3"])

            @block.sync
            def _(sp):
                for c in range(SLOTS):
                    sp.sem_inc(loaded[c], 16)
                for c in range(SLOTS, DB):
                    sp.wait_ge(s["lo_done"], c - SLOTS + 1)
                    sp.dma_start(k.ring[:, c % SLOTS, :], A["w_out"][bass.ds(l, 1), c, :, :].rearrange("a p c -> (a p) c")).then_inc(loaded[c % SLOTS], 16)

            @block.scalar
            def _(act):
                for c in range(DB):
                    act.wait_ge(loaded[c % SLOTS], 16 * (c // SLOTS + 1))
                    if c >= 2:
                        act.wait_ge(s["block_done"], c - 1)
                    nc.scalar.copy(m_hi[:, c % 2, :], k.mixed[:, c, :])
                    nc.scalar.copy(w_hi[:, c % 2, :], k.ring[:, c % SLOTS, :]).then_inc(s["hi_done"], 1)

            @block.tensor
            def _(pe):
                for c in range(DB):
                    pe.wait_ge(s["lo_done"], c + 1)
                    for t in range(TT):
                        for half in range(2):
                            token, o = slice(t * P, (t + 1) * P), slice(half * 512, (half + 1) * 512)
                            last = three_products(nc, k.bank[2 * t + half][:, :], (m_hi[:, c % 2, token], m_lo[:, c % 2, token]),
                                                  (w_hi[:, c % 2, o], w_lo[:, c % 2, o]), c == 0, c == DB - 1)
                    last.then_inc(s["block_done"], 1)

            @block.vector
            def _(dve):
                for c in range(DB):
                    dve.wait_ge(s["hi_done"], c + 1)
                    nc.vector.tensor_tensor(m_lo[:, c % 2, :], k.mixed[:, c, :], m_hi[:, c % 2, :].bitcast(F32), ALU.subtract)
                    nc.vector.tensor_tensor(w_lo[:, c % 2, :], k.ring[:, c % SLOTS, :], w_hi[:, c % 2, :].bitcast(F32),
                                            ALU.subtract).then_inc(s["lo_done"], 1)
                dve.wait_ge(s["block_done"], DB)
                for t in range(TT):
                    for half in range(2):
                        o = slice(half * 512, (half + 1) * 512)
                        nc.vector.tensor_tensor(k.h[:, t, o], k.h[:, t, o], k.bank[2 * t + half][:, :], ALU.add).then_inc(s["added"], 1)


HEADS = 8
TOP = 16
GJ = 4
N_GROUPS = P // GJ
AHEAD = 2
NEAR = GJ - AHEAD
AHEAD_BANK = 5
AHEAD_SEMS = ("ahead_u_in0", "ahead_u_in1", "ahead_u_hi", "ahead_u_lo", "ahead_u_done", "ahead_acts", "ahead_stored0", "ahead_stored1")
PAIRS_PER_TILE = 6
PAIRS_CHOOSING = TT * PAIRS_PER_TILE


class ExpertsAhead:

    def __init__(self, nc, k, s, A, l, a, first_group, bank):
        self.nc, self.k, self.s, self.u, self.l, self.a = nc, k, s, A["peer_u"], l, a
        self.first_group, self.bank = first_group, bank
        self.u_in = (s["ahead_u_in0"], s["ahead_u_in1"])
        self.stored = (s["ahead_stored0"], s["ahead_stored1"])

    def load(self, sp, q, first=False):
        for j in range(AHEAD):
            if not first:
                sp.wait_ge(self.s["ahead_u_lo"], q * AHEAD + (j + 1 - AHEAD))
            tile = self.l * P + q * GJ + (self.first_group * GJ + j)
            sp.dma_start(self.k.ring[:, AHEAD + j, :], self.u[bass.ds(tile, 1), :, :].rearrange("a p c -> (a p) c")).then_inc(self.u_in[j], 16)

    def start(self, pe, act):
        if pe is not None:
            pe.sem_inc(self.s["ahead_acts"], AHEAD)
        if act is not None:
            for j in range(AHEAD):
                act.sem_inc(self.stored[j], 16)

    def high(self, act, q, j):
        act.wait_ge(self.u_in[j], q * 16 + 16)
        self.nc.scalar.copy(self.a.u_hi[:, j, :], self.k.ring[:, AHEAD + j, :]).then_inc(self.s["ahead_u_hi"], 1)

    def low(self, pool, q, j):
        pool.wait_ge(self.s["ahead_u_hi"], q * AHEAD + (j + 1))
        self.nc.gpsimd.tensor_tensor(self.a.u_lo[:, j, :], self.k.ring[:, AHEAD + j, :], self.a.u_hi[:, j, :].bitcast(F32),
                                     ALU.subtract).then_inc(self.s["ahead_u_lo"], 1)

    def products(self, pe, q, j, blocks=range(DB)):
        if 0 in blocks:
            pe.wait_ge(self.s["ahead_u_lo"], q * AHEAD + (j + 1))
            pe.wait_ge(self.s["ahead_acts"], q * AHEAD + (j + 1))
        for b in blocks:
            c = slice(b * P, (b + 1) * P)
            last = three_products(self.nc, self.k.bank[self.bank + j][:, :], (self.a.u_hi[:, j, c], self.a.u_lo[:, j, c]),
                                  (self.a.x_hi[:, b, :], self.a.x_lo[:, b, :]), b == 0, b == DB - 1)
        if DB - 1 in blocks:
            last.then_inc(self.s["ahead_u_done"], 1)

    def gelu(self, act, q, j):
        act.wait_ge(self.s["ahead_u_done"], q * AHEAD + (j + 1))
        act.wait_ge(self.stored[j], q * 16 + 16)
        self.nc.scalar.activation(self.a.act[:, j, :], self.k.bank[self.bank + j][:, :],
                                  ACT.Gelu_apprx_tanh).then_inc(self.s["ahead_acts"], 1)

    def store(self, act, q, j):
        act.wait_ge(self.s["ahead_acts"], q * AHEAD + (j + 1 + AHEAD))
        g = slice(q + self.first_group, q + self.first_group + 1) if isinstance(q, int) else bass.ds(q + self.first_group, 1)
        act.dma_start(self.a.ahead[:, g, j * SEQ:(j + 1) * SEQ].rearrange("p a c -> p (a c)"), self.a.act[:, j, :]).then_inc(self.stored[j], 16)

    def end(self, act, steps):
        for j in range(AHEAD):
            act.wait_ge(self.stored[j], 16 * steps + 16)


def ahead_buffers(held, nc, x_hi, x_lo, ahead, when):
    a = Named()
    a.x_hi, a.x_lo, a.ahead = x_hi, x_lo, ahead
    a.u_hi, a.u_lo = (held.enter_context(nc.sbuf_tensor(f"ahead_{n}_{when}", [P, AHEAD, DM], F32R)) for n in ("u_hi", "u_lo"))
    a.act = held.enter_context(nc.sbuf_tensor(f"ahead_act_{when}", [P, AHEAD, SEQ], F32))
    return a


def choose_experts(nc, k, p, A, l, a):
    half = PAIRS_PER_TILE // 2
    with stage(nc, *AHEAD_SEMS, "keys_in", "scores", "ranked", "dve_done", "positions", "converted", "matched", "weighed", "shifted",
               "exps", "chosen", "turned", "kept") as (block, s):
        e = ExpertsAhead(nc, k, s, A, l, a, 0, AHEAD_BANK)

        @block.sync
        def _(sp):
            sp.dma_start(p.keys[:, :], A["peer_keys"][bass.ds(l, 1), :, :].rearrange("a p c -> (a p) c")).then_inc(s["keys_in"], 16)
            e.load(sp, 0, first=True)
            with sp.Fori(1, PAIRS_CHOOSING) as q:
                e.load(sp, q)
            sp.wait_ge(s["keys_in"], 16)

        @block.gpsimd
        def _(pool):
            with pool.Fori(0, PAIRS_CHOOSING) as q:
                for j in range(AHEAD):
                    e.low(pool, q, j)

        @block.tensor
        def _(pe):
            e.start(pe, None)
            pe.wait_ge(s["keys_in"], 16)

            def turn(t):
                pe.wait_ge(s["chosen"], t + 1)
                if t:
                    pe.wait_ge(s["kept"], t)
                for n in range(3):
                    last = nc.tensor.transpose(k.bank[4][:, n * P:(n + 1) * P], p.chosen[:, n, :], k.ident[:, :])
                last.then_inc(s["turned"], 1)

            def score(t):
                if t:
                    pe.wait_ge(s["ranked"], t)
                for n in range(2 * HEADS):
                    last = nc.tensor.matmul(k.bank[n // 4][:, (n % 4) * P:(n % 4 + 1) * P], p.q[:, n, t * P:(t + 1) * P],
                                            p.keys[:, n * P:(n + 1) * P], start=True, stop=True)
                last.then_inc(s["scores"], 1)

            def run_ahead(first, last):
                with pe.Fori(first, last) as q:
                    for j in range(AHEAD):
                        e.products(pe, q, j)
            score(0)
            for t in range(TT):
                at = t * PAIRS_PER_TILE
                run_ahead(at, at + half)
                if t < TT - 1:
                    score(t + 1)
                run_ahead(at + half, at + PAIRS_PER_TILE)
                turn(t)

        @block.vector
        def _(dve):
            step = in_order(dve, s["dve_done"])

            def top16(values, best, index):
                step(nc.vector.max(out=best[:, 0:8], in_=values))
                nc.vector.max_index(out=index[:, 0:8], in_max=best[:, 0:8], in_values=values)
                rest = p.rest[:, 0:values.shape[1]]
                step(nc.vector.match_replace(out=rest, in_to_replace=best[:, 0:8], in_values=values, imm_value=-3.0e38))
                step(nc.vector.max(out=best[:, 8:16], in_=rest))
                return nc.vector.max_index(out=index[:, 8:16], in_max=best[:, 8:16], in_values=rest)
            for t in range(TT):
                dve.wait_ge(s["scores"], t + 1)
                for n in range(2 * HEADS):
                    last = top16(k.bank[n // 4][:, (n % 4) * P:(n % 4 + 1) * P], p.best[:, n, :], p.index[:, n, :])
                last.then_inc(s["ranked"], 1)
                dve.wait_ge(s["ranked"], t + 1)
                best = p.best[:, :, :].rearrange("p (h c) k -> p h c k", c=2)
                step(nc.vector.tensor_tensor(p.sums[:, :, :, :], best[:, :, 0, :].unsqueeze(3).to_broadcast([P, HEADS, TOP, TOP]),
                                             best[:, :, 1, :].unsqueeze(2).to_broadcast([P, HEADS, TOP, TOP]), ALU.add))
                for h in range(HEADS):
                    last = top16(p.sums[:, h, :, :].rearrange("p a b -> p (a b)"), p.top[:, h, :], p.where[:, h, :])
                step(last)
                if t:
                    dve.wait_ge(s["turned"], t)
                step(nc.vector.tensor_tensor(p.chosen[:, 2, :].rearrange("p (h k) -> p h k", k=TOP), p.top[:, :, :],
                                             p.top[:, :, 0:1].to_broadcast([P, HEADS, TOP]), ALU.subtract))
                dve.sem_inc(s["shifted"], 1)
                flat = p.where[:, :, :].rearrange("p h k -> p (h k)")
                step(nc.vector.tensor_scalar(p.rank[:, 0, :], flat, 4, None, ALU.logical_shift_right))
                step(nc.vector.tensor_scalar(p.rank[:, 1, :], flat, 15, None, ALU.bitwise_and))
                step(nc.vector.tensor_copy(p.rank_f[:, :, :], p.rank[:, :, :]))
                step(nc.vector.tensor_copy(p.index_f[:, :, :], p.index[:, :, :]))
                index = p.index_f[:, :, :].rearrange("p (h c) k -> p h c k", c=2)
                for c in range(2):
                    hot = p.hot[:, c, :, :, :].rearrange("p h k a -> p (h k) a")
                    step(nc.vector.tensor_tensor(hot, p.rank_f[:, c, :].unsqueeze(2).to_broadcast([P, P, TOP]),
                                                 k.iota16[:, :].unsqueeze(1).to_broadcast([P, P, TOP]), ALU.is_equal))
                    step(nc.vector.tensor_tensor(p.hot[:, c, :, :, :], p.hot[:, c, :, :, :],
                                                 index[:, :, c, :].unsqueeze(2).to_broadcast([P, HEADS, TOP, TOP]), ALU.mult))
                    step(nc.vector.tensor_reduce(out=p.chosen[:, c, :], in_=hot, axis=AX.X, op=ALU.add))
                dve.wait_ge(s["exps"], t + 1)
                gate = p.chosen[:, 2, :].rearrange("p (h k) -> p h k", k=TOP)
                step(nc.vector.tensor_reduce(out=p.total[:, :], in_=gate, axis=AX.X, op=ALU.add))
                step(nc.vector.reciprocal(p.total[:, :], p.total[:, :]))
                nc.vector.tensor_tensor(gate, gate, p.total[:, :].unsqueeze(2).to_broadcast([P, HEADS, TOP]), ALU.mult).then_inc(s["chosen"], 1)
                dve.wait_ge(s["chosen"], t + 1)

        @block.scalar
        def _(act):
            e.start(None, act)
            for j in range(AHEAD):
                e.high(act, 0, j)

            def finish(q, more):
                for j in range(AHEAD):
                    e.gelu(act, q, j)
                    if more:
                        e.high(act, q + 1, j)
                    e.store(act, q, j)
            for t in range(TT):
                at = t * PAIRS_PER_TILE
                with act.Fori(at, at + PAIRS_PER_TILE - 1) as q:
                    finish(q, True)
                act.wait_ge(s["shifted"], t + 1)
                nc.scalar.activation(p.chosen[:, 2, :], p.chosen[:, 2, :], ACT.Exp).then_inc(s["exps"], 1)
                finish(at + PAIRS_PER_TILE - 1, t < TT - 1)
                act.wait_ge(s["turned"], t + 1)
                nc.scalar.copy(p.picks[:, :, t * P:(t + 1) * P], k.bank[4][:, 0:3 * P].rearrange("p (n t) -> p n t", n=3)).then_inc(s["kept"], 1)
            e.end(act, PAIRS_CHOOSING)


GROUP = 32
HOTS = 16
BATCH = 8


GATE_BANKS = 4


def spread_gates(nc, k, p, A, l, a):
    per = 2 * GROUP
    quads = per // 4
    steps = SEQ // per
    piece = {q: [] for q in range(quads)}
    for n in range(AHEAD * DB):
        piece[2 + n * (quads - 2) // (AHEAD * DB)].append((n // DB, n % DB))
    with stage(nc, *AHEAD_SEMS, "near_in", "picked", "hots", "products", "copied", "stored0", "stored1") as (block, s):
        stored = (s["stored0"], s["stored1"])
        e = ExpertsAhead(nc, k, s, A, l, a, PAIRS_CHOOSING, GATE_BANKS)

        @block.gpsimd
        def _(pool):
            with pool.Fori(0, steps) as it:
                for j in range(AHEAD):
                    e.low(pool, it, j)

        @block.vector
        def _(dve):
            dve.sem_inc(s["hots"], 1)
            with dve.Fori(0, SEQ // per) as it:
                dve.wait_ge(s["hots"], it * per + 1)
                nc.vector.tensor_copy(p.now[:, :, :], p.picks[:, :, bass.ds(it * per, per)]).then_inc(s["picked"], 1)
                dve.wait_ge(s["picked"], it + 1)
                for n in range(per):
                    if n % BATCH == 0:
                        dve.wait_ge(s["products"], it * per + (n + BATCH))
                        nc.vector.tensor_tensor(p.hot1[:, n % HOTS:n % HOTS + BATCH, :],
                                                k.iota128[:, :].unsqueeze(1).to_broadcast([P, BATCH, P]),
                                                p.now[:, 0, n:n + BATCH].unsqueeze(2).to_broadcast([P, BATCH, P]), ALU.is_equal)
                    nc.vector.tensor_scalar(p.hot2[:, n % HOTS, :], k.iota128[:, :], p.now[:, 1, n:n + 1],
                                            p.now[:, 2, n:n + 1], ALU.is_equal, ALU.mult).then_inc(s["hots"], 1)

        @block.tensor
        def _(pe):
            pe.sem_inc(s["products"], HOTS)
            e.start(pe, None)
            with pe.Fori(0, SEQ // per) as it:
                for n in range(per):
                    if n % 4 == 0:
                        pe.wait_ge(s["copied"], it * quads + n // 4 + 1)
                    pe.wait_ge(s["hots"], it * per + n + 2)
                    nc.tensor.matmul(k.bank[n // 4 % GATE_BANKS][:, (n % 4) * P:(n % 4 + 1) * P], p.hot1[:, n % HOTS, :],
                                     p.hot2[:, n % HOTS, :], start=True, stop=True).then_inc(s["products"], 1)
                    if n % 4 == 3:
                        for j, b in piece[n // 4]:
                            e.products(pe, it, j, range(b, b + 1))

        @block.scalar
        def _(act):
            act.sem_inc(s["copied"], GATE_BANKS)
            e.start(None, act)
            with act.Fori(0, SEQ // per) as it:
                for q in range(quads):
                    if q < AHEAD:
                        e.high(act, it, q)
                    g = q // (quads // 2)
                    if q % (quads // 2) == 0:
                        act.wait_ge(stored[g], it * 16 + 16)
                    act.wait_ge(s["products"], it * per + 4 * (q + 1) + HOTS)
                    tok = 4 * (q % (quads // 2))
                    nc.scalar.copy(p.out[:, g, :, tok:tok + 4].rearrange("p j t -> p t j"),
                                   k.bank[q % GATE_BANKS][:, :].rearrange("p (t j) -> p t j", t=4)).then_inc(s["copied"], 1)
                    if q == quads - 4:
                        e.gelu(act, it, 0)
                        e.store(act, it, 0)
                e.gelu(act, it, 1)
                e.store(act, it, 1)
            e.end(act, steps)

        @block.sync
        def _(sp):
            for g in range(2):
                sp.sem_inc(stored[g], 16)
            e.load(sp, 0, first=True)
            for j in range(NEAR):
                sp.dma_start(k.ring[:, j, :], A["peer_u"][bass.ds(l * P + AHEAD + j, 1), :, :].rearrange("a p c -> (a p) c")).then_inc(s["near_in"], 16)

            def keep(it, g):
                sp.wait_ge(s["copied"], it * quads + ((g + 1) * (quads // 2) + GATE_BANKS))
                at = slice(it * 2 + g, it * 2 + g + 1) if isinstance(it, int) else bass.ds(it * 2 + g, 1)
                sp.dma_start(p.gates[:, at, :, :].rearrange("p a j t -> p (a j t)"),
                             p.out[:, g, :, :].rearrange("p j t -> p (j t)")).then_inc(stored[g], 16)
            with sp.Fori(0, steps - 1) as it:
                keep(it, 0)
                e.load(sp, it + 1)
                keep(it, 1)
            for g in range(2):
                keep(steps - 1, g)
            for g in range(2):
                sp.wait_ge(stored[g], 16 * (SEQ // per) + 16)
            sp.wait_ge(s["near_in"], 16 * NEAR)


def run_experts(nc, k, d, A, l):
    with stage(nc, "u_in0", "u_in1", "v_in", "g_in0", "g_in1", "ahead_in0", "ahead_in1", "u_hi", "u_lo", "v_hi", "v_lo",
               "u_done", "acts", "gated", "a_hi", "a_lo", "y_done", "y_added") as (block, s):
        u_in, g_in, ahead_in = (s["u_in0"], s["u_in1"]), (s["g_in0"], s["g_in1"]), (s["ahead_in0"], s["ahead_in1"])
        FIRST, MIDDLE, LAST = range(3)
        raw_u = k.ring[:, :, :].rearrange("p (e j) c -> p e j c", e=2)
        raw_v = k.xT[:, :, :].rearrange("p b t -> p (b t)").rearrange("p (j c) -> p j c", j=GJ)

        def early(e, j):
            return k.wide[:, e, j * SEQ:(j + 1) * SEQ]

        def pairs(engine, body):
            for e in range(2):
                body(0, e, FIRST if e == 0 else MIDDLE)
            with engine.Fori(1, N_GROUPS // 2 - 1) as it:
                for e in range(2):
                    body(it, e, MIDDLE)
            for e in range(2):
                body(N_GROUPS // 2 - 1, e, LAST if e == 1 else MIDDLE)

        @block.sync
        def _(sp):
            def tiles(w, tile, n):
                return w[bass.ds(l * P + tile, n), :, :].rearrange("n p c -> p n c")

            def load_ahead(it, e, first):
                g = it * 2 + e
                if isinstance(it, int) and g == 0:
                    sp.sem_inc(u_in[0], 16)
                else:
                    if not first:
                        sp.wait_ge(s["u_lo"], g * NEAR - NEAR)
                    sp.dma_start(raw_u[:, e % 2, :, :], tiles(A["peer_u"], g * GJ + AHEAD, NEAR)).then_inc(u_in[e % 2], 16)
                if not first:
                    sp.wait_ge(s["a_lo"], g * GJ - GJ)
                one = slice(g, g + 1) if isinstance(it, int) else bass.ds(g, 1)
                sp.dma_start(k.wide[:, e % 2, :], d.ahead[:, one, :].rearrange("p a c -> p (a c)")).then_inc(ahead_in[e % 2], 16)
                at = slice(g * GJ, (g + 1) * GJ) if isinstance(it, int) else bass.ds(g * GJ, GJ)
                sp.dma_start(d.g[:, e % 2, :, :, :], d.gates[:, :, at, :]).then_inc(g_in[e % 2], 16)

            def load(it, e, where):
                if where == FIRST:
                    load_ahead(0, 0, True)
                if where != LAST:
                    load_ahead(it, e + 1, where == FIRST)
                if where != FIRST:
                    sp.wait_ge(s["v_lo"], (it * 2 + e) * GJ)
                sp.dma_start(raw_v, tiles(A["peer_v"], (it * 2 + e) * GJ, GJ)).then_inc(s["v_in"], 16)
            pairs(sp, load)

        @block.tensor
        def _(pe):
            def with_u(it, e):
                g = it * 2 + e
                for i in range(NEAR):
                    pe.wait_ge(s["u_lo"], g * NEAR + (i + 1))
                    pe.wait_ge(s["acts"], g * NEAR + (i + 1))
                    for b in range(DB):
                        c = slice(b * P, (b + 1) * P)
                        last = three_products(nc, k.bank[e * NEAR + i][:, :], (d.u_hi[:, i, c], d.u_lo[:, i, c]),
                                              (d.x_hi[:, b, :], d.x_lo[:, b, :]), b == 0, b == DB - 1)
                    last.then_inc(s["u_done"], 1)

            def with_v(it, e):
                g = it * 2 + e
                pe.wait_ge(s["v_lo"], g * GJ + GJ)
                pe.wait_ge(s["a_lo"], g * GJ + GJ)
                for o in range(8):
                    pe.wait_ge(s["y_added"], g * 8 + (o + 1))
                    t, half = slice(o // 2 * P, (o // 2 + 1) * P), slice(o % 2 * 512, (o % 2 + 1) * 512)
                    for j in range(GJ):
                        last = three_products(nc, k.bank[4 + o % 4][:, :], (d.a_hi[:, e, j, t], d.a_lo[:, e, j, t]),
                                              (d.v_hi[:, j, half], d.v_lo[:, j, half]), j == 0, j == GJ - 1)
                    last.then_inc(s["y_done"], 1)

            def body(it, e, where):
                with_u(it, e)
                if where != FIRST:
                    with_v(it + (e - 1), 1 - e)
                if where == LAST:
                    with_v(it, e)
            pairs(pe, body)

        @block.scalar
        def _(act):
            act.sem_inc(s["acts"], 2 * NEAR)

            def u_high(it, e, i):
                act.wait_ge(u_in[e % 2], it * 16 + 16 * (e // 2 + 1))
                nc.scalar.copy(d.u_hi[:, i, :], raw_u[:, e % 2, i, :]).then_inc(s["u_hi"], 1)

            def v_high():
                for j in range(GJ):
                    nc.scalar.copy(d.v_hi[:, j, :], raw_v[:, j, :]).then_inc(s["v_hi"], 1)

            def a_high(n, e, j, source):
                act.wait_ge(s["gated"], n + (j + 1))
                nc.scalar.copy(d.a_hi[:, e, j, :], source).then_inc(s["a_hi"], 1)

            def body(it, e, where):
                g = it * 2 + e
                n = g * GJ
                if where == FIRST:
                    for i in range(NEAR):
                        u_high(0, 0, i)
                else:
                    act.wait_ge(s["v_in"], g * 16)
                    if not (isinstance(it, int) and g == 1):
                        act.wait_ge(s["y_done"], g * 8 - 8)
                    v_high()
                for j in range(AHEAD):
                    a_high(n, e, j, early(e, j))
                for i in range(NEAR):
                    act.wait_ge(s["u_done"], g * NEAR + (i + 1))
                    if where != LAST:
                        u_high(it, e + 1, i)
                    if where != FIRST:
                        act.wait_ge(s["a_lo"], n + (i + 1 + AHEAD - GJ))
                    nc.scalar.activation(d.act[:, i, :], k.bank[e * NEAR + i][:, :], ACT.Gelu_apprx_tanh).then_inc(s["acts"], 1)
                    a_high(n, e, AHEAD + i, d.act[:, i, :])
                if where == LAST:
                    act.wait_ge(s["v_in"], g * 16 + 16)
                    act.wait_ge(s["y_done"], g * 8)
                    v_high()
            pairs(act, body)

        @block.vector
        def _(dve):
            dve.sem_inc(s["y_added"], 4)

            def u_low(it, e, i):
                dve.wait_ge(s["u_hi"], (it * 2 + e) * NEAR + (i + 1))
                nc.vector.tensor_tensor(d.u_lo[:, i, :], raw_u[:, e % 2, i, :], d.u_hi[:, i, :].bitcast(F32),
                                        ALU.subtract).then_inc(s["u_lo"], 1)

            def v_low(g):
                for j in range(GJ):
                    dve.wait_ge(s["v_hi"], g * GJ + (j + 1))
                    nc.vector.tensor_tensor(d.v_lo[:, j, :], raw_v[:, j, :], d.v_hi[:, j, :].bitcast(F32), ALU.subtract).then_inc(s["v_lo"], 1)

            def gate(e, j, acts):
                blocks = acts.rearrange("p (b t) -> p b t", t=GROUP)
                nc.vector.tensor_tensor(blocks, blocks, d.g[:, e, :, j, :], ALU.mult).then_inc(s["gated"], 1)

            def a_low(n, e, j, acts):
                dve.wait_ge(s["a_hi"], n + (j + 1))
                nc.vector.tensor_tensor(d.a_lo[:, e, j, :], acts, d.a_hi[:, e, j, :].bitcast(F32), ALU.subtract).then_inc(s["a_lo"], 1)

            def add(it, e):
                g = it * 2 + e
                for o in range(8):
                    dve.wait_ge(s["y_done"], g * 8 + (o + 1))
                    c = slice(o % 2 * 512, (o % 2 + 1) * 512)
                    nc.vector.tensor_tensor(k.h[:, o // 2, c], k.h[:, o // 2, c], k.bank[4 + o % 4][:, :], ALU.add).then_inc(s["y_added"], 1)

            def body(it, e, where):
                g = it * 2 + e
                n = g * GJ
                if where == FIRST:
                    for i in range(NEAR):
                        u_low(0, 0, i)
                else:
                    v_low(it * 2 + (e - 1))
                dve.wait_ge(ahead_in[e], it * 16 + 16)
                dve.wait_ge(g_in[e], it * 16 + 16)
                for j in range(AHEAD):
                    gate(e, j, early(e, j))
                for j in range(AHEAD):
                    a_low(n, e, j, early(e, j))
                for i in range(NEAR):
                    if where != LAST:
                        u_low(it, e + 1, i)
                    dve.wait_ge(s["acts"], g * NEAR + (i + 1 + 2 * NEAR))
                    gate(e, AHEAD + i, d.act[:, i, :])
                    a_low(n, e, AHEAD + i, d.act[:, i, :])
                if where != FIRST:
                    add(it + (e - 1), 1 - e)
                if where == LAST:
                    v_low(g)
                    add(it, e)
            pairs(dve, body)


def peer(nc, k, A, l, gates, ahead, x_hi, x_lo):
    with ExitStack() as held:
        def sb(name, shape, dt=F32):
            return held.enter_context(nc.sbuf_tensor(name, shape, dt))
        p = Named()
        p.gates = gates
        p.picks = sb("peer_picks", [P, 3, SEQ])
        with ExitStack() as first:
            fb = lambda name, shape, dt=F32: first.enter_context(nc.sbuf_tensor(name, shape, dt))
            p.q = fb("peer_q", [P, 2 * HEADS, SEQ])
            project(nc, k, A["peer_wq"], l * 16, 16, p.q, 0, x_hi, x_lo)
            p.keys = fb("peer_keys", [P, 2 * HEADS * P])
            p.best = fb("peer_best", [P, 2 * HEADS, TOP])
            p.index = fb("peer_index", [P, 2 * HEADS, TOP], U32)
            p.index_f = fb("peer_index_f", [P, 2 * HEADS, TOP])
            p.rest = fb("peer_rest", [P, TOP * TOP])
            p.sums = fb("peer_sums", [P, HEADS, TOP, TOP])
            p.top = fb("peer_top", [P, HEADS, TOP])
            p.where = fb("peer_where", [P, HEADS, TOP], U32)
            p.rank = fb("peer_rank", [P, 2, P], U32)
            p.rank_f = fb("peer_rank_f", [P, 2, P])
            p.hot = fb("peer_hot", [P, 2, HEADS, TOP, TOP])
            p.chosen = fb("peer_chosen", [P, 3, P])
            p.total = fb("peer_total", [P, HEADS])
            choose_experts(nc, k, p, A, l, ahead_buffers(first, nc, x_hi, x_lo, ahead, "choosing"))
        with ExitStack() as second:
            fb = lambda name, shape, dt=F32: second.enter_context(nc.sbuf_tensor(name, shape, dt))
            p.now = fb("peer_now", [P, 3, 2 * GROUP])
            p.hot1 = fb("peer_hot1", [P, HOTS, P])
            p.hot2 = fb("peer_hot2", [P, HOTS, P])
            p.out = fb("peer_out", [P, 2, P, GROUP])
            spread_gates(nc, k, p, A, l, ahead_buffers(second, nc, x_hi, x_lo, ahead, "spreading"))
    with ExitStack() as held:
        fb = lambda name, shape, dt=F32: held.enter_context(nc.sbuf_tensor(name, shape, dt))
        d = Named()
        d.gates, d.ahead = gates, ahead
        d.x_hi, d.x_lo = x_hi, x_lo
        d.u_hi, d.u_lo = fb("peer_u_hi", [P, NEAR, DM], F32R), fb("peer_u_lo", [P, NEAR, DM], F32R)
        d.v_hi, d.v_lo = fb("peer_v_hi", [P, GJ, DM], F32R), fb("peer_v_lo", [P, GJ, DM], F32R)
        d.a_hi, d.a_lo = fb("peer_a_hi", [P, 2, GJ, SEQ], F32R), fb("peer_a_lo", [P, 2, GJ, SEQ], F32R)
        d.act = fb("peer_act", [P, NEAR, SEQ])
        d.g = fb("peer_g", [P, 2, SEQ // GROUP, GJ, GROUP])
        run_experts(nc, k, d, A, l)


def final_norm(nc, k, A, out):
    with stage(nc, "gain_in", "squares", "variance", "deviation", "dve_done", "normed", "stored") as (block, s):
        @block.sync
        def _(sp):
            sp.dma_start(k.xT[:, 0:2, :].rearrange("p a c -> p (a c)"), A["final_norm"].to_broadcast([P, DM])).then_inc(s["gain_in"], 16)
            for t in range(TT):
                sp.wait_ge(s["normed"], t + 1)
                sp.dma_start(out[t * P:(t + 1) * P, :], k.wide[:, t, :]).then_inc(s["stored"], 16)
            sp.wait_ge(s["stored"], 16 * TT)

        @block.scalar
        def _(act):
            for t in range(TT):
                if t:
                    act.wait_ge(s["squares"], t)
                nc.scalar.activation(k.xT[:, 2:4, :].rearrange("p a c -> p (a c)"), k.h[:, t, :], ACT.Square,
                                     accum_out=k.stat[:, t:t + 1]).then_inc(s["squares"], 1)
            act.wait_ge(s["variance"], 1)
            nc.scalar.activation(k.stat[:, 8:12], k.stat[:, 4:8], ACT.Sqrt).then_inc(s["deviation"], 1)

        @block.vector
        def _(dve):
            step = in_order(dve, s["dve_done"])
            dve.wait_ge(s["squares"], TT)
            nc.vector.tensor_scalar(k.stat[:, 4:8], k.stat[:, 0:4], 1.0 / DM, EPS, ALU.mult, ALU.add).then_inc(s["variance"], 1)
            dve.wait_ge(s["deviation"], 1)
            step(nc.vector.reciprocal(k.stat[:, 12:16], k.stat[:, 8:12]))
            dve.wait_ge(s["gain_in"], 16)
            for t in range(TT):
                nc.vector.scalar_tensor_tensor(out=k.wide[:, t, :], in0=k.h[:, t, :], scalar=k.stat[:, 12 + t:13 + t],
                                               in1=k.xT[:, 0:2, :].rearrange("p a c -> p (a c)"),
                                               op0=ALU.mult, op1=ALU.mult).then_inc(s["normed"], 1)


def program(nc, A, out):
    ctx = ExitStack()
    with ctx:
        def sb(name, shape, dt=F32):
            return ctx.enter_context(nc.sbuf_tensor(name, shape, dt))
        k = Named()
        k.h = sb("h", [P, TT, DM])
        k.xT = sb("xT", [P, DB, SEQ])
        k.wide = sb("wide", [P, TT, DM])
        k.ring = sb("ring", [P, SLOTS, DB * P])
        k.vec = sb("vec", [P, N_VEC])
        k.stat = sb("stat", [P, 32])
        k.smallT = sb("smallT", [P, TT, 16])
        k.lru_w = sb("lru_w", [P, 2, 2, 64])
        k.lora = sb("lora", [P, 512])
        k.ident = sb("ident", [P, P])
        k.ones = sb("ones", [P, P])
        k.upper = sb("upper", [P, P])
        k.strict = sb("strict", [P, P])
        k.lower = sb("lower", [P, P])
        k.same = {b: sb(f"same{b}", [P, P]) for b in (8, 16, 32, 64)}
        k.reset = sb("reset", [P, SEQ])
        k.iota16 = sb("iota16", [P, 16])
        k.iota128 = sb("iota128", [P, P])
        k.bank = [ctx.enter_context(nc.psum_tensor(f"bank{i}", [P, 512], F32)) for i in range(8)]
        gates = nc.dram_tensor("gates", (P, SEQ // GROUP, P, GROUP), F32, kind="Internal").ap()
        ahead = nc.dram_tensor("ahead", (P, N_GROUPS, AHEAD * SEQ), F32, kind="Internal").ap()
        make_constants(nc, k)
        with stage(nc, "x_in") as (block, s):
            @block.sync
            def _(sp):
                sp.dma_start(k.h[:, :, :].rearrange("p t c -> p (t c)"), A["x"]).then_inc(s["x_in"], 16)
                sp.wait_ge(s["x_in"], 16)
        with nc.Fori(0, DEPTH) as l:
            with ExitStack() as held:
                k.cols = held.enter_context(nc.sbuf_tensor("cols", [P, N_COLS, LEAD + SEQ], F32))
                k.mixed = held.enter_context(nc.sbuf_tensor("mixed", [P, DB, SEQ], F32))
                load_layer_vectors(nc, k, A, l)
                with ExitStack() as ssd:
                    xbc = ssd.enter_context(nc.sbuf_tensor("ssd_xbc", [P, 4, SEQ], F32))
                    silu_z = ssd.enter_context(nc.sbuf_tensor("ssd_silu_z", [P, 2, SEQ], F32))
                    with ExitStack() as split:
                        x_hi, x_lo = (split.enter_context(nc.sbuf_tensor(n, [P, DB, SEQ], F32R)) for n in ("mix_x_hi", "mix_x_lo"))
                        norm_and_transpose(nc, k, VEC["mix_norm"], x_hi, x_lo, A["w_in"], l * N_COLS)
                        project(nc, k, A["w_in"], l * N_COLS, N_COLS, k.cols, LEAD, x_hi, x_lo,
                                MixersBeside(nc, k, split, xbc[:, :, :], silu_z[:, :, :]))
                    ssd_mixer(nc, k, xbc, silu_z)
                rwkv_mixer(nc, k)
                nsa_mixer(nc, k, A, l)
                output_projection(nc, k, A, l)
            with ExitStack() as split:
                x_hi, x_lo = (split.enter_context(nc.sbuf_tensor(n, [P, DB, SEQ], F32R)) for n in ("ffn_x_hi", "ffn_x_lo"))
                norm_and_transpose(nc, k, VEC["ffn_norm"], x_hi, x_lo, A["peer_wq"], l * 16)
                peer(nc, k, A, l, gates, ahead, x_hi, x_lo)
        final_norm(nc, k, A, out)


def kernel(**inputs):
    import concourse.bacc as bacc
    from concourse.bass_utils import run_bass_kernel_spmd

    nc = bacc.Bacc("TRN2", target_bir_lowering=False, num_devices=1)
    arrays = {"in_" + n: a for n, a in lay_out({n: np.asarray(a) for n, a in inputs.items()}).items()}
    A = {n[3:]: nc.dram_tensor(n, a.shape, mybir.dt.from_np(a.dtype), kind="ExternalInput").ap() for n, a in arrays.items()}
    out = nc.dram_tensor("out", (SEQ, DM), F32, kind="ExternalOutput").ap()
    program(nc, A, out)
    r = run_bass_kernel_spmd(nc, [arrays], core_ids=[0])
    return r.results[0]["out"].reshape(1, SEQ, DM)
```
